# Optimizing a Trainium2 kernel written in Bass

```python
import math
import jax, jax.numpy as jnp
from jax import lax
import numpy as np

D_MODEL = 1024
BATCH = 1
SEQ = 256
DEPTH = 1

SSD_EXPAND = 2
SSD_INNER = SSD_EXPAND * D_MODEL
SSD_HEAD_DIM = 64
SSD_HEADS = SSD_INNER // SSD_HEAD_DIM
SSD_GROUPS = 4
SSD_STATE = 128
SSD_CONV = 4
SSD_CHUNK = 128
XBC_WIDTH = SSD_INNER + 2 * SSD_GROUPS * SSD_STATE
DIFF_HEADS = 8
DIFF_HEAD_DIM = D_MODEL // (2 * DIFF_HEADS)
DIFF_V_DIM = 2 * DIFF_HEAD_DIM
DIFF_WIDTH = DIFF_HEADS * DIFF_V_DIM
Q_BLOCK = 128
REL_BUCKETS = 32
REL_MAX_DIST = 128
MEM_LEN = 256
MEM_HEADS = 4
MEM_HEAD_DIM = D_MODEL // MEM_HEADS
N_EXPERTS = 64
TOP_K = 8
N_EXPERT_GROUPS = 8
TOP_GROUPS = 4
EXPERT_FF = 256
SHARED_FF = 256
ROUTED_SCALE = 2.5
DN_ALPHA = (2.0 * DEPTH) ** 0.25
DN_BETA = (8.0 * DEPTH) ** -0.25
NORM_EPS = 1e-5
IN_WIDTH = SSD_INNER + XBC_WIDTH + SSD_HEADS + 3 * DIFF_WIDTH + 2 * D_MODEL

kernel_name = "hybrid_ssd_diffattn_moe_deepnorm"

def layer_norm(x, g, b):
    xf = x.astype(jnp.float32)
    mu = jnp.mean(xf, axis=-1, keepdims=True)
    var = jnp.mean(jnp.square(xf - mu), axis=-1, keepdims=True)
    return ((xf - mu) * lax.rsqrt(var + NORM_EPS) * g.astype(jnp.float32) + b.astype(jnp.float32)).astype(x.dtype)

def rms_norm(x, g):
    xf = x.astype(jnp.float32)
    return (xf * lax.rsqrt(jnp.mean(jnp.square(xf), axis=-1, keepdims=True) + NORM_EPS) * g.astype(jnp.float32)).astype(x.dtype)

def causal_dwconv(u, w, b):
    c = u.shape[-1]
    out = lax.conv_general_dilated(u, w[:, None, :].astype(u.dtype), window_strides=(1,),
                                   padding=[(SSD_CONV - 1, 0)],
                                   dimension_numbers=('NWC', 'WIO', 'NWC'),
                                   feature_group_count=c)
    return out + b

def ssd_chunked(xs, a, bm, cm):
    b, s, h, p = xs.shape
    c, l, g, j = s // SSD_CHUNK, SSD_CHUNK, SSD_GROUPS, h // SSD_GROUPS
    xs = xs.reshape(b, c, l, g, j, p)
    bm = bm.reshape(b, c, l, g, SSD_STATE)
    cm = cm.reshape(b, c, l, g, SSD_STATE)
    acs = jnp.cumsum(a.reshape(b, c, l, g, j).transpose(0, 3, 4, 1, 2), axis=-1)
    causal = jnp.tril(jnp.ones((l, l), dtype=bool))
    decay_in = jnp.exp(jnp.where(causal, acs[..., :, None] - acs[..., None, :], -jnp.inf))
    cb = jnp.einsum('bclgn,bcsgn->bgcls', cm, bm)
    y_diag = jnp.einsum('bgcls,bgjcls,bcsgjp->bclgjp', cb, decay_in, xs)
    decay_out = jnp.exp(acs[..., -1:] - acs)
    states = jnp.einsum('bclgn,bgjcl,bclgjp->cbgjpn', bm, decay_out, xs)
    chunk_decay = jnp.exp(acs[..., -1]).transpose(3, 0, 1, 2)

    def step(hstate, inp):
        st, dec = inp
        return hstate * dec[..., None, None] + st, hstate

    h0 = jnp.zeros(states.shape[1:], states.dtype)
    _, prev = lax.scan(step, h0, (states, chunk_decay.astype(states.dtype)))
    y_off = jnp.einsum('bclgn,cbgjpn,bgjcl->bclgjp', cm, prev, jnp.exp(acs))
    return (y_diag + y_off).reshape(b, s, h, p)

def ssd_branch(z, xbc, dt_raw, conv_w, conv_b, dt_bias, a_log, d_skip, norm_g, w_br):
    b, s, _ = z.shape
    nbc = SSD_GROUPS * SSD_STATE
    xbc = jax.nn.silu(causal_dwconv(xbc, conv_w, conv_b))
    xs = xbc[..., :SSD_INNER].reshape(b, s, SSD_HEADS, SSD_HEAD_DIM)
    bm = xbc[..., SSD_INNER:SSD_INNER + nbc].reshape(b, s, SSD_GROUPS, SSD_STATE)
    cm = xbc[..., SSD_INNER + nbc:].reshape(b, s, SSD_GROUPS, SSD_STATE)
    dt = jax.nn.softplus(dt_raw.astype(jnp.float32) + dt_bias.astype(jnp.float32))
    a = -jnp.exp(a_log.astype(jnp.float32)) * dt
    y = ssd_chunked(xs * dt[..., None], a, bm, cm)
    y = (y + d_skip[:, None] * xs).reshape(b, s, SSD_INNER) * jax.nn.silu(z)
    y = rms_norm(y.reshape(b, s, SSD_GROUPS, -1), norm_g.reshape(SSD_GROUPS, -1)).reshape(b, s, SSD_INNER)
    return y @ w_br

def t5_bucket(dist):
    max_exact = REL_BUCKETS // 2
    d = jnp.maximum(dist, 1).astype(jnp.float32)
    large = max_exact + (jnp.log(d / max_exact) / math.log(REL_MAX_DIST / max_exact)
                         * (REL_BUCKETS - max_exact)).astype(jnp.int32)
    large = jnp.minimum(large, REL_BUCKETS - 1)
    return jnp.where(dist < max_exact, dist, large)

def diff_attention(q, k, v, lam, rel_bias):
    s = q.shape[1]
    q = q * DIFF_HEAD_DIM ** -0.5
    outs = []
    for i in range(s // Q_BLOCK):
        q0, kend = i * Q_BLOCK, (i + 1) * Q_BLOCK
        logits = jnp.einsum('bqhmd,bkhmd->bhmqk', q[:, q0:kend], k[:, :kend]).astype(jnp.float32)
        dist = (q0 + jnp.arange(Q_BLOCK))[:, None] - jnp.arange(kend)[None, :]
        bias = rel_bias.astype(jnp.float32)[t5_bucket(jnp.maximum(dist, 0))]
        logits = jnp.where(dist >= 0, logits + bias.transpose(2, 0, 1)[:, None], -jnp.inf)
        p = jax.nn.softmax(logits, axis=-1)
        attn = p[:, :, 0] - lam * p[:, :, 1]
        outs.append(jnp.einsum('bhqk,bkhe->bqhe', attn.astype(v.dtype), v[:, :kend]))
    return jnp.concatenate(outs, axis=1)

def diff_branch(q, k, v, lq1, lk1, lq2, lk2, subln_g, rel_bias, w_br, layer_idx):
    b, s, _ = q.shape
    lam_init = 0.8 - 0.6 * math.exp(-0.3 * layer_idx)
    f32 = jnp.float32
    lam = (jnp.exp(jnp.sum(lq1.astype(f32) * lk1.astype(f32)))
           - jnp.exp(jnp.sum(lq2.astype(f32) * lk2.astype(f32))) + lam_init)
    o = diff_attention(q.reshape(b, s, DIFF_HEADS, 2, DIFF_HEAD_DIM),
                       k.reshape(b, s, DIFF_HEADS, 2, DIFF_HEAD_DIM),
                       v.reshape(b, s, DIFF_HEADS, DIFF_V_DIM), lam, rel_bias)
    o = rms_norm(o, subln_g) * (1.0 - lam_init)
    return o.reshape(b, s, DIFF_WIDTH) @ w_br

def memory_cross_attention(x, mem, w_cq, w_ckv, w_co):
    b, s, d = x.shape
    q = (x @ w_cq).reshape(b, s, MEM_HEADS, MEM_HEAD_DIM)
    kv = (mem @ w_ckv).reshape(b, mem.shape[1], 2, MEM_HEADS, MEM_HEAD_DIM)
    logits = jnp.einsum('bqhd,bkhd->bhqk', q, kv[:, :, 0]).astype(jnp.float32) * MEM_HEAD_DIM ** -0.5
    p = jax.nn.softmax(logits, axis=-1).astype(x.dtype)
    o = jnp.einsum('bhqk,bkhd->bqhd', p, kv[:, :, 1]).reshape(b, s, d)
    return o @ w_co

def moe_ffn(x, w_router, router_bias, w_exp_gu, w_exp_down, w_sh_gu, w_sh_down):
    b, s, d = x.shape
    t = x.reshape(-1, d)
    n_tok = t.shape[0]
    scores = jax.nn.sigmoid(jnp.dot(t, w_router).astype(jnp.float32))
    choice = scores + router_bias.astype(jnp.float32)
    grp = choice.reshape(n_tok, N_EXPERT_GROUPS, N_EXPERTS // N_EXPERT_GROUPS)
    grp_score = jnp.sum(lax.top_k(grp, 2)[0], axis=-1)
    _, top_g = lax.top_k(grp_score, TOP_GROUPS)
    gmask = jnp.any(top_g[..., None] == jnp.arange(N_EXPERT_GROUPS), axis=-2)
    emask = jnp.repeat(gmask, N_EXPERTS // N_EXPERT_GROUPS, axis=-1)
    _, idx = lax.top_k(jnp.where(emask, choice, -jnp.inf), TOP_K)
    w = jnp.take_along_axis(scores, idx, axis=-1)
    w = w / jnp.sum(w, axis=-1, keepdims=True) * ROUTED_SCALE
    gates = jnp.zeros((n_tok, N_EXPERTS), jnp.float32).at[jnp.arange(n_tok)[:, None], idx].set(w).astype(t.dtype)
    gu = t @ w_sh_gu
    y = (jax.nn.silu(gu[:, :SHARED_FF]) * gu[:, SHARED_FF:]) @ w_sh_down
    for e in range(N_EXPERTS):
        gu = t @ w_exp_gu[e]
        h = jax.nn.silu(gu[:, :EXPERT_FF]) * gu[:, EXPERT_FF:]
        y = y + gates[:, e:e + 1] * (h @ w_exp_down[e])
    return y.reshape(b, s, d)

def setup_inputs(seed: int = 0) -> dict:
    key = jax.random.key(seed)
    ks = iter(jax.random.split(key, 48))
    L = DEPTH

    def nrm(shape, scale):
        return jax.random.normal(next(ks), shape, jnp.float32) * scale

    dt0 = jnp.exp(jax.random.uniform(next(ks), (L, SSD_HEADS), jnp.float32,
                                     minval=math.log(1e-3), maxval=math.log(1e-1)))
    return {
        "x": nrm((BATCH, SEQ, D_MODEL), 1.0),
        "mem": nrm((BATCH, MEM_LEN, D_MODEL), 1.0),
        "w_in": nrm((L, D_MODEL, IN_WIDTH), D_MODEL ** -0.5),
        "conv_w": nrm((L, SSD_CONV, XBC_WIDTH), SSD_CONV ** -0.5),
        "conv_b": nrm((L, XBC_WIDTH), 0.02),
        "dt_bias": dt0 + jnp.log(-jnp.expm1(-dt0)),
        "a_log": jnp.log(jax.random.uniform(next(ks), (L, SSD_HEADS), jnp.float32, minval=1.0, maxval=16.0)),
        "d_skip": 1.0 + nrm((L, SSD_HEADS), 0.1),
        "ssd_norm_g": 1.0 + nrm((L, SSD_INNER), 0.02),
        "lambda_q1": nrm((L, DIFF_HEAD_DIM), 0.1),
        "lambda_k1": nrm((L, DIFF_HEAD_DIM), 0.1),
        "lambda_q2": nrm((L, DIFF_HEAD_DIM), 0.1),
        "lambda_k2": nrm((L, DIFF_HEAD_DIM), 0.1),
        "subln_g": 1.0 + nrm((L, DIFF_V_DIM), 0.02),
        "rel_bias": nrm((REL_BUCKETS, DIFF_HEADS), 0.5),
        "w_ssd_br": nrm((L, SSD_INNER, D_MODEL), SSD_INNER ** -0.5),
        "w_diff_br": nrm((L, DIFF_WIDTH, D_MODEL), DIFF_WIDTH ** -0.5),
        "w_mix_out": nrm((L, D_MODEL, D_MODEL), D_MODEL ** -0.5 * DN_BETA),
        "ln1_g": 1.0 + nrm((L, D_MODEL), 0.02),
        "ln1_b": nrm((L, D_MODEL), 0.02),
        "w_cq": nrm((L, D_MODEL, D_MODEL), D_MODEL ** -0.5),
        "w_ckv": nrm((L, D_MODEL, 2 * D_MODEL), D_MODEL ** -0.5),
        "w_co": nrm((L, D_MODEL, D_MODEL), D_MODEL ** -0.5 * DN_BETA),
        "ln2_g": 1.0 + nrm((L, D_MODEL), 0.02),
        "ln2_b": nrm((L, D_MODEL), 0.02),
        "w_router": nrm((L, D_MODEL, N_EXPERTS), D_MODEL ** -0.5),
        "router_bias": nrm((L, N_EXPERTS), 0.01),
        "w_exp_gu": nrm((L, N_EXPERTS, D_MODEL, 2 * EXPERT_FF), D_MODEL ** -0.5),
        "w_exp_down": nrm((L, N_EXPERTS, EXPERT_FF, D_MODEL), EXPERT_FF ** -0.5 * DN_BETA),
        "w_sh_gu": nrm((L, D_MODEL, 2 * SHARED_FF), D_MODEL ** -0.5),
        "w_sh_down": nrm((L, SHARED_FF, D_MODEL), SHARED_FF ** -0.5 * DN_BETA),
        "ln3_g": 1.0 + nrm((L, D_MODEL), 0.02),
        "ln3_b": nrm((L, D_MODEL), 0.02),
    }

def reference(x, mem, w_in, conv_w, conv_b, dt_bias, a_log, d_skip, ssd_norm_g,
              lambda_q1, lambda_k1, lambda_q2, lambda_k2, subln_g, rel_bias,
              w_ssd_br, w_diff_br, w_mix_out, ln1_g, ln1_b,
              w_cq, w_ckv, w_co, ln2_g, ln2_b,
              w_router, router_bias, w_exp_gu, w_exp_down, w_sh_gu, w_sh_down,
              ln3_g, ln3_b):
    o_z = SSD_INNER
    o_xbc = o_z + XBC_WIDTH
    o_dt = o_xbc + SSD_HEADS
    o_q = o_dt + DIFF_WIDTH
    o_k = o_q + DIFF_WIDTH
    o_v = o_k + DIFF_WIDTH
    for l in range(DEPTH):
        proj = jnp.einsum('bsd,de->bse', x, w_in[l])
        z, xbc, dt_raw = proj[..., :o_z], proj[..., o_z:o_xbc], proj[..., o_xbc:o_dt]
        q, k, v = proj[..., o_dt:o_q], proj[..., o_q:o_k], proj[..., o_k:o_v]
        gates = jax.nn.sigmoid(proj[..., o_v:])
        ssd_out = ssd_branch(z, xbc, dt_raw, conv_w[l], conv_b[l], dt_bias[l], a_log[l],
                             d_skip[l], ssd_norm_g[l], w_ssd_br[l])
        diff_out = diff_branch(q, k, v, lambda_q1[l], lambda_k1[l], lambda_q2[l], lambda_k2[l],
                               subln_g[l], rel_bias, w_diff_br[l], l)
        mixed = (gates[..., :D_MODEL] * ssd_out + gates[..., D_MODEL:] * diff_out) @ w_mix_out[l]
        x = layer_norm(DN_ALPHA * x + mixed, ln1_g[l], ln1_b[l])
        x = layer_norm(DN_ALPHA * x + memory_cross_attention(x, mem, w_cq[l], w_ckv[l], w_co[l]),
                       ln2_g[l], ln2_b[l])
        x = layer_norm(DN_ALPHA * x + moe_ffn(x, w_router[l], router_bias[l], w_exp_gu[l],
                                              w_exp_down[l], w_sh_gu[l], w_sh_down[l]),
                       ln3_g[l], ln3_b[l])
    return x


_drawn_inputs = setup_inputs


def setup_inputs(seed=0):
    import zlib

    import numpy as np

    out = dict(_drawn_inputs(seed))
    spreads = {}
    factors = {'ssd_norm_g': 3.9,
     'lambda_q1': 3.533,
     'lambda_k1': 7.106,
     'subln_g': 3.28,
     'ln3_g': 8.445,
     'ln3_b': 7.969,
     'lambda_k2': 3.492}
    for name, (base, spread) in spreads.items():
        noise = np.random.default_rng([zlib.crc32(name.encode()), seed]).standard_normal(out[name].shape)
        drawn = base * np.exp(spread * noise) if base else spread * noise
        out[name] = __import__('jax').numpy.asarray(drawn.astype(out[name].dtype))
    for name, factor in factors.items():
        out[name] = (out[name] * factor).astype(out[name].dtype)
    return out
```

```python
import math
from contextlib import ExitStack

import numpy as np

import concourse.bass as bass
from concourse import mybir

F32 = mybir.dt.float32
F32R = mybir.dt.float32r
I32 = mybir.dt.int32
ALU = mybir.AluOpType
ACT = mybir.ActivationFunctionType
AX = mybir.AxisListType

P = 128
SEQ = 256
TB = SEQ // P
D = 1024
KB = D // P
INNER = 2048
SSD_HEADS = 32
HEAD = 64
GROUPS = 4
STATE = 128
CONV = 4
XBC = INNER + 2 * GROUPS * STATE
NXB = XBC // P
XS_BLOCKS = INNER // P
DIFF_HEADS = 8
MEM_HEADS = 4
BUCKETS = 32
MAX_DIST = 128
EXPERTS = 64
PAIRS = EXPERTS // 2
EGROUPS = 8
TOP_GROUPS = 4
FF = 256
SLOTS = 64
CHUNKS = SEQ // SLOTS
EXTRA = (CHUNKS - 1) * PAIRS
PER_GROUP = 8
ROUTED_SCALE = 2.5
ALPHA = 2.0 ** 0.25
EPS = 1e-5
LAM_INIT = 0.8 - 0.6 * math.exp(0.0)
SUBLN_SCALE = 1.0 - LAM_INIT
MASKED = -1.0e30
TILE = 4096

O_XBC = INNER
O_DT = O_XBC + XBC
O_Q = O_DT + SSD_HEADS
O_K = O_Q + D
O_V = O_K + D
O_G = O_V + D

STREAM = ([("xbc", 4)] * 6 + [("q", 4)] * 2 + [("k", 4)] * 2 + [("v", 2)] * 2 + [("z", 4)] * 4 + [("gate", 4)] * 4
          + [("ck", 4)] * 2 + [("cv", 2)] * 2 + [("ssd", 2)] * 4 + [("diff", 4)] * 2 + [("mix", 2)] * 2
          + [("cq", 4)] * 2 + [("co", 2)] * 2 + [("sh", 2)])
N_DENSE = len(STREAM)
FIRST_OUT = [sum(m for _, m in STREAM[:t]) for t in range(N_DENSE + 1)]
TILE_OF = {}
for _t, (_k, _m) in enumerate(STREAM):
    TILE_OF.setdefault(_k, _t)
BY_DVE = {"ssd", "diff", "mix", "co", "sh"}
OUT_KIND = [k for k, m in STREAM for _ in range(m)]
DENSE_RING = 3
RING = 6

C_ID, C_TRI, C_STRICT, C_ONES, C_IOTA = 0, 128, 256, 384, 512
C_LOW, C_ROFF, C_ITEM, C_ITEMS, C_FLIP, C_HOT = 640, 704, 800, 808, 904, 1032
C_CONVW = C_HOT + 384
C_CONVB = C_CONVW + NXB * CONV
C_SSDG = C_CONVB + NXB
C_DSKIP = C_SSDG + XS_BLOCKS
C_SUBLN = C_DSKIP + XS_BLOCKS
C_RB = C_SUBLN + 8
C_WDT = C_RB + 8
C_WR = C_WDT + KB * SSD_HEADS
N_SMALL = C_WR + KB * EXPERTS
R_DTB, R_ALOG, R_LAM, R_RB = 0, 32, 64, 320
N_ROW = 384


def out_index(kind, k=0):
    return FIRST_OUT[TILE_OF[kind]] + k


def taken_count(n):
    by = OUT_KIND[n] in BY_DVE
    return sum((k in BY_DVE) == by for k in OUT_KIND[:n + 1])


def layer_kernel(nc, small, rows, lnp, xT_in, memT_in, x_in, wstream, wshd, out):
    ctx = ExitStack()
    with ctx:
        def sb(name, shape, offset, dt=F32):
            return nc.alloc_sbuf_tensor_at(name, shape, dt, offset=offset)

        def sem(name):
            return ctx.enter_context(nc.semaphore(name))

        KIB = 1024
        at = 16512
        cs = sb("cs", [P, N_SMALL], at)
        at += N_SMALL * 4
        row = sb("row", [P, N_ROW], at)
        at += N_ROW * 4

        def tiny(name, shape, dt=F32):
            nonlocal at
            t = sb(name, shape, at, dt)
            at += (int(np.prod(shape[1:])) * 4 + 31) // 32 * 32
            return t

        dt_v = tiny("dt_v", [P, TB, SSD_HEADS])
        a_v = tiny("a_v", [P, TB, SSD_HEADS])
        dt_t = [tiny(f"dt_t{i}", [P, TB, SSD_HEADS]) for i in range(4)]
        exp_alog = tiny("exp_alog", [P, SSD_HEADS])
        decay_end = tiny("decay_end", [P, SSD_HEADS])
        lam_d = tiny("lam_d", [P, 2])
        lam_e = tiny("lam_e", [P, 2])
        neg_lam = tiny("neg_lam", [P, 1])
        lam_tmp = tiny("lam_tmp", [P, 64])
        a_max = tiny("a_max", [P, 4])
        a_neg = tiny("a_neg", [P, 4])
        a_sum = tiny("a_sum", [P, 4])
        a_rcp = tiny("a_rcp", [P, 4])
        c_neg = tiny("c_neg", [P, MEM_HEADS, TB])
        c_sum = tiny("c_sum", [P, MEM_HEADS, TB])
        c_rcp = tiny("c_rcp", [P, MEM_HEADS, TB])
        bn = tiny("bn", [P, TB, 2, 6])
        mv = tiny("mv", [P, TB, 2])
        rvar = tiny("rvar", [P, TB])
        rstd = tiny("rstd", [P, TB])
        max8 = tiny("max8", [P, TB, EGROUPS, 8])
        gsc = tiny("gsc", [P, TB, EGROUPS])
        gcmp = tiny("gcmp", [P, TB, EGROUPS, EGROUPS])
        geq = tiny("geq", [P, TB, EGROUPS, EGROUPS])
        gmask = tiny("gmask", [P, TB, EGROUPS])
        goff = tiny("goff", [P, TB, EGROUPS])
        top8 = tiny("top8", [P, TB, 8])
        w_sum = tiny("w_sum", [P, TB])
        w_rcp = tiny("w_rcp", [P, TB])
        slot_gate = tiny("slot_gate", [P, 1])
        place_off = tiny("place_off", [P, TB, 2])
        pair_n = tiny("pair_n", [P, PAIRS])
        item_col = tiny("item_col", [P, 2], I32)
        item_f = tiny("item_f", [P, 2])
        items = tiny("items", [P, P + 1], I32)
        place_e = tiny("place_e", [P, TB, EXPERTS + PER_GROUP])
        gates_e = tiny("gates_e", [P, TB, EXPERTS])
        RING0 = 131040
        W0 = RING0 - 6176 - 88 * KIB
        assert at <= W0, (at, W0)
        A = W0
        G = A + 8 * KIB
        FR = G + 8 * KIB
        E = FR + 8 * KIB
        C = E + 16 * KIB
        Z = C + 16 * KIB
        H = Z + 16 * KIB
        L = H + 16 * KIB
        SL3 = RING0 + 3 * 16 * KIB
        SL4 = SL3 + 16 * KIB
        ring = sb("ring", [P, RING, TILE], RING0)
        xT = sb("xT", [P, KB, SEQ], A)
        mixT = sb("mixT", [P, KB, SEQ], A)
        rel = sb("rel", [P, DIFF_HEADS, SEQ], G)
        rel_flipped = sb("rel_flipped", [P, DIFF_HEADS, SEQ], H)
        lnw = sb("lnw", [P, 2, D], G)
        v = sb("v", [P, TB, D], FR)
        qT = sb("qT", [P, DIFF_HEADS, SEQ], E)
        kT = sb("kT", [P, DIFF_HEADS, SEQ], E + 8 * KIB)
        oT = qT
        xsdt = sb("xsdt", [P, TB, INNER], C)
        sqd = sb("sqd", [P, DIFF_HEADS, SEQ], C)
        xres = sb("xres", [P, TB, D], C + 8 * KIB)
        z = sb("z", [P, XS_BLOCKS, SEQ], Z)
        gt = sb("gt", [P, 2 * KB, SEQ], H)
        xc = sb("xc", [P, NXB, SEQ], SL4)
        cbm = sb("cbm", [P, GROUPS, 3 * P], SL4 + XS_BLOCKS * KIB)
        memT = sb("memT", [P, KB, SEQ], SL4 + 24 * KIB)
        lg = sb("lg", [P, 768], L)
        attn = sb("attn", [P, 384], L + 3072)
        attnT = sb("attnT", [P, 384], L + 4608)
        dec = sb("dec", [P, TB, 4, P], SL3)
        gdec = sb("gdec", [P, TB, 4, P], SL3 + 4 * KIB)
        bds = sb("bds", [P, 384], SL3)
        PADDED = SEQ + CONV - 1
        xpad = sb("xpad", [P, 4, PADDED], SL3 + 8 * KIB)
        acc = sb("acc", [P, 2, SEQ], SL3 + 8 * KIB + 4160)
        fac = sb("fac", [P, 2, P], SL3 + 8 * KIB)
        yo = sb("yo", [P, 2, P], SL3 + 9 * KIB)
        xend = sb("xend", [P, 4, HEAD], SL3 + 10 * KIB)
        dtmp = sb("dtmp", [P, 512], SL3 + 11 * KIB)
        rms = sb("rms", [P, 8, 512], SL3)
        kcT = sb("kcT", [P, KB, SEQ], E + 8 * KIB)
        vc = sb("vc", [P, TB, D], FR)
        x1T = sb("x1T", [P, KB, SEQ], Z)
        qcT = sb("qcT", [P, KB, SEQ], Z + 8 * KIB)
        pc = sb("pc", [P, MEM_HEADS, TB, SEQ], H)
        pcT = sb("pcT", [P, MEM_HEADS, TB, SEQ], H + 8 * KIB)
        ocT = sb("ocT", [P, KB, SEQ], A)
        x2T = sb("x2T", [P, KB, SEQ], FR)
        scores = sb("scores", [P, TB, EXPERTS], Z)
        choice = sb("choice", [P, TB, EXPERTS], Z + 512)
        masked = sb("masked", [P, TB, EXPERTS], Z + 1024)
        sel = sb("sel", [P, TB, EXPERTS], Z + 1536)
        flags = sb("flags", [P, 2, EXTRA], Z + 2048)
        item_eq = sb("item_eq", [P, EXTRA], Z + 2048 + 1024)
        wsd = sb("wsd", [P, 2, D], G)
        x2h = sb("x2h", [P, TB, D], E, F32R)
        x2l = sb("x2l", [P, TB, D], E + 8 * KIB, F32R)
        onehot = sb("onehot", [P, 2, TB, PER_GROUP, SLOTS], A, F32R)
        yh = sb("yh", [P, D], C, F32R)
        yl = sb("yl", [P, D], C + 4 * KIB, F32R)
        xg = [sb("xg0", [P, KB, PER_GROUP * SLOTS], H), sb("xg1", [P, KB, PER_GROUP * SLOTS], Z)]
        ln3 = sb("ln3", [P, 2, D], Z)
        scatT = sb("scatT", [P, SEQ], FR, F32R)
        ident_r = sb("ident_r", [P, P], FR + 1 * KIB, F32R)
        hT = sb("hT", [P, 2, P], FR + 2 * KIB)
        hsT = sb("hsT", [P, 2, SEQ], L)
        h1 = sb("h1", [P, FF], L + 2 * KIB)
        hh = sb("hh", [P, FF], L + 3 * KIB)

        S = [ctx.enter_context(nc.psum_tensor(f"stream{i}", [P, 512], F32)) for i in range(4)]
        W = [ctx.enter_context(nc.psum_tensor(f"work{i}", [P, 512], F32)) for i in range(4)]

        ident = cs[:, C_ID:C_ID + P]
        tri = cs[:, C_TRI:C_TRI + P]
        strict = cs[:, C_STRICT:C_STRICT + P]
        flip = cs[:, C_FLIP:C_FLIP + P]
        ones = cs[:, C_ONES:C_ONES + P]
        slot_no = cs[:, C_IOTA:C_IOTA + SLOTS]
        part_no = cs[:, C_ITEM + 1:C_ITEM + 2]
        lower8 = cs[:, C_LOW:C_LOW + 64].rearrange("p (i j) -> p i j", i=8)
        conv_w = cs[:, C_CONVW:C_CONVW + NXB * CONV].rearrange("p (b j) -> p b j", j=CONV)
        conv_b = cs[:, C_CONVB:C_CONVB + NXB]
        ssd_g = cs[:, C_SSDG:C_SSDG + XS_BLOCKS]
        d_skip = cs[:, C_DSKIP:C_DSKIP + XS_BLOCKS]
        subln = cs[:, C_SUBLN:C_SUBLN + 1]
        w_dt = cs[:, C_WDT:C_WDT + KB * SSD_HEADS].rearrange("p (k h) -> p k h", k=KB)
        w_router = cs[:, C_WR:C_WR + KB * EXPERTS].rearrange("p (k e) -> p k e", k=KB)
        rel_scratch = nc.dram_tensor("rel_scratch", [DIFF_HEADS, 384], F32, kind="Internal").ap()

        small_in = sem("small_in")
        xT_ld = sem("xT_ld")
        memT_ld = sem("memT_ld")
        rel_stored = sem("rel_stored")
        rel_ld = sem("rel_ld")
        ln_ld = [sem(f"ln{i}_ld") for i in range(3)]
        xres_ld = sem("xres_ld")
        wsd_ld = sem("wsd_ld")
        items_ld = sem("items_ld")
        dense_ld = [sem(f"dense_ld{i}") for i in range(DENSE_RING)]
        expert_ld = [sem(f"expert_ld{i}") for i in range(RING)]
        extra_ld = sem("extra_ld")
        stored = sem("stored")
        proj_ready = sem("proj_ready")
        rel_mm = sem("rel_mm")
        flip_mm = sem("flip_mm")
        dt_mm = sem("dt_mm")
        end_mm = sem("end_mm")
        cb_mm = sem("cb_mm")
        xs_mm = sem("xs_mm")
        seg_mm = sem("seg_mm")
        logit_mm = sem("logit_mm")
        y_mm = sem("y_mm")
        off_mm = sem("off_mm")
        attnT_mm = sem("attnT_mm")
        av_mm = sem("av_mm")
        ssq_mm = sem("ssq_mm")
        xt_mm = sem("xt_mm")
        clog_mm = sem("clog_mm")
        cpT_mm = sem("cpT_mm")
        cav_mm = sem("cav_mm")
        score_mm = sem("score_mm")
        hsT_mm = sem("hsT_mm")
        rank_mm = sem("rank_mm")
        gath_mm = sem("gath_mm")
        gu_mm = sem("gu_mm")
        scatT_mm = sem("scatT_mm")
        hT_mm = sem("hT_mm")
        down_mm = sem("down_mm")
        moe_mm = sem("moe_mm")
        act_took = sem("act_took")
        xpad_full = sem("xpad_full")
        conv_silu = sem("conv_silu")
        small_exp = sem("small_exp")
        flip_cp = sem("flip_cp")
        seg_exp = sem("seg_exp")
        prob_exp = sem("prob_exp")
        fac_exp = sem("fac_exp")
        attnT_cp = sem("attnT_cp")
        av_cp = sem("av_cp")
        z_silu = sem("z_silu")
        squared = sem("squared")
        gate_sig = sem("gate_sig")
        rms_sqrt = sem("rms_sqrt")
        ln_sqrt = sem("ln_sqrt")
        xt_cp = sem("xt_cp")
        cprob_exp = sem("cprob_exp")
        cpT_cp = sem("cpT_cp")
        cav_cp = sem("cav_cp")
        score_sig = sem("score_sig")
        sh_silu = sem("sh_silu")
        hsT_cp = sem("hsT_cp")
        split_h = sem("split_h")
        gath_act = sem("gath_act")
        h_silu = sem("h_silu")
        hT_cp = sem("hT_cp")
        yh_done = sem("yh_done")
        dve = sem("dve_chain")
        dve_took = sem("dve_took")
        pad_zero = sem("pad_zero")
        rel_cp = sem("rel_cp")
        conv_done = sem("conv_done")
        lam_dots = sem("lam_dots")
        dt_pre = sem("dt_pre")
        a_done = sem("a_done")
        cb_cp = sem("cb_cp")
        xs_cp = sem("xs_cp")
        amax_done = sem("amax_done")
        masked_dec = sem("masked_dec")
        attn_done = sem("attn_done")
        y_done = sem("y_done")
        yz_done = sem("yz_done")
        rms_rcp = sem("rms_rcp")
        yT_done = sem("yT_done")
        oT_done = sem("oT_done")
        mix_done = sem("mix_done")
        ln_var = sem("ln_var")
        ln_done = sem("ln_done")
        cmax_done = sem("cmax_done")
        cprob_done = sem("cprob_done")
        sh_done = sem("sh_done")
        sel_done = sem("sel_done")
        place_done = sem("place_done")
        onehot_done = sem("onehot_done")
        split_l = sem("split_l")
        gath_dve = sem("gath_dve")
        h_done = sem("h_done")
        scatT_cp = sem("scatT_cp")
        gate_cp = sem("gate_cp")
        yl_done = sem("yl_done")
        item_done = sem("item_done")
        gdec_done = sem("gdec_done")
        xend_done = sem("xend_done")
        o_hot, o_gath, o_xg, o_gu, o_h1, o_h, o_T, o_Tcp, o_down, o_y, o_scat = (
            sem(n) for n in ("o_hot", "o_gath", "o_xg", "o_gu", "o_h1", "o_h", "o_T", "o_Tcp", "o_down", "o_y",
                             "o_scat"))

        block = ctx.enter_context(nc.Block())

        def expert_tile(jj, kind):
            return (3 * jj + kind + 3) % RING

        def expert_count(i, jj, kind):
            return (i * (3 * 8 // RING) + (3 * jj + kind) // RING + 1) * 16

        @block.sync
        def _(sp):
            sp.dma_start(cs[:], small).then_inc(small_in, 16)
            sp.dma_start(row[:], rows.partition_broadcast(P)).then_inc(small_in, 16)
            sp.dma_start(xT[:], xT_in).then_inc(xT_ld, 16)

            def dense_tile(t):
                slot = (t + 2) % DENSE_RING
                if t >= DENSE_RING:
                    sp.wait_ge(proj_ready, FIRST_OUT[t - DENSE_RING + 1])
                sp.dma_start(ring[:, slot, :], wstream[t]).then_inc(dense_ld[slot], 16)

            for t in range(3):
                dense_tile(t)
            sp.dma_start(memT[:], memT_in).then_inc(memT_ld, 16)
            sp.wait_ge(rel_cp, 1)
            sp.dma_start(rel_scratch, bds[0:DIFF_HEADS, :]).then_inc(rel_stored, 16)
            sp.wait_ge(rel_stored, 16)
            sp.dma_start(rel_flipped[:], bass.AP(rel_scratch.tensor, 0, [[1, P], [384, DIFF_HEADS], [1, SEQ]])
                         ).then_inc(rel_ld, 16)
            for t in range(3, TILE_OF["cq"] + 2):
                dense_tile(t)
            sp.wait_ge(oT_done, 2 * GROUPS)
            sp.dma_start(ring[:, 3, :], wstream[N_DENSE]).then_inc(expert_ld[3], 16)
            sp.dma_start(ring[:, 4, :], wstream[N_DENSE + 1]).then_inc(expert_ld[4], 16)
            sp.dma_start(ring[:, 5, :], wstream[N_DENSE + 2]).then_inc(expert_ld[5], 16)
            for t in range(TILE_OF["co"], N_DENSE):
                dense_tile(t)
            for x in range(3, RING):
                sp.wait_ge(proj_ready, FIRST_OUT[N_DENSE - RING + x + 1])
                sp.dma_start(ring[:, x - 3, :], wstream[N_DENSE + x]).then_inc(expert_ld[x - 3], 16)
            with sp.Fori(0, 3 * PAIRS // RING - 1) as k:
                for m in range(RING):
                    if m % 3 < 2:
                        sp.wait_ge(gu_mm, k * 2 + (m // 3 + 1))
                    else:
                        sp.wait_ge(down_mm, k * 4 + 2 * (m // 3 + 1))
                    slot = (m + 3) % RING
                    sp.dma_start(ring[:, slot, :], wstream[k * RING + (N_DENSE + RING + m)]
                                 ).then_inc(expert_ld[slot], 16)
            sp.wait_ge(items_ld, 32)
            n_items = sp.value_load(items[0:1, P:P + 1], min_val=0, max_val=EXTRA)
            sp.wait_ge(down_mm, 2 * PAIRS)
            with sp.If(n_items > 0):
                with sp.Fori(0, n_items) as i:
                    item = sp.value_load(items[0:1, bass.ds(i, 1)], min_val=0, max_val=EXTRA - 1)
                    sp.wait_ge(o_scat, i)
                    for m in range(3):
                        sp.dma_start(ring[:, m, :], wstream[(item % PAIRS) * 3 + (N_DENSE + m)]
                                     ).then_inc(extra_ld, 16)
            for t in range(TB):
                sp.wait_ge(ln_done, 3 * TB - TB + t + 1)
                sp.dma_start(out[0, t * P:(t + 1) * P, :], xres[:, t, :]).then_inc(stored, 16)
            sp.wait_ge(stored, 16 * TB)

        @block.gpsimd
        def _(pool):
            for i in range(XS_BLOCKS // 2):
                for t in range(TB):
                    if i == 0:
                        pool.wait_ge(a_done, 1)
                    else:
                        pool.wait_ge(seg_mm, 2 * (i - 1) + t + 1)
                    nc.gpsimd.tensor_tensor(gdec[:, t], strict.unsqueeze(1).to_broadcast([P, 4, P]),
                                            a_v[:, t, 4 * i:4 * i + 4].unsqueeze(2).to_broadcast([P, 4, P]),
                                            ALU.mult).then_inc(gdec_done, 1)
                if i == 0:
                    pool.wait_ge(small_exp, 3)
                    pool.wait_ge(xs_cp, 8)
                else:
                    pool.wait_ge(off_mm, i)
                nc.gpsimd.tensor_tensor(xend[:], xsdt[:, 0, 256 * i:256 * i + 256].rearrange("p (h e) -> p h e", h=4),
                                        decay_end[:, 4 * i:4 * i + 4].unsqueeze(2).to_broadcast([P, 4, HEAD]),
                                        ALU.mult).then_inc(xend_done, 1)
            pool.wait_ge(y_mm, XS_BLOCKS // 2)
            pool.wait_ge(off_mm, XS_BLOCKS // 2)
            pool.wait_ge(xend_done, XS_BLOCKS // 2)
            pool.dma_start(xres[:], x_in).then_inc(xres_ld, 16)
            pool.wait_ge(attn_done, DIFF_HEADS)
            pool.dma_start(lnw[:], lnp[0:1].rearrange("a b d -> (a b) d").partition_broadcast(P)).then_inc(ln_ld[0], 16)
            pool.wait_ge(ln_done, TB)
            pool.dma_start(lnw[:], lnp[1:2].rearrange("a b d -> (a b) d").partition_broadcast(P)).then_inc(ln_ld[1], 16)
            pool.wait_ge(ln_done, 2 * TB)
            pool.dma_start(wsd[:], wshd).then_inc(wsd_ld, 16)
            pool.wait_ge(item_done, 2)
            pool.dma_start(items[0:1, 0:P], item_col[:, 0:1]).then_inc(items_ld, 16)
            pool.dma_start(items[0:1, P:P + 1], item_col[0:1, 1:2]).then_inc(items_ld, 16)
            pool.wait_ge(gu_mm, PAIRS)
            pool.dma_start(ln3[:], lnp[2:3].rearrange("a b d -> (a b) d").partition_broadcast(P)).then_inc(ln_ld[2], 16)

        @block.scalar
        def _(act):
            taken = [0]

            def took(ins, n):
                ins.then_inc(act_took, 1)

            act.wait_ge(small_in, 32)
            act.wait_ge(lam_dots, 2)
            nc.scalar.activation(exp_alog[:], row[:, R_ALOG:R_ALOG + SSD_HEADS], ACT.Exp).then_inc(small_exp, 1)
            nc.scalar.activation(lam_e[:], lam_d[:], ACT.Exp).then_inc(small_exp, 1)

            def conv_act(b):
                act.wait_ge(conv_done, b + 1)
                nc.scalar.activation(xc[:, b, :], acc[:, b % 2, :], ACT.Silu, bias=conv_b[:, b:b + 1]
                                     ).then_inc(conv_silu, 1)

            act.wait_ge(pad_zero, 1)
            for b in range(NXB):
                n = out_index("xbc", b)
                act.wait_ge(proj_ready, n + 1)
                if b >= 4:
                    act.wait_ge(conv_done, b - 3)
                nc.scalar.activation(xpad[:, b % 4, CONV - 1:PADDED], S[n % 4][:, 0:SEQ], ACT.Copy
                                     ).then_inc(act_took, 1)
                if b >= 1:
                    conv_act(b - 1)
            conv_act(NXB - 1)
            act.wait_ge(dt_pre, 1)
            nc.scalar.activation(dt_t[1][:], dt_t[1][:], ACT.Exp, scale=-1.0).then_inc(small_exp, 1)

            def leave(kind, k, dst, scale=1.0, cols=SEQ):
                n = out_index(kind, k)
                act.wait_ge(proj_ready, n + 1)
                nc.scalar.activation(dst, S[n % 4][:, 0:cols], ACT.Copy, scale=scale).then_inc(act_took, 1)

            for h in range(DIFF_HEADS):
                leave("q", h, qT[:, h, :], scale=HEAD ** -0.5)
            for h in range(DIFF_HEADS):
                leave("k", h, kT[:, h, :])
            for k in range(4):
                act.wait_ge(flip_mm, k + 1)
                nc.scalar.activation(rel[:, 2 * k:2 * k + 2, :], W[k][:].rearrange("p (h k) -> p h k", h=2), ACT.Copy
                                     ).then_inc(flip_cp, 1)
            act.wait_ge(end_mm, 1)
            nc.scalar.activation(decay_end[:], W[0][:, 0:SSD_HEADS], ACT.Exp).then_inc(small_exp, 1)
            for k in range(4):
                leave("v", k, v[:, k % TB, k // TB * 512:k // TB * 512 + 512], cols=512)

            for i in range(8):
                for t in range(TB):
                    act.wait_ge(seg_mm, 2 * i + t + 1)
                    if i >= 1:
                        act.wait_ge(y_mm, i)
                    nc.scalar.activation(dec[:, t], W[2 + t][:].rearrange("p (h l) -> p h l", h=4), ACT.Exp
                                         ).then_inc(seg_exp, 1)
                act.wait_ge(amax_done, i + 1)
                for c, (o, w) in enumerate(((0, P), (P, SEQ), (P + SEQ, P), (2 * P + SEQ, SEQ))):
                    nc.scalar.activation(lg[:, o:o + w], lg[:, o:o + w], ACT.Exp, bias=a_neg[:, c:c + 1],
                                         accum_out=a_sum[:, c:c + 1]).then_inc(prob_exp, 1)
                kind, dst = ("z", z) if i < 4 else ("gate", gt)
                k0 = 4 * (i % 4)
                leave(kind, k0, dst[:, k0, :])
                leave(kind, k0 + 1, dst[:, k0 + 1, :])
                act.wait_ge(off_mm, i + 1)
                if i >= 1:
                    act.wait_ge(y_done, i)
                nc.scalar.activation(fac[:], W[3][:, SEQ:2 * SEQ].rearrange("p (b l) -> p b l", b=2), ACT.Exp
                                     ).then_inc(fac_exp, 1)
                act.wait_ge(attnT_mm, i + 1)
                if i >= 1:
                    act.wait_ge(av_mm, i)
                nc.scalar.activation(attnT[:], W[0][:, 0:384], ACT.Copy).then_inc(attnT_cp, 1)
                leave(kind, k0 + 2, dst[:, k0 + 2, :])
                leave(kind, k0 + 3, dst[:, k0 + 3, :])
                act.wait_ge(av_mm, i + 1)
                nc.scalar.activation(oT[:, i, :], W[1][:, 0:SEQ], ACT.Copy).then_inc(av_cp, 1)

            act.wait_ge(act_took, taken_count(out_index("z", 15)))
            for g in range(GROUPS):
                nc.scalar.activation(z[:, 4 * g:4 * g + 4, :], z[:, 4 * g:4 * g + 4, :], ACT.Silu).then_inc(z_silu, 1)
            for k in range(4):
                leave("ck", k, kcT[:, k, :])
            for g in range(GROUPS):
                act.wait_ge(yz_done, g + 1)
                nc.scalar.activation(z[:, 4 * g:4 * g + 4, :], xc[:, 4 * g:4 * g + 4, :], ACT.Square
                                     ).then_inc(squared, 1)
                if g == 1:
                    for k in range(4, 8):
                        leave("ck", k, kcT[:, k, :])
            act.wait_ge(av_cp, DIFF_HEADS)
            for k in range(4):
                nc.scalar.activation(sqd[:, 2 * k:2 * k + 2, :], oT[:, 2 * k:2 * k + 2, :], ACT.Square
                                     ).then_inc(squared, 1)
            for k in range(4):
                leave("cv", k, vc[:, k % TB, k // TB * 512:k // TB * 512 + 512], cols=512)
            act.wait_ge(act_took, taken_count(out_index("gate", 15)))
            for g in range(GROUPS):
                nc.scalar.activation(gt[:, 4 * g:4 * g + 4, :], gt[:, 4 * g:4 * g + 4, :], ACT.Sigmoid
                                     ).then_inc(gate_sig, 1)
            for k in range(2 * GROUPS):
                w = SEQ if k < GROUPS else 512
                act.wait_ge(rms_rcp, k + 1)
                nc.scalar.activation(rms[:, k, 0:w], rms[:, k, 0:w], ACT.Sqrt).then_inc(rms_sqrt, 1)

            def norm_sqrt(which):
                for t in range(TB):
                    act.wait_ge(ln_var, TB * which + t + 1)
                    nc.scalar.activation(rstd[:, t:t + 1], rvar[:, t:t + 1], ACT.Sqrt).then_inc(ln_sqrt, 1)

            def turned(which, dst):
                for k in range(4):
                    act.wait_ge(xt_mm, 4 * which + k + 1)
                    nc.scalar.activation(dst[:, 4 * (k % 2):4 * (k % 2) + 4, k // 2 * P:(k // 2 + 1) * P],
                                         W[k][:].rearrange("p (b t) -> p b t", b=4), ACT.Copy).then_inc(xt_cp, 1)

            norm_sqrt(0)
            turned(0, x1T)
            for k in range(KB):
                leave("cq", k, qcT[:, k, :], scale=(D // MEM_HEADS) ** -0.5)
            for h in range(MEM_HEADS):
                act.wait_ge(cmax_done, h + 1)
                for t in range(TB):
                    nc.scalar.activation(pc[:, h, t, :], W[h][:, t * SEQ:(t + 1) * SEQ], ACT.Exp,
                                         bias=c_neg[:, h, t:t + 1], accum_out=c_sum[:, h, t:t + 1]
                                         ).then_inc(cprob_exp, 1)
            for h in range(MEM_HEADS):
                act.wait_ge(cpT_mm, h + 1)
                nc.scalar.activation(pcT[:, h], W[h][:].rearrange("p (k q) -> p k q", k=2), ACT.Copy
                                     ).then_inc(cpT_cp, 1)
            for h in range(MEM_HEADS):
                act.wait_ge(cav_mm, h + 1)
                nc.scalar.activation(ocT[:, 2 * h:2 * h + 2, :], W[h][:].rearrange("p (k q) -> p k q", k=2), ACT.Copy
                                     ).then_inc(cav_cp, 1)
            norm_sqrt(1)
            turned(1, x2T)
            act.wait_ge(score_mm, 1)
            nc.scalar.activation(scores[:], W[0][:, 0:TB * EXPERTS].rearrange("p (t e) -> p t e", t=TB), ACT.Sigmoid
                                 ).then_inc(score_sig, 1)
            for t in range(TB):
                act.wait_ge(ln_done, TB + t + 1)
                nc.scalar.activation(x2h[:, t, :], xres[:, t, :], ACT.Copy).then_inc(split_h, 1)
            act.wait_ge(xt_mm, 8)
            act.wait_ge(proj_ready, out_index("sh", 0) + 1)
            for t in range(TB):
                n = out_index("sh", t)
                act.wait_ge(proj_ready, n + 1)
                if t:
                    act.wait_ge(sh_done, t)
                nc.scalar.activation(h1[:], S[n % 4][:, 0:FF], ACT.Silu).then_inc(sh_silu, 1)
                act.wait_ge(hsT_mm, t + 1)
                nc.scalar.activation(hsT[:, :, t * P:(t + 1) * P],
                                     W[1][:, t * SEQ:(t + 1) * SEQ].rearrange("p (k q) -> p k q", k=2), ACT.Copy
                                     ).then_inc(hsT_cp, 1)
            nc.scalar.activation(ident_r[:], ident, ACT.Copy).then_inc(hsT_cp, 1)
            for k in range(0, KB, 2):
                act.wait_ge(gath_mm, k + 1)
                nc.scalar.activation(xg[0][:, k, :], S[0][:], ACT.Copy).then_inc(gath_act, 1)
            with act.Fori(0, PAIRS // 8) as i:
                for jj in range(8):
                    act.wait_ge(gu_mm, i * 8 + (jj + 1))
                    nc.scalar.activation(h1[:], S[2][:, 0:FF], ACT.Silu).then_inc(h_silu, 1)
                    act.wait_ge(gath_mm, i * 16 + (KB + 2 * jj + 1))
                    nc.scalar.activation(xg[(jj // 4 + 1) % 2][:, 2 * (jj % 4), :], S[0][:], ACT.Copy
                                         ).then_inc(gath_act, 1)
                    act.wait_ge(hT_mm, i * 8 + (jj + 1))
                    nc.scalar.activation(hT[:], S[2][:, 0:2 * P].rearrange("p (k s) -> p k s", k=2), ACT.Copy
                                         ).then_inc(hT_cp, 1)
                    act.wait_ge(gate_cp, i * 16 + 2 * (jj + 1))
                    for c in range(2):
                        act.wait_ge(down_mm, i * 16 + (2 * jj + c + 1))
                        nc.scalar.activation(yh[:, c * 512:(c + 1) * 512], (S[3], S[1])[c][:], ACT.Copy,
                                             scale=slot_gate[:, 0:1]).then_inc(yh_done, 1)
            act.wait_ge(items_ld, 32)
            n_items = act.value_load(items[0:1, P:P + 1], min_val=0, max_val=EXTRA)
            with act.If(n_items > 0):
                with act.Fori(0, n_items) as i:
                    act.wait_ge(o_gu, i + 1)
                    nc.scalar.activation(h1[:], S[2][:, 0:FF], ACT.Silu).then_inc(o_h1, 1)
                    act.wait_ge(o_down, i + 1)
                    for c in range(2):
                        nc.scalar.activation(yh[:, c * 512:(c + 1) * 512], (S[3], S[1])[c][:], ACT.Copy,
                                             scale=slot_gate[:, 0:1]).then_inc(o_y, 1)
            norm_sqrt(2)

        @block.vector
        def _(ve):
            steps = [0]

            def link(ins):
                steps[0] += 1
                ins.then_inc(dve, 1)
                ve.wait_ge(dve, steps[0])

            tt = nc.vector.tensor_tensor
            ts = nc.vector.tensor_scalar
            stt = nc.vector.scalar_tensor_tensor

            link(nc.vector.memset(place_e[:], 0.0))
            nc.vector.memset(xpad[:], 0.0).then_inc(pad_zero, 1)
            ve.wait_ge(small_in, 32)
            ve.wait_ge(rel_mm, 1)
            nc.vector.tensor_copy(bds[0:DIFF_HEADS, :], W[0][0:DIFF_HEADS, 0:384]).then_inc(rel_cp, 1)
            for k in range(2):
                q = R_LAM + 128 * k
                link(tt(lam_tmp[:], row[:, q:q + 64], row[:, q + 64:q + 128], ALU.mult))
                nc.vector.tensor_reduce(lam_d[:, k:k + 1], lam_tmp[:], AX.X, ALU.add).then_inc(lam_dots, 1)
                ve.wait_ge(lam_dots, k + 1)
            ve.wait_ge(small_exp, 2)
            link(stt(neg_lam[:], lam_e[:, 1:2], -LAM_INIT, lam_e[:, 0:1], ALU.add, ALU.subtract))
            link(ts(exp_alog[:], exp_alog[:], -1.0, None, ALU.mult))

            ve.wait_ge(pad_zero, 1)
            for b in range(NXB):
                ve.wait_ge(act_took, b + 1)
                if b >= 2:
                    ve.wait_ge(conv_silu, b - 1)
                link(ts(acc[:, b % 2, :], xpad[:, b % 4, 0:SEQ], conv_w[:, b, 0:1], None, ALU.mult))
                for j in range(1, CONV):
                    ins = stt(acc[:, b % 2, :], xpad[:, b % 4, j:j + SEQ], conv_w[:, b, j:j + 1], acc[:, b % 2, :],
                              ALU.mult, ALU.add)
                    if j < CONV - 1:
                        link(ins)
                ins.then_inc(conv_done, 1)

            ve.wait_ge(dt_mm, 1)
            u, e, s, s2 = (x[:] for x in dt_t)
            raw = W[1][:, 0:TB * SSD_HEADS].rearrange("p (t h) -> p t h", t=TB)
            link(tt(u, raw, row[:, R_DTB:R_DTB + SSD_HEADS].unsqueeze(1).to_broadcast([P, TB, SSD_HEADS]), ALU.add))
            link(ts(s, u, -1.0, None, ALU.mult))
            tt(e, u, s, ALU.max).then_inc(dt_pre, 1)
            ve.wait_ge(small_exp, 3)
            link(ts(s, e, 2.0, None, ALU.add))
            link(nc.vector.reciprocal(s2, s))
            link(tt(s, e, s2, ALU.mult))
            link(tt(s2, s, s, ALU.mult))
            link(ts(e, s2, 1.0 / 15, 1.0 / 13, ALU.mult, ALU.add))
            for c in (11, 9, 7, 5, 3, 1):
                link(tt(e, e, s2, ALU.mult))
                link(ts(e, e, 1.0 / c, None, ALU.add))
            link(tt(e, e, s, ALU.mult))
            link(ts(u, u, 0.0, None, ALU.max))
            link(stt(dt_v[:], e, 2.0, u, ALU.mult, ALU.add))
            tt(a_v[:], dt_v[:], exp_alog[:].unsqueeze(1).to_broadcast([P, TB, SSD_HEADS]), ALU.mult
               ).then_inc(a_done, 1)

            ve.wait_ge(cb_mm, GROUPS)
            for g in range(GROUPS):
                bank = W[(1 + g) % 4]
                tt(cbm[:, g].rearrange("p (a l) -> p a l", a=3)[:, 0:3:2, :],
                   bank[:, 0:384].rearrange("p (a l) -> p a l", a=3)[:, 0:3:2, :],
                   tri.unsqueeze(1).to_broadcast([P, 2, P]), ALU.mult).then_inc(cb_cp, 1)
                nc.vector.tensor_copy(cbm[:, g, P:2 * P], bank[:, P:2 * P]).then_inc(cb_cp, 1)
            for k in range(8):
                t, quad = k // 4, k % 4
                ve.wait_ge(xs_mm, k + 1)
                tt(xsdt[:, t, quad * 512:(quad + 1) * 512].rearrange("p (h e) -> p h e", h=8),
                   W[(1 + k) % 4][:].rearrange("p (h e) -> p h e", h=8),
                   dt_v[:, t, quad * 8:(quad + 1) * 8].unsqueeze(2).to_broadcast([P, 8, HEAD]), ALU.mult
                   ).then_inc(xs_cp, 1)

            ve.wait_ge(flip_cp, 4)
            for i in range(8):
                ve.wait_ge(logit_mm, i + 1)
                if i >= 1:
                    ve.wait_ge(attnT_mm, i)
                for m in range(2):
                    o = m * 384
                    for c, (o2, w, r0) in enumerate(((0, P, P), (P, SEQ, 0))):
                        ins = nc.vector.tensor_tensor_reduce(
                            lg[:, o + o2:o + o2 + w], W[m][:, o2:o2 + w], rel[:, i, r0:r0 + w], 1.0, -3.0e38,
                            ALU.add, ALU.max, a_max[:, 2 * m + c:2 * m + c + 1])
                        link(ins)
                ts(a_neg[:], a_max[:], -1.0, None, ALU.mult).then_inc(amax_done, 1)
                for t in range(TB):
                    ve.wait_ge(seg_exp, 2 * i + t + 1)
                    tt(dec[:, t], dec[:, t],
                       cbm[:, i // 2, 2 * t * P:(2 * t + 1) * P].unsqueeze(1).to_broadcast([P, 4, P]), ALU.mult
                       ).then_inc(masked_dec, 1)
                ve.wait_ge(prob_exp, 4 * i + 4)
                link(nc.vector.reciprocal(a_rcp[:], a_sum[:]))
                link(ts(a_rcp[:, 2:4], a_rcp[:, 2:4], neg_lam[:, 0:1], None, ALU.mult))
                link(ts(dtmp[:, 0:P], lg[:, 384:384 + P], a_rcp[:, 2:3], None, ALU.mult))
                link(ts(dtmp[:, P:384], lg[:, 512:768], a_rcp[:, 3:4], None, ALU.mult))
                link(stt(attn[:, 0:P], lg[:, 0:P], a_rcp[:, 0:1], dtmp[:, 0:P], ALU.mult, ALU.add))
                stt(attn[:, P:384], lg[:, P:384], a_rcp[:, 1:2], dtmp[:, P:384], ALU.mult, ALU.add
                    ).then_inc(attn_done, 1)
                ve.wait_ge(y_mm, i + 1)
                for j in range(2):
                    b = 2 * i + j
                    link(stt(xc[:, b, :], xc[:, b, :], d_skip[:, b:b + 1], W[2][:, j * SEQ:(j + 1) * SEQ],
                             ALU.mult, ALU.add))
                ve.wait_ge(fac_exp, i + 1)
                link(tt(yo[:], W[3][:, 0:SEQ].rearrange("p (b l) -> p b l", b=2), fac[:], ALU.mult))
                tt(xc[:, 2 * i:2 * i + 2, P:SEQ], xc[:, 2 * i:2 * i + 2, P:SEQ], yo[:], ALU.add).then_inc(y_done, 1)

            for g in range(GROUPS):
                ve.wait_ge(z_silu, g + 1)
                ve.wait_ge(y_done, 2 * g + 2)
                tt(xc[:, 4 * g:4 * g + 4, :], xc[:, 4 * g:4 * g + 4, :], z[:, 4 * g:4 * g + 4, :], ALU.mult
                   ).then_inc(yz_done, 1)
            for k in range(2 * GROUPS):
                ssd = k < GROUPS
                w = SEQ if ssd else 512
                width, factor = (INNER // GROUPS, 1.0) if ssd else (P, SUBLN_SCALE ** 2)
                ve.wait_ge(ssq_mm, k + 1)
                link(ts(rms[:, k, 0:w], W[k % 4][:, 0:w], 1.0 / width / factor, EPS / factor, ALU.mult, ALU.add))
                nc.vector.reciprocal(rms[:, k, 0:w], rms[:, k, 0:w]).then_inc(rms_rcp, 1)
            ve.wait_ge(yz_done, GROUPS)
            for g in range(GROUPS):
                ve.wait_ge(rms_sqrt, g + 1)
                for j in range(4):
                    b = 4 * g + j
                    ins = stt(xc[:, b, :], xc[:, b, :], ssd_g[:, b:b + 1], rms[:, g, 0:SEQ], ALU.mult, ALU.mult)
                    ins.then_inc(yT_done, 1)
            for k in range(GROUPS):
                ve.wait_ge(rms_sqrt, GROUPS + k + 1)
                for j in range(2):
                    h = 2 * k + j
                    stt(oT[:, h, :], oT[:, h, :], subln, rms[:, GROUPS + k, j * SEQ:(j + 1) * SEQ],
                        ALU.mult, ALU.mult).then_inc(oT_done, 1)
            for k in range(KB):
                n = out_index("ssd", k)
                ve.wait_ge(proj_ready, n + 1)
                ve.wait_ge(gate_sig, k // 4 + 1)
                tt(mixT[:, k, :], S[n % 4][:, 0:SEQ], gt[:, k, :], ALU.mult).then_inc(dve_took, 1)
            for k in range(KB):
                n = out_index("diff", k)
                ve.wait_ge(proj_ready, n + 1)
                ve.wait_ge(gate_sig, 2 + k // 4 + 1)
                tt(gt[:, KB + k, :], S[n % 4][:, 0:SEQ], gt[:, KB + k, :], ALU.mult).then_inc(dve_took, 1)
                ve.wait_ge(dve_took, taken_count(n))
                tt(mixT[:, k, :], mixT[:, k, :], gt[:, KB + k, :], ALU.add).then_inc(mix_done, 1)

            def layer_norm(which, weights, residual):
                for t in range(TB):
                    for c in range(2):
                        link(nc.vector.bn_stats(bn[:, t, c, :], xres[:, t, c * 512:(c + 1) * 512]))
                    link(nc.vector.bn_aggr(mv[:, t, :], bn[:, t].rearrange("p c s -> p (c s)")))
                    link(ts(rvar[:, t:t + 1], mv[:, t, 1:2], EPS, None, ALU.add))
                    nc.vector.reciprocal(rvar[:, t:t + 1], rvar[:, t:t + 1]).then_inc(ln_var, 1)
                ve.wait_ge(ln_ld[which], 16)
                for t in range(TB):
                    ve.wait_ge(ln_sqrt, TB * which + t + 1)
                    link(ts(xres[:, t, :], xres[:, t, :], mv[:, t, 0:1], rstd[:, t:t + 1], ALU.subtract, ALU.mult))
                    link(tt(xres[:, t, :], xres[:, t, :], weights[:, 0, :], ALU.mult))
                    tt(xres[:, t, :], xres[:, t, :], weights[:, 1, :], ALU.add).then_inc(ln_done, 1)

            def add_output(kind):
                for k in range(4):
                    n = out_index(kind, k)
                    ve.wait_ge(proj_ready, n + 1)
                    half = xres[:, k % TB, k // TB * 512:k // TB * 512 + 512]
                    stt(half, half, ALPHA, S[n % 4][:], ALU.mult, ALU.add).then_inc(dve_took, 1)
                ve.wait_ge(dve_took, taken_count(out_index(kind, 3)))

            ve.wait_ge(xres_ld, 16)
            add_output("mix")
            layer_norm(0, lnw, None)
            for h in range(MEM_HEADS):
                ve.wait_ge(clog_mm, h + 1)
                nc.vector.tensor_reduce(c_neg[:, h, :], W[h][:].rearrange("p (t k) -> p t k", t=TB), AX.X, ALU.max,
                                        negate=True).then_inc(cmax_done, 1)
            for h in range(MEM_HEADS):
                ve.wait_ge(cprob_exp, TB * h + TB)
                link(nc.vector.reciprocal(c_rcp[:, h, :], c_sum[:, h, :]))
                for t in range(TB):
                    ts(pc[:, h, t, :], pc[:, h, t, :], c_rcp[:, h, t:t + 1], None, ALU.mult).then_inc(cprob_done, 1)
            ve.wait_ge(ln_done, TB)
            add_output("co")
            layer_norm(1, lnw, None)

            ve.wait_ge(score_sig, 1)
            link(tt(choice[:], scores[:], row[:, R_RB:R_RB + EXPERTS].unsqueeze(1).to_broadcast([P, TB, EXPERTS]),
                    ALU.add))
            for t in range(TB):
                for g in range(EGROUPS):
                    ins = nc.vector.max(max8[:, t, g, :], choice[:, t, 8 * g:8 * g + 8])
                    if g == EGROUPS - 1:
                        link(ins)
            link(tt(gsc[:], max8[:, :, :, 0], max8[:, :, :, 1], ALU.add))
            other = gsc[:].unsqueeze(2).to_broadcast([P, TB, EGROUPS, EGROUPS])
            own = gsc[:].unsqueeze(3).to_broadcast([P, TB, EGROUPS, EGROUPS])
            tt(gcmp[:], other, own, ALU.is_gt)
            link(tt(geq[:], other, own, ALU.is_equal))
            for t in range(TB):
                link(tt(geq[:, t], geq[:, t], lower8, ALU.mult))
            link(tt(gcmp[:], gcmp[:], geq[:], ALU.add))
            link(nc.vector.tensor_reduce(goff[:], gcmp[:], AX.X, ALU.add))
            link(ts(gmask[:], goff[:], TOP_GROUPS - 0.5, None, ALU.is_lt))
            link(ts(goff[:], gmask[:], -MASKED, MASKED, ALU.mult, ALU.add))
            for t in range(TB):
                by_group = masked[:, t].rearrange("p (g e) -> p g e", g=EGROUPS)
                link(tt(by_group, choice[:, t].rearrange("p (g e) -> p g e", g=EGROUPS),
                        gmask[:, t].unsqueeze(2).to_broadcast([P, EGROUPS, 8]), ALU.mult))
                link(tt(by_group, by_group, goff[:, t].unsqueeze(2).to_broadcast([P, EGROUPS, 8]), ALU.add))
            for t in range(TB):
                link(nc.vector.max(top8[:, t, :], masked[:, t, :]))
                link(nc.vector.match_replace(choice[:, t, :], top8[:, t, :], masked[:, t, :], -2.0 * MASKED))
            ts(sel[:], choice[:], -MASKED, None, ALU.is_gt).then_inc(sel_done, 1)
            ve.wait_ge(sel_done, 1)
            link(tt(gates_e[:], scores[:], sel[:], ALU.mult))
            link(nc.vector.tensor_reduce(w_sum[:], gates_e[:], AX.X, ALU.add))
            link(nc.vector.reciprocal(w_rcp[:], w_sum[:]))
            for t in range(TB):
                link(ts(gates_e[:, t, :], gates_e[:, t, :], w_rcp[:, t:t + 1], ROUTED_SCALE, ALU.mult, ALU.mult))
            ve.wait_ge(rank_mm, 1)
            tt(place_e[:, :, 0:EXPERTS], W[2][:, 0:TB * EXPERTS].rearrange("p (t e) -> p t e", t=TB), sel[:], ALU.mult
               ).then_inc(place_done, 1)
            ve.wait_ge(place_done, 1)

            def make_onehot(buf, first):
                for t in range(TB):
                    tt(onehot[:, buf, t], slot_no.unsqueeze(1).to_broadcast([P, PER_GROUP, SLOTS]),
                       place_e[:, t, first].unsqueeze(2).to_broadcast([P, PER_GROUP, SLOTS]), ALU.is_equal
                       ).then_inc(onehot_done, 1)

            make_onehot(0, slice(0, PER_GROUP))
            for t in range(TB):
                ve.wait_ge(split_h, t + 1)
                tt(x2l[:, t, :], xres[:, t, :], x2h[:, t, :].bitcast(F32), ALU.subtract).then_inc(split_l, 1)
            for t in range(TB):
                n = out_index("sh", t)
                ve.wait_ge(sh_silu, t + 1)
                if t:
                    ve.wait_ge(hsT_mm, t)
                tt(hh[:], h1[:], S[n % 4][:, FF:2 * FF], ALU.mult).then_inc(sh_done, 1)
            ve.wait_ge(place_done, 1)
            cnt = W[2][:, TB * EXPERTS:(TB + 1) * EXPERTS].rearrange("p (q e) -> p e q", e=2)
            link(nc.vector.tensor_copy(pair_n[:], cnt[:, 0, :]))
            tt(pair_n[:], pair_n[:], cnt[:, 1, :], ALU.max).then_inc(place_done, 1)
            ve.wait_ge(place_done, 2)
            for r in range(1, CHUNKS):
                ins = ts(flags[:, 0, (r - 1) * PAIRS:r * PAIRS], pair_n[:], SLOTS * r + 0.5, None, ALU.is_gt)
            link(ins)
            link(nc.vector.tensor_copy(item_eq[:], flags[:, 0, :]))
            cur, width = 0, 1
            while width < EXTRA:
                link(nc.vector.tensor_copy(flags[:, 1 - cur, 0:width], flags[:, cur, 0:width]))
                link(tt(flags[:, 1 - cur, width:EXTRA], flags[:, cur, width:EXTRA], flags[:, cur, 0:EXTRA - width],
                        ALU.add))
                cur, width = 1 - cur, 2 * width
            link(nc.vector.tensor_copy(item_f[:, 1:2], flags[:, cur, EXTRA - 1:EXTRA]))
            link(tt(item_eq[:], item_eq[:], flags[:, cur, :], ALU.mult))
            link(ts(item_eq[:], item_eq[:], part_no, None, ALU.is_equal))
            link(tt(item_eq[:], item_eq[:], cs[:, C_ITEMS:C_ITEMS + EXTRA],
                    ALU.mult))
            link(nc.vector.tensor_reduce(item_f[:, 0:1], item_eq[:], AX.X, ALU.add))
            nc.vector.tensor_copy(item_col[:], item_f[:]).then_inc(item_done, 2)
            for k in range(1, KB, 2):
                ve.wait_ge(gath_mm, k + 1)
                nc.vector.tensor_copy(xg[0][:, k, :], S[1][:]).then_inc(gath_dve, 1)
            with ve.Fori(0, PAIRS // 8) as i:
                for jj in range(8):
                    if jj % 4 == 0:
                        make_onehot((jj // 4 + 1) % 2, bass.ds(i * 16 + (8 * (jj // 4) + 8), PER_GROUP))
                    ve.wait_ge(h_silu, i * 8 + (jj + 1))
                    tt(hh[:], h1[:], S[2][:, FF:2 * FF], ALU.mult).then_inc(h_done, 1)
                    ve.wait_ge(scatT_mm, i * 8 + (jj + 1))
                    for c in range(2):
                        r = slice(c * SLOTS, (c + 1) * SLOTS)
                        nc.vector.tensor_copy(slot_gate[r, :], S[0][r, SEQ + c:SEQ + c + 1]).then_inc(gate_cp, 1)
                    nc.vector.tensor_copy(scatT[:], S[0][:, 0:SEQ]).then_inc(scatT_cp, 1)
                    ve.wait_ge(gath_mm, i * 16 + (KB + 2 * jj + 2))
                    nc.vector.tensor_copy(xg[(jj // 4 + 1) % 2][:, 2 * (jj % 4) + 1, :], S[0][:]).then_inc(gath_dve, 1)
                    for c in range(2):
                        ve.wait_ge(yh_done, i * 16 + (2 * jj + c + 1))
                        stt(yl[:, c * 512:(c + 1) * 512], (S[3], S[1])[c][:], slot_gate[:, 0:1],
                            yh[:, c * 512:(c + 1) * 512].bitcast(F32), ALU.mult, ALU.subtract).then_inc(yl_done, 1)
            ve.wait_ge(items_ld, 32)
            n_items = ve.value_load(items[0:1, P:P + 1], min_val=0, max_val=EXTRA)
            with ve.If(n_items > 0):
                with ve.Fori(0, n_items) as i:
                    item = ve.value_load(items[0:1, bass.ds(i, 1)], min_val=0, max_val=EXTRA - 1)
                    ve.wait_ge(o_scat, i)
                    for t in range(TB):
                        ts(place_off[:, t, :], place_e[:, t, bass.ds((item % PAIRS) * 2, 2)],
                           cs[:, bass.ds(item + C_ROFF, 1)], None, ALU.subtract).then_inc(o_hot, 1)
                    ve.wait_ge(o_hot, i * 4 + 2)
                    for t in range(TB):
                        tt(onehot[:, 0, t, 0:2, :], slot_no.unsqueeze(1).to_broadcast([P, 2, SLOTS]),
                           place_off[:, t, :].unsqueeze(2).to_broadcast([P, 2, SLOTS]), ALU.is_equal
                           ).then_inc(o_hot, 1)
                    ve.wait_ge(o_gath, i + 1)
                    for c in range(2):
                        nc.vector.tensor_copy(xg[0][:, 4 * c:4 * c + 4, 0:P],
                                              S[c][:].rearrange("p (k s) -> p k s", k=4)).then_inc(o_xg, 1)
                    ve.wait_ge(o_h1, i + 1)
                    tt(hh[:], h1[:], S[2][:, FF:2 * FF], ALU.mult).then_inc(o_h, 1)
                    ve.wait_ge(o_T, i + 1)
                    for c in range(2):
                        r = slice(c * SLOTS, (c + 1) * SLOTS)
                        nc.vector.tensor_copy(slot_gate[r, :], S[0][r, SEQ + c:SEQ + c + 1]).then_inc(o_Tcp, 1)
                    nc.vector.tensor_copy(scatT[:], S[0][:, 0:SEQ]).then_inc(o_Tcp, 1)
                    nc.vector.tensor_copy(hT[:], S[2][:, 0:2 * P].rearrange("p (k s) -> p k s", k=2)
                                          ).then_inc(o_Tcp, 1)
                    ve.wait_ge(o_y, i * 4 + 2)
                    for c in range(2):
                        stt(yl[:, c * 512:(c + 1) * 512], (S[3], S[1])[c][:], slot_gate[:, 0:1],
                            yh[:, c * 512:(c + 1) * 512].bitcast(F32), ALU.mult, ALU.subtract).then_inc(o_y, 1)
            ve.wait_ge(moe_mm, 1)
            for t in range(TB):
                for c in range(2):
                    half = xres[:, t, c * 512:(c + 1) * 512]
                    link(stt(half, half, ALPHA, W[2 * t + c][:], ALU.mult, ALU.add))
            layer_norm(2, ln3, None)

        @block.tensor
        def _(pe):
            mm = nc.tensor.matmul

            def bank_free(n):
                if n >= 4:
                    pe.wait_ge(dve_took if OUT_KIND[n - 4] in BY_DVE else act_took, taken_count(n - 4))

            def tile_here(t):
                slot = (t + 2) % DENSE_RING
                pe.wait_ge(dense_ld[slot], 16 * (t // DENSE_RING + 1))
                return slot

            def feature_major(kind, k, act_T, kbs=KB):
                n = out_index(kind, k)
                per = STREAM[TILE_OF[kind]][1]
                slot = tile_here(TILE_OF[kind] + k // per)
                w = ring[:, slot, :].rearrange("p (k c) -> p k c", k=kbs)
                bank_free(n)
                for kb in range(kbs):
                    last = mm(S[n % 4][:, 0:SEQ], w[:, kb, (k % per) * P:(k % per + 1) * P], act_T[:, kb, :],
                              start=(kb == 0), stop=(kb == kbs - 1))
                last.then_inc(proj_ready, 1)

            def token_major(kind, k, act_T):
                n = out_index(kind, k)
                slot = tile_here(TILE_OF[kind] + k // TB)
                t = k % TB
                bank_free(n)
                for kb in range(KB):
                    last = mm(S[n % 4][:], act_T[:, kb, t * P:(t + 1) * P], ring[:, slot, kb * 512:(kb + 1) * 512],
                              start=(kb == 0), stop=(kb == KB - 1))
                last.then_inc(proj_ready, 1)

            pe.wait_ge(small_in, 32)
            mm(W[0][0:DIFF_HEADS, 0:384], cs[0:BUCKETS + 1, C_RB:C_RB + 8], cs[0:BUCKETS + 1, C_HOT:C_HOT + 384],
               start=True, stop=True).then_inc(rel_mm, 1)
            pe.wait_ge(xT_ld, 16)
            for b in range(NXB):
                feature_major("xbc", b, xT)
            for t in range(TB):
                for kb in range(KB):
                    last = mm(W[1][:, t * SSD_HEADS:(t + 1) * SSD_HEADS], xT[:, kb, t * P:(t + 1) * P], w_dt[:, kb, :],
                              start=(kb == 0), stop=(kb == KB - 1))
            last.then_inc(dt_mm, 1)
            for h in range(DIFF_HEADS):
                feature_major("q", h, xT)
            for h in range(DIFF_HEADS):
                feature_major("k", h, xT)
            pe.wait_ge(rel_ld, 16)
            pe.wait_ge(rel_cp, 1)
            pe.wait_ge(a_done, 1)
            for k in range(4):
                mm(W[k][:], flip, rel_flipped[:, 2 * k:2 * k + 2, :], start=True, stop=True).then_inc(flip_mm, 1)
            pe.wait_ge(flip_cp, 4)
            mm(W[0][:, 0:SSD_HEADS], strict, a_v[:, 0, :], start=True, stop=True).then_inc(end_mm, 1)
            pe.wait_ge(conv_silu, NXB)
            for g in range(GROUPS):
                if g == 3:
                    pe.wait_ge(small_exp, 4)
                bank = W[(1 + g) % 4]
                bT, cT = xc[:, XS_BLOCKS + g, :], xc[:, XS_BLOCKS + GROUPS + g, :]
                mm(bank[:, 0:SEQ], bT[:, 0:P], cT, start=True, stop=True)
                mm(bank[:, SEQ:384], bT[:, P:SEQ], cT[:, P:SEQ], start=True, stop=True).then_inc(cb_mm, 1)
            for k in range(8):
                t, quad = k // 4, k % 4
                if k < 4:
                    pe.wait_ge(cb_cp, 2 * k + 2)
                else:
                    pe.wait_ge(xs_cp, k - 3)
                for j in range(4):
                    last = nc.tensor.transpose(W[(1 + k) % 4][:, j * P:(j + 1) * P],
                                               xc[:, 4 * quad + j, t * P:(t + 1) * P], ident)
                last.then_inc(xs_mm, 1)
            for k in range(4):
                token_major("v", k, xT)

            for i in range(8):
                for t in range(TB):
                    pe.wait_ge(gdec_done, 2 * i + t + 1)
                    if i == 0:
                        pe.wait_ge(xs_cp, 8)
                    else:
                        pe.wait_ge(y_done, i)
                    for h in range(4):
                        last = mm(W[2 + t][:, h * P:(h + 1) * P], gdec[:, t, h, :], tri, start=True, stop=True)
                    last.then_inc(seg_mm, 1)
                if i >= 1:
                    pe.wait_ge(attnT_cp, i)
                    pe.wait_ge(av_cp, i)
                if i == 0:
                    pe.wait_ge(act_took, taken_count(out_index("k", 7)))
                for m in range(2):
                    r = slice(HEAD * m, HEAD * m + HEAD)
                    mm(W[m][:, 0:P], qT[r, i, 0:P], kT[r, i, 0:P], start=True, stop=True)
                    last = mm(W[m][:, P:384], qT[r, i, P:SEQ], kT[r, i, :], start=True, stop=True)
                last.then_inc(logit_mm, 1)
                kind = "z" if i < 4 else "gate"
                k0 = 4 * (i % 4)
                feature_major(kind, k0, xT)
                feature_major(kind, k0 + 1, xT)
                pe.wait_ge(masked_dec, 2 * i + 2)
                for j in range(2):
                    for t in range(TB):
                        for h in range(2):
                            c = 256 * i + P * j + HEAD * h
                            last = mm(W[2][HEAD * h:HEAD * h + HEAD, j * SEQ + t * P:j * SEQ + (t + 1) * P],
                                      xsdt[:, t, c:c + HEAD], dec[:, t, 2 * j + h, :], start=True, stop=True)
                last.then_inc(y_mm, 1)
                pe.wait_ge(xend_done, i + 1)
                for j in range(2):
                    mm(W[3][:, j * P:(j + 1) * P], xend[:, 2 * j:2 * j + 2, :].rearrange("p h e -> p (h e)"),
                       cbm[:, i // 2, P:2 * P], start=True, stop=True)
                for j in range(2):
                    for h in range(2):
                        a_h = a_v[:, 1, 4 * i + 2 * j + h:4 * i + 2 * j + h + 1].to_broadcast([P, HEAD])
                        last = mm(W[3][HEAD * h:HEAD * h + HEAD, SEQ + j * P:SEQ + (j + 1) * P], a_h, tri,
                                  start=True, stop=True)
                last.then_inc(off_mm, 1)
                pe.wait_ge(attn_done, i + 1)
                for j in range(3):
                    last = nc.tensor.transpose(W[0][:, j * P:(j + 1) * P], attn[:, j * P:(j + 1) * P], ident)
                last.then_inc(attnT_mm, 1)
                feature_major(kind, k0 + 2, xT)
                feature_major(kind, k0 + 3, xT)
                if i == 0:
                    pe.wait_ge(act_took, taken_count(out_index("v", 3)))
                pe.wait_ge(attnT_cp, i + 1)
                mm(W[1][:, 0:SEQ], v[:, 0, i * P:(i + 1) * P], attnT[:, 0:SEQ], start=True, stop=False,
                   skip_group_check=True)
                mm(W[1][:, P:SEQ], v[:, 1, i * P:(i + 1) * P], attnT[:, SEQ:384], start=False, stop=True,
                   skip_group_check=True).then_inc(av_mm, 1)

            pe.wait_ge(memT_ld, 16)

            def sums_of_squares(k):
                pe.wait_ge(squared, k + 1)
                if k < GROUPS:
                    if k == 0:
                        pe.wait_ge(attnT_cp, 8)
                        pe.wait_ge(av_cp, 8)
                        pe.wait_ge(y_done, 8)
                    for j in range(4):
                        last = mm(W[k][:, 0:SEQ], ones, z[:, 4 * k + j, :], start=(j == 0), stop=(j == 3))
                else:
                    pe.wait_ge(rms_rcp, k - GROUPS + 1)
                    last = mm(W[k - GROUPS][:], ones, sqd[:, 2 * (k - GROUPS):2 * (k - GROUPS) + 2, :],
                              start=True, stop=True)
                last.then_inc(ssq_mm, 1)

            for k in range(4):
                feature_major("ck", k, memT)
            sums_of_squares(0)
            sums_of_squares(1)
            for k in range(4, 8):
                feature_major("ck", k, memT)
            sums_of_squares(2)
            sums_of_squares(3)
            token_major("cv", 0, memT)
            token_major("cv", 1, memT)
            for k in range(4):
                sums_of_squares(GROUPS + k)
            token_major("cv", 2, memT)
            token_major("cv", 3, memT)
            pe.wait_ge(yT_done, XS_BLOCKS)
            for k in range(KB):
                feature_major("ssd", k, xc, kbs=XS_BLOCKS)
            pe.wait_ge(oT_done, DIFF_HEADS)
            for k in range(KB):
                feature_major("diff", k, oT)
            pe.wait_ge(mix_done, KB)
            for k in range(4):
                token_major("mix", k, mixT)

            def turn(which):
                for t in range(TB):
                    pe.wait_ge(ln_done, TB * which + t + 1)
                    for c in range(2):
                        for j in range(4):
                            last = nc.tensor.transpose(W[2 * t + c][:, j * P:(j + 1) * P],
                                                       xres[:, t, (4 * c + j) * P:(4 * c + j + 1) * P], ident)
                        last.then_inc(xt_mm, 1)

            pe.wait_ge(rms_rcp, 2 * GROUPS)
            turn(0)
            pe.wait_ge(xt_cp, 4)
            for k in range(KB):
                feature_major("cq", k, x1T)
            for h in range(MEM_HEADS):
                pe.wait_ge(act_took, taken_count(out_index("cq", 2 * h + 1)))
                for t in range(TB):
                    for c in range(2):
                        last = mm(W[h][:, t * SEQ:(t + 1) * SEQ], qcT[:, 2 * h + c, t * P:(t + 1) * P],
                                  kcT[:, 2 * h + c, :], start=(c == 0), stop=(c == 1))
                last.then_inc(clog_mm, 1)
            for h in range(MEM_HEADS):
                pe.wait_ge(cprob_done, TB * (h + 1))
                for kb in range(2):
                    for t in range(TB):
                        last = nc.tensor.transpose(W[h][:, kb * SEQ + t * P:kb * SEQ + (t + 1) * P],
                                                   pc[:, h, t, kb * P:(kb + 1) * P], ident)
                last.then_inc(cpT_mm, 1)
            for h in range(MEM_HEADS):
                pe.wait_ge(cpT_cp, h + 1)
                for c in range(2):
                    for kb in range(2):
                        last = mm(W[h][:, c * SEQ:(c + 1) * SEQ], vc[:, kb, (2 * h + c) * P:(2 * h + c + 1) * P],
                                  pcT[:, h, kb, :], start=(kb == 0), stop=(kb == 1))
                last.then_inc(cav_mm, 1)
            pe.wait_ge(cav_cp, MEM_HEADS)
            for k in range(4):
                token_major("co", k, ocT)
            turn(1)
            pe.wait_ge(xt_cp, 8)
            for t in range(TB):
                for kb in range(KB):
                    last = mm(W[0][:, t * EXPERTS:(t + 1) * EXPERTS], x2T[:, kb, t * P:(t + 1) * P], w_router[:, kb, :],
                              start=(kb == 0), stop=(kb == KB - 1))
            last.then_inc(score_mm, 1)
            for t in range(TB):
                token_major("sh", t, x2T)
            pe.wait_ge(sel_done, 1)
            mm(W[2][:, 0:EXPERTS], tri, sel[:, 0, :], start=True, stop=True)
            mm(W[2][:, EXPERTS:2 * EXPERTS], ones, sel[:, 0, :], start=True, stop=False)
            mm(W[2][:, EXPERTS:2 * EXPERTS], tri, sel[:, 1, :], start=False, stop=True)
            mm(W[2][:, 2 * EXPERTS:3 * EXPERTS], ones, sel[:, 0, :], start=True, stop=False)
            mm(W[2][:, 2 * EXPERTS:3 * EXPERTS], ones, sel[:, 1, :], start=False, stop=True).then_inc(rank_mm, 1)
            for t in range(TB):
                pe.wait_ge(sh_done, t + 1)
                for c in range(2):
                    last = nc.tensor.transpose(W[1][:, t * SEQ + c * P:t * SEQ + (c + 1) * P],
                                               hh[:, c * P:(c + 1) * P], ident)
                last.then_inc(hsT_mm, 1)

            def gather(block, bank, buf, done):
                parts = [(x, t) for t in range(TB) for x in (x2h, x2l)]
                for k, (x, t) in enumerate(parts):
                    last = mm(bank[:], x[:, t, block * P:(block + 1) * P],
                              onehot[:, buf, t].rearrange("p e s -> p (e s)"),
                              start=(k == 0), stop=(k == len(parts) - 1))
                last.then_inc(done, 1)

            pe.wait_ge(onehot_done, 2)
            pe.wait_ge(split_l, 2)
            pe.wait_ge(sh_done, 2)
            for k in range(KB):
                if k >= 2:
                    pe.wait_ge((gath_act, gath_dve)[k % 2], k // 2)
                gather(k, S[k % 2], 0, gath_mm)
            pe.wait_ge(hsT_cp, TB + 1)
            pe.wait_ge(wsd_ld, 16)
            pe.wait_ge(place_done, 2)

            def shared_down(kb, last_one):
                for t in range(TB):
                    for c in range(2):
                        last = mm(W[2 * t + c][:], hsT[:, kb, t * P:(t + 1) * P], wsd[:, kb, c * 512:(c + 1) * 512],
                                  start=not last_one, stop=last_one, skip_group_check=True)
                return last

            shared_down(0, False)

            def scatter(done=None):
                for t in range(TB):
                    for c in range(2):
                        for y in (yh, yl):
                            last = mm(W[2 * t + c][:], scatT[:, t * P:(t + 1) * P], y[:, c * 512:(c + 1) * 512],
                                      start=False, stop=False, skip_group_check=True)
                if done is not None:
                    last.then_inc(done, 1)

            def gate_up(x, col, slots, done):
                for kb in range(KB):
                    for e in range(2):
                        last = mm(S[2][e * SLOTS:(e + 1) * SLOTS, :], x[:, kb, col + e * SLOTS:col + (e + 1) * SLOTS],
                                  ring[:, slots[e], kb * 512:(kb + 1) * 512], start=(kb == 0), stop=(kb == KB - 1))
                last.then_inc(done, 1)

            def turn_onehot(buf, col, gates, done):
                for t in range(TB):
                    mm(S[0][:, t * P:(t + 1) * P], onehot[:, buf, t].rearrange("p e s -> p (e s)")[:, col:col + P],
                       ident_r[:], start=True, stop=True)
                for t in range(TB):
                    last = mm(S[0][:, SEQ:SEQ + 2],
                              onehot[:, buf, t].rearrange("p e s -> p (e s)")[:, col:col + P].bitcast(F32),
                              gates(t), start=(t == 0), stop=(t == TB - 1))
                last.then_inc(done, 1)

            def turn_h(done):
                for c in range(2):
                    last = nc.tensor.transpose(S[2][:, c * P:(c + 1) * P], hh[:, c * P:(c + 1) * P], ident)
                last.then_inc(done, 1)

            def down(c, slot, done):
                for kb in range(2):
                    for e in range(2):
                        o = (e * 2 + kb) * D + c * 512
                        last = mm((S[3], S[1])[c][e * SLOTS:(e + 1) * SLOTS, :], hT[:, kb, e * SLOTS:(e + 1) * SLOTS],
                                  ring[:, slot, o:o + 512], start=(kb == 0), stop=(kb == 1))
                if done is not None:
                    last.then_inc(done, 1)

            pe.wait_ge(gath_act, KB // 2)
            pe.wait_ge(gath_dve, KB // 2)
            with pe.Fori(0, PAIRS // 8) as i:
                for jj in range(8):
                    buf, col = jj // 4, (jj % 4) * P
                    if jj % 4 == 0:
                        pe.wait_ge(gath_act, i * 8 + (KB // 2 + jj))
                        pe.wait_ge(gath_dve, i * 8 + (KB // 2 + jj))
                    for kind in range(2):
                        pe.wait_ge(expert_ld[expert_tile(jj, kind)], expert_count(i, jj, kind))
                    gate_up(xg[buf], col, (expert_tile(jj, 0), expert_tile(jj, 1)), gu_mm)
                    if jj >= 1:
                        pe.wait_ge(yl_done, i * 16 + 2 * jj)
                        scatter()
                    pe.wait_ge(gath_dve, i * 8 + (KB // 2 + jj))
                    turn_onehot(buf, col, lambda t: gates_e[:, t, bass.ds(i * 16 + 2 * jj, 2)], scatT_mm)
                    pe.wait_ge(onehot_done, i * 4 + (2 * (jj // 4) + 4))
                    pe.wait_ge(scatT_cp, i * 8 + (jj + 1))
                    gather(2 * (jj % 4), S[0], (buf + 1) % 2, gath_mm)
                    pe.wait_ge(h_done, i * 8 + (jj + 1))
                    turn_h(hT_mm)
                    pe.wait_ge(gath_act, i * 8 + (KB // 2 + jj + 1))
                    gather(2 * (jj % 4) + 1, S[0], (buf + 1) % 2, gath_mm)
                    pe.wait_ge(hT_cp, i * 8 + (jj + 1))
                    pe.wait_ge(expert_ld[expert_tile(jj, 2)], expert_count(i, jj, 2))
                    down(0, expert_tile(jj, 2), down_mm)
                    down(1, expert_tile(jj, 2), down_mm)
                pe.wait_ge(yl_done, i * 16 + 16)
                scatter()
            pe.wait_ge(gath_dve, KB // 2 + PAIRS)
            pe.wait_ge(items_ld, 32)
            n_items = pe.value_load(items[0:1, P:P + 1], min_val=0, max_val=EXTRA)
            with pe.If(n_items > 0):
                with pe.Fori(0, n_items) as i:
                    item = pe.value_load(items[0:1, bass.ds(i, 1)], min_val=0, max_val=EXTRA - 1)
                    pe.wait_ge(o_hot, i * 4 + 4)
                    for k in range(KB):
                        parts = [(x, t) for t in range(TB) for x in (x2h, x2l)]
                        for n, (x, t) in enumerate(parts):
                            last = mm(S[k // 4][:, (k % 4) * P:(k % 4 + 1) * P], x[:, t, k * P:(k + 1) * P],
                                      onehot[:, 0, t, 0:2, :].rearrange("p e s -> p (e s)"),
                                      start=(n == 0), stop=(n == 3))
                    last.then_inc(o_gath, 1)
                    pe.wait_ge(o_xg, i * 2 + 2)
                    pe.wait_ge(extra_ld, i * 48 + 48)
                    gate_up(xg[0], 0, (0, 1), o_gu)
                    pe.wait_ge(o_h, i + 1)
                    for t in range(TB):
                        mm(S[0][:, t * P:(t + 1) * P], onehot[:, 0, t, 0:2, :].rearrange("p e s -> p (e s)"),
                           ident_r[:], start=True, stop=True)
                    for t in range(TB):
                        mm(S[0][:, SEQ:SEQ + 2], onehot[:, 0, t, 0:2, :].rearrange("p e s -> p (e s)").bitcast(F32),
                           gates_e[:, t, bass.ds((item % PAIRS) * 2, 2)], start=(t == 0), stop=(t == TB - 1))
                    turn_h(o_T)
                    pe.wait_ge(o_Tcp, i * 4 + 4)
                    down(0, 2, None)
                    down(1, 2, o_down)
                    pe.wait_ge(o_y, i * 4 + 4)
                    scatter(o_scat)
            shared_down(1, True).then_inc(moe_mm, 1)


def constants():
    c = np.zeros((P, C_CONVW), np.float32)
    p, f = np.arange(P)[:, None], np.arange(P)[None, :]
    c[:, C_ID:C_ID + P] = p == f
    c[:, C_TRI:C_TRI + P] = p <= f
    c[:, C_STRICT:C_STRICT + P] = p > f
    c[:, C_ONES:C_ONES + P] = 1.0
    c[:, C_FLIP:C_FLIP + P] = p + f == P - 1
    c[:, C_IOTA:C_IOTA + P] = f + 1
    c[:, C_LOW:C_LOW + 64] = (np.arange(8)[None, :] < np.arange(8)[:, None]).reshape(-1)
    item = np.arange(EXTRA)
    c[:, C_ROFF:C_ROFF + EXTRA] = SLOTS * (item // PAIRS + 1)
    c[:, C_ITEMS:C_ITEMS + EXTRA] = item
    c[:, C_ITEM + 1] = np.arange(P) + 1
    dist = SEQ - 1 - np.arange(384)
    exact = BUCKETS // 2
    d = np.maximum(dist, 1).astype(np.float32)
    large = exact + (np.log(d / exact) / math.log(MAX_DIST / exact) * (BUCKETS - exact)).astype(np.int32)
    bucket = np.where(dist < exact, dist, np.minimum(large, BUCKETS - 1))
    for j in range(384):
        if dist[j] >= 0:
            c[bucket[j], C_HOT + j] = 1.0
        else:
            c[BUCKETS, C_HOT + j] = MASKED
    return c


def lay_out(inp):
    f = {k: np.asarray(a, dtype=np.float32) for k, a in inp.items()}

    def tiles(w, cols, kbs=KB):
        n = w.shape[1] // cols
        return w.reshape(kbs, P, n, cols).transpose(2, 1, 0, 3).reshape(n, P, kbs * cols)

    w_in = f["w_in"][0]
    dense = [
        tiles(w_in[:, O_XBC:O_DT], 512), tiles(w_in[:, O_Q:O_K], 512), tiles(w_in[:, O_K:O_V], 512),
        tiles(w_in[:, O_V:O_G], 512), tiles(w_in[:, 0:INNER], 512), tiles(w_in[:, O_G:], 512),
        tiles(f["w_ckv"][0], 512), tiles(f["w_ssd_br"][0], 256, XS_BLOCKS), tiles(f["w_diff_br"][0], 512),
        tiles(f["w_mix_out"][0], 512), tiles(f["w_cq"][0], 512), tiles(f["w_co"][0], 512), tiles(f["w_sh_gu"][0], 512),
    ]
    gu = f["w_exp_gu"][0].reshape(PAIRS, 2, KB, P, 2 * FF).transpose(0, 1, 3, 2, 4).reshape(PAIRS, 2, P, TILE)
    dn = f["w_exp_down"][0].reshape(PAIRS, 2, 2, P, D).transpose(0, 3, 1, 2, 4).reshape(PAIRS, 1, P, TILE)
    experts = np.concatenate([gu, dn], axis=1).reshape(3 * PAIRS, P, TILE)
    wstream = np.concatenate(dense + [experts], axis=0)
    small = np.concatenate([
        constants(),
        f["conv_w"][0].reshape(CONV, NXB, P).transpose(2, 1, 0).reshape(P, NXB * CONV),
        f["conv_b"][0].reshape(NXB, P).T,
        f["ssd_norm_g"][0].reshape(XS_BLOCKS, P).T,
        np.repeat(f["d_skip"][0], HEAD).reshape(XS_BLOCKS, P).T,
        np.repeat(f["subln_g"][0].reshape(P, 1), 8, axis=1),
        np.concatenate([f["rel_bias"], np.ones((1, 8), np.float32), np.zeros((P - BUCKETS - 1, 8), np.float32)]),
        w_in[:, O_DT:O_Q].reshape(KB, P, SSD_HEADS).transpose(1, 0, 2).reshape(P, -1),
        f["w_router"][0].reshape(KB, P, EXPERTS).transpose(1, 0, 2).reshape(P, -1),
    ], axis=1)
    rows = np.concatenate([f["dt_bias"][0], f["a_log"][0], f["lambda_q1"][0], f["lambda_k1"][0], f["lambda_q2"][0],
                           f["lambda_k2"][0], f["router_bias"][0]])
    lnp = np.stack([np.stack([f[f"ln{i}_g"][0], f[f"ln{i}_b"][0]]) for i in (1, 2, 3)])

    def turned(x):
        return x[0].T.reshape(KB, P, -1).transpose(1, 0, 2)

    return {
        "small": small, "rows": rows, "lnp": lnp, "xT": turned(f["x"]), "memT": turned(f["mem"]),
        "x_tok": f["x"][0].reshape(TB, P, D).transpose(1, 0, 2), "wstream": wstream,
        "wshd": f["w_sh_down"][0].reshape(2, P, D).transpose(1, 0, 2),
    }


def kernel(**inputs):
    import concourse.bacc as bacc
    from concourse.bass_utils import run_bass_kernel_spmd

    nc = bacc.Bacc("TRN2", target_bir_lowering=False, num_devices=1)
    arrays = {f"in_{k}": np.ascontiguousarray(a) for k, a in lay_out(inputs).items()}
    args = [nc.dram_tensor(k, a.shape, mybir.dt.from_np(a.dtype), kind="ExternalInput").ap() for k, a in arrays.items()]
    out = nc.dram_tensor("out_dram", (1, SEQ, D), F32, kind="ExternalOutput").ap()
    layer_kernel(nc, *args, out)
    r = run_bass_kernel_spmd(nc, [arrays], core_ids=[0])
    return r.results[0]["out_dram"]
```

```python
import math
from contextlib import ExitStack

import numpy as np

import concourse.bass as bass
from concourse import mybir

F32 = mybir.dt.float32
F32R = mybir.dt.float32r
I32 = mybir.dt.int32
ALU = mybir.AluOpType
ACT = mybir.ActivationFunctionType
AX = mybir.AxisListType

P = 128
SEQ = 256
TB = SEQ // P
D = 1024
KB = D // P
INNER = 2048
SSD_HEADS = 32
HEAD = 64
GROUPS = 4
STATE = 128
CONV = 4
XBC = INNER + 2 * GROUPS * STATE
NXB = XBC // P
XS_BLOCKS = INNER // P
DIFF_HEADS = 8
MEM_HEADS = 4
BUCKETS = 32
MAX_DIST = 128
EXPERTS = 64
PAIRS = EXPERTS // 2
EGROUPS = 8
TOP_GROUPS = 4
FF = 256
SLOTS = 64
CHUNKS = SEQ // SLOTS
EXTRA = (CHUNKS - 1) * PAIRS
PER_GROUP = 8
ROUTED_SCALE = 2.5
ALPHA = 2.0 ** 0.25
EPS = 1e-5
LAM_INIT = 0.8 - 0.6 * math.exp(0.0)
SUBLN_SCALE = 1.0 - LAM_INIT
MASKED = -1.0e30
TILE = 4096

O_XBC = INNER
O_DT = O_XBC + XBC
O_Q = O_DT + SSD_HEADS
O_K = O_Q + D
O_V = O_K + D
O_G = O_V + D

STREAM = [("xbc", NXB, 1), ("q", 8, 1), ("k", 8, 1), ("v", 8, 1), ("z", 16, 1), ("gate", 16, 1), ("ck", 8, 1),
          ("cv", 4, 1), ("diff", 8, 1), ("ssd", 8, 2), ("mix", 8, 1), ("cvb", 4, 1), ("cq", 8, 1), ("co", 8, 1),
          ("sh", 4, 1)]
TOKEN_MAJOR = {"v", "cv", "cvb", "mix", "co", "sh"}
BY_DVE = {"ssd", "diff", "mix", "co", "sh"}
OUT_KIND = [k for k, m, _ in STREAM for _ in range(m)]
OUT0, CHUNK0, DONE = {}, {}, []
for _k, _m, _c in STREAM:
    OUT0[_k], CHUNK0[_k] = sum(m for k, m, _ in STREAM[:len(OUT0)]), len(DONE)
    for _q in range(_m * _c):
        DONE.append(OUT0[_k] + (2 * (_q // 2) + 2 if _k in TOKEN_MAJOR else _q // _c + 1))
N_CHUNKS = len(DONE)
N_SPLIT = CHUNK0["sh"]
CHUNK = KB * P
RAW_TILES = 3
ROUNDED = 4
RING = 6

C_ID, C_TRI, C_STRICT, C_ONES, C_IOTA = 0, 128, 256, 384, 512
C_LOW, C_ROFF, C_ITEM, C_ITEMS, C_FLIP, C_HOT = 640, 704, 800, 808, 904, 1032
C_CONVW = C_HOT + 384
C_CONVB = C_CONVW + NXB * CONV
C_SSDG = C_CONVB + NXB
C_DSKIP = C_SSDG + XS_BLOCKS
C_SUBLN = C_DSKIP + XS_BLOCKS
C_RB = C_SUBLN + 8
C_WDT = C_RB + 8
C_WR = C_WDT + KB * SSD_HEADS
N_SMALL = C_WR + KB * EXPERTS
R_DTB, R_ALOG, R_LAM, R_RB = 0, 32, 64, 320
N_ROW = 384


def out_index(kind, k=0):
    return OUT0[kind] + k


def rest_by_dve(q):
    return q == 0 or q % 4 == 3


def rest_count(q):
    return sum(rest_by_dve(c) == rest_by_dve(q) for c in range(q + 1))


def taken_count(n):
    by = OUT_KIND[n] in BY_DVE
    return sum((k in BY_DVE) == by for k in OUT_KIND[:n + 1])


def layer_kernel(nc, small, rows, lnp, xT_in, memT_in, x_in, wdense, wstream, wshd, out):
    ctx = ExitStack()
    with ctx:
        def sb(name, shape, offset, dt=F32):
            return nc.alloc_sbuf_tensor_at(name, shape, dt, offset=offset)

        def sem(name):
            return ctx.enter_context(nc.semaphore(name))

        KIB = 1024
        at = 16512
        cs = sb("cs", [P, N_SMALL], at)
        at += N_SMALL * 4
        row = sb("row", [P, N_ROW], at)
        at += N_ROW * 4

        def tiny(name, shape, dt=F32):
            nonlocal at
            t = sb(name, shape, at, dt)
            at += (int(np.prod(shape[1:])) * 4 + 31) // 32 * 32
            return t

        dt_v = tiny("dt_v", [P, TB, SSD_HEADS])
        a_v = tiny("a_v", [P, TB, SSD_HEADS])
        dt_t = [tiny(f"dt_t{i}", [P, TB, SSD_HEADS]) for i in range(4)]
        exp_alog = tiny("exp_alog", [P, SSD_HEADS])
        decay_end = tiny("decay_end", [P, SSD_HEADS])
        lam_d = tiny("lam_d", [P, 2])
        lam_e = tiny("lam_e", [P, 2])
        neg_lam = tiny("neg_lam", [P, 1])
        lam_tmp = tiny("lam_tmp", [P, 64])
        a_max = tiny("a_max", [P, 4])
        a_neg = tiny("a_neg", [P, 4])
        a_sum = tiny("a_sum", [P, 4])
        a_rcp = tiny("a_rcp", [P, 4])
        c_neg = tiny("c_neg", [P, MEM_HEADS, TB])
        c_sum = tiny("c_sum", [P, MEM_HEADS, TB])
        c_rcp = tiny("c_rcp", [P, MEM_HEADS, TB])
        bn = tiny("bn", [P, TB, 2, 6])
        mv = tiny("mv", [P, TB, 2])
        rvar = tiny("rvar", [P, TB])
        rstd = tiny("rstd", [P, TB])
        max8 = tiny("max8", [P, TB, EGROUPS, 8])
        gsc = tiny("gsc", [P, TB, EGROUPS])
        gcmp = tiny("gcmp", [P, TB, EGROUPS, EGROUPS])
        geq = tiny("geq", [P, TB, EGROUPS, EGROUPS])
        gmask = tiny("gmask", [P, TB, EGROUPS])
        goff = tiny("goff", [P, TB, EGROUPS])
        top8 = tiny("top8", [P, TB, 8])
        w_sum = tiny("w_sum", [P, TB])
        w_rcp = tiny("w_rcp", [P, TB])
        slot_gate = tiny("slot_gate", [P, 1])
        place_off = tiny("place_off", [P, TB, 2])
        pair_n = tiny("pair_n", [P, PAIRS])
        item_col = tiny("item_col", [P, 2], I32)
        item_f = tiny("item_f", [P, 2])
        items = tiny("items", [P, P + 1], I32)
        place_e = tiny("place_e", [P, TB, EXPERTS + PER_GROUP])
        gates_e = tiny("gates_e", [P, TB, EXPERTS])
        RING0 = 131040
        W0 = RING0 - 6176 - 88 * KIB
        assert at <= W0, (at, W0)
        A = W0
        G = A + 8 * KIB
        FR = G + 8 * KIB
        E = FR + 8 * KIB
        C = E + 16 * KIB
        Z = C + 16 * KIB
        H = Z + 16 * KIB
        L = H + 16 * KIB
        SL3 = RING0 + 3 * 16 * KIB
        SL4 = SL3 + 16 * KIB
        ring = sb("ring", [P, RING, TILE], RING0)
        raw = sb("raw", [P, RAW_TILES * 2, CHUNK], RING0)
        w_lo = sb("w_lo", [P, RAW_TILES * 2, CHUNK], RING0, F32R)
        w_hi = sb("w_hi", [P, ROUNDED, CHUNK], RING0 + 24 * KIB, F32R)
        MEM = RING0 + 40 * KIB
        XH = SL4 + 24 * KIB
        xT = sb("xT", [P, KB, SEQ], A)
        xT_r = (sb("xT_hi", [P, KB, SEQ], XH, F32R), sb("xT_lo", [P, KB, SEQ], A, F32R))
        wdt_r = (sb("wdt_hi", [P, KB, SSD_HEADS], L, F32R), sb("wdt_lo", [P, KB, SSD_HEADS], L + KIB, F32R))
        dtT = sb("dtT", [P, SEQ], L + 2 * KIB)
        mixT = sb("mixT", [P, KB, SEQ], A)
        mixT_r = (sb("mixT_hi", [P, KB, SEQ], H, F32R), sb("mixT_lo", [P, KB, SEQ], A, F32R))
        rel = sb("rel", [P, DIFF_HEADS, SEQ], G)
        rel_flipped = sb("rel_flipped", [P, DIFF_HEADS, SEQ], H)
        ln1 = sb("ln1", [P, 2, D], Z + 8 * KIB)
        ln2 = sb("ln2", [P, 2, D], G)
        v = sb("v", [P, TB, D], FR)
        qT = sb("qT", [P, DIFF_HEADS, SEQ], E)
        kT = sb("kT", [P, DIFF_HEADS, SEQ], E + 8 * KIB)
        oT = qT
        oT_r = (sb("oT_hi", [P, DIFF_HEADS, SEQ], C, F32R), sb("oT_lo", [P, DIFF_HEADS, SEQ], E, F32R))
        xsdt = sb("xsdt", [P, TB, INNER], C)
        sqd = sb("sqd", [P, DIFF_HEADS, SEQ], C)
        xres = sb("xres", [P, TB, D], C + 8 * KIB)
        z = sb("z", [P, XS_BLOCKS, SEQ], Z)
        gt = sb("gt", [P, 2 * KB, SEQ], H)
        xc = sb("xc", [P, NXB, SEQ], SL4)
        yT_r = (sb("yT_hi", [P, XS_BLOCKS, SEQ], Z, F32R), sb("yT_lo", [P, XS_BLOCKS, SEQ], SL4, F32R))
        cbm = sb("cbm", [P, GROUPS, 3 * P], SL4 + XS_BLOCKS * KIB)
        memT = sb("memT", [P, KB, SEQ], MEM)
        memT_r = (sb("memT_hi", [P, KB, SEQ], G, F32R), sb("memT_lo", [P, KB, SEQ], MEM, F32R))
        lg = sb("lg", [P, 768], L)
        attn = sb("attn", [P, 384], L + 3072)
        attnT = sb("attnT", [P, 384], L + 4608)
        dec = sb("dec", [P, TB, 4, P], SL3)
        gdec = sb("gdec", [P, TB, 4, P], SL3 + 4 * KIB)
        bds = sb("bds", [P, 384], SL3)
        PADDED = SEQ + CONV - 1
        xpad = sb("xpad", [P, 4, PADDED], SL3 + 8 * KIB)
        acc = sb("acc", [P, 2, SEQ], SL3 + 8 * KIB + 4160)
        fac = sb("fac", [P, 2, P], SL3 + 8 * KIB)
        yo = sb("yo", [P, 2, P], SL3 + 9 * KIB)
        xend = sb("xend", [P, 4, HEAD], SL3 + 10 * KIB)
        dtmp = sb("dtmp", [P, 512], SL3 + 11 * KIB)
        rms = sb("rms", [P, 8, 512], SL3)
        kcT = sb("kcT", [P, KB, SEQ], E + 8 * KIB)
        vc = sb("vc", [P, TB, D], FR)
        x1T_r = (sb("x1T_hi", [P, KB, SEQ], A, F32R), sb("x1T_lo", [P, KB, SEQ], Z, F32R))
        qcT = sb("qcT", [P, KB, SEQ], Z + 8 * KIB)
        pc = sb("pc", [P, MEM_HEADS, TB, SEQ], H)
        pcT = sb("pcT", [P, MEM_HEADS, TB, SEQ], H + 8 * KIB)
        ocT_r = (sb("ocT_hi", [P, KB, SEQ], A, F32R), sb("ocT_lo", [P, KB, SEQ], Z, F32R))
        x2T = sb("x2T", [P, KB, SEQ], FR)
        scores = sb("scores", [P, TB, EXPERTS], Z)
        choice = sb("choice", [P, TB, EXPERTS], Z + 512)
        masked = sb("masked", [P, TB, EXPERTS], Z + 1024)
        sel = sb("sel", [P, TB, EXPERTS], Z + 1536)
        flags = sb("flags", [P, 2, EXTRA], Z + 2048)
        item_eq = sb("item_eq", [P, EXTRA], Z + 2048 + 1024)
        wsd = sb("wsd", [P, 2, D], G)
        x2h = sb("x2h", [P, TB, D], E, F32R)
        x2l = sb("x2l", [P, TB, D], E + 8 * KIB, F32R)
        onehot = sb("onehot", [P, 2, TB, PER_GROUP, SLOTS], A, F32R)
        yh = sb("yh", [P, D], C, F32R)
        yl = sb("yl", [P, D], C + 4 * KIB, F32R)
        xg = [sb("xg0", [P, KB, PER_GROUP * SLOTS], H), sb("xg1", [P, KB, PER_GROUP * SLOTS], Z)]
        ln3 = sb("ln3", [P, 2, D], Z)
        scatT = sb("scatT", [P, SEQ], FR, F32R)
        ident_r = sb("ident_r", [P, P], FR + 1 * KIB, F32R)
        hT = sb("hT", [P, 2, P], FR + 2 * KIB)
        hsT = sb("hsT", [P, 2, SEQ], L)
        h1 = sb("h1", [P, FF], L + 2 * KIB)
        hh = sb("hh", [P, FF], L + 3 * KIB)

        S = [ctx.enter_context(nc.psum_tensor(f"stream{i}", [P, 512], F32)) for i in range(4)]
        W = [ctx.enter_context(nc.psum_tensor(f"work{i}", [P, 512], F32)) for i in range(4)]

        ident = cs[:, C_ID:C_ID + P]
        tri = cs[:, C_TRI:C_TRI + P]
        strict = cs[:, C_STRICT:C_STRICT + P]
        flip = cs[:, C_FLIP:C_FLIP + P]
        ones = cs[:, C_ONES:C_ONES + P]
        slot_no = cs[:, C_IOTA:C_IOTA + SLOTS]
        part_no = cs[:, C_ITEM + 1:C_ITEM + 2]
        lower8 = cs[:, C_LOW:C_LOW + 64].rearrange("p (i j) -> p i j", i=8)
        conv_w = cs[:, C_CONVW:C_CONVW + NXB * CONV].rearrange("p (b j) -> p b j", j=CONV)
        conv_b = cs[:, C_CONVB:C_CONVB + NXB]
        ssd_g = cs[:, C_SSDG:C_SSDG + XS_BLOCKS]
        d_skip = cs[:, C_DSKIP:C_DSKIP + XS_BLOCKS]
        subln = cs[:, C_SUBLN:C_SUBLN + 1]
        w_dt = cs[:, C_WDT:C_WDT + KB * SSD_HEADS].rearrange("p (k h) -> p k h", k=KB)
        w_router = cs[:, C_WR:C_WR + KB * EXPERTS].rearrange("p (k e) -> p k e", k=KB)
        rel_scratch = nc.dram_tensor("rel_scratch", [DIFF_HEADS, 384], F32, kind="Internal").ap()

        small_in = sem("small_in")
        xT_ld = [sem(f"xT_ld{i}") for i in range(2)]
        memT_ld = sem("memT_ld")
        rel_stored = sem("rel_stored")
        rel_ld = sem("rel_ld")
        ln_ld = [sem(f"ln{i}_ld") for i in range(3)]
        xres_ld = sem("xres_ld")
        wsd_ld = sem("wsd_ld")
        items_ld = sem("items_ld")
        dense_ld = [sem(f"dense_ld{i}") for i in range(RAW_TILES)]
        expert_ld = [sem(f"expert_ld{i}") for i in range(RING)]
        extra_ld = sem("extra_ld")
        stored = sem("stored")
        proj_ready = sem("proj_ready")
        rel_mm = sem("rel_mm")
        flip_mm = sem("flip_mm")
        dt_mm = sem("dt_mm")
        dtT_mm = sem("dtT_mm")
        end_mm = sem("end_mm")
        cb_mm = sem("cb_mm")
        xs_mm = sem("xs_mm")
        seg_mm = sem("seg_mm")
        logit_mm = sem("logit_mm")
        y_mm = sem("y_mm")
        off_mm = sem("off_mm")
        attnT_mm = sem("attnT_mm")
        av_mm = sem("av_mm")
        ssq_mm = sem("ssq_mm")
        xt_mm = sem("xt_mm")
        clog_mm = sem("clog_mm")
        cpT_mm = sem("cpT_mm")
        cav_mm = sem("cav_mm")
        score_mm = sem("score_mm")
        hsT_mm = sem("hsT_mm")
        rank_mm = sem("rank_mm")
        gath_mm = sem("gath_mm")
        gu_mm = sem("gu_mm")
        scatT_mm = sem("scatT_mm")
        hT_mm = sem("hT_mm")
        down_mm = sem("down_mm")
        moe_mm = sem("moe_mm")
        w_rounded = sem("w_rounded")
        x_rounded = sem("x_rounded")
        mem_rounded = sem("mem_rounded")
        oT_rounded = sem("oT_rounded")
        yT_rounded = sem("yT_rounded")
        mixT_rounded = sem("mixT_rounded")
        act_took = sem("act_took")
        xpad_full = sem("xpad_full")
        conv_silu = sem("conv_silu")
        small_exp = sem("small_exp")
        flip_cp = sem("flip_cp")
        seg_exp = sem("seg_exp")
        prob_exp = sem("prob_exp")
        fac_exp = sem("fac_exp")
        attnT_cp = sem("attnT_cp")
        av_cp = sem("av_cp")
        z_silu = sem("z_silu")
        squared = sem("squared")
        gate_sig = sem("gate_sig")
        rms_sqrt = sem("rms_sqrt")
        ln_sqrt = sem("ln_sqrt")
        xt_cp = sem("xt_cp")
        cprob_exp = sem("cprob_exp")
        cpT_cp = sem("cpT_cp")
        cav_cp = sem("cav_cp")
        score_sig = sem("score_sig")
        sh_silu = sem("sh_silu")
        hsT_cp = sem("hsT_cp")
        split_h = sem("split_h")
        gath_act = sem("gath_act")
        h_silu = sem("h_silu")
        hT_cp = sem("hT_cp")
        yh_done = sem("yh_done")
        dve = sem("dve_chain")
        w_rest_dve = sem("w_rest_dve")
        w_rest_pool = sem("w_rest_pool")
        x_rest = sem("x_rest")
        mem_rest = sem("mem_rest")
        oT_rest = sem("oT_rest")
        yT_rest = sem("yT_rest")
        mixT_rest = sem("mixT_rest")
        xt_rest = sem("xt_rest")
        cav_rest = sem("cav_rest")
        dtT_cp = sem("dtT_cp")
        dve_took = sem("dve_took")
        pad_zero = sem("pad_zero")
        rel_cp = sem("rel_cp")
        conv_done = sem("conv_done")
        lam_dots = sem("lam_dots")
        dt_pre = sem("dt_pre")
        a_done = sem("a_done")
        cb_cp = sem("cb_cp")
        xs_cp = sem("xs_cp")
        amax_done = sem("amax_done")
        masked_dec = sem("masked_dec")
        attn_done = sem("attn_done")
        y_done = sem("y_done")
        yz_done = sem("yz_done")
        rms_rcp = sem("rms_rcp")
        yT_done = sem("yT_done")
        oT_done = sem("oT_done")
        mix_done = sem("mix_done")
        ln_var = sem("ln_var")
        ln_done = sem("ln_done")
        cmax_done = sem("cmax_done")
        cprob_done = sem("cprob_done")
        sh_done = sem("sh_done")
        sel_done = sem("sel_done")
        place_done = sem("place_done")
        onehot_done = sem("onehot_done")
        split_l = sem("split_l")
        gath_dve = sem("gath_dve")
        h_done = sem("h_done")
        scatT_cp = sem("scatT_cp")
        gate_cp = sem("gate_cp")
        yl_done = sem("yl_done")
        item_done = sem("item_done")
        gdec_done = sem("gdec_done")
        xend_done = sem("xend_done")
        o_hot, o_gath, o_xg, o_gu, o_h1, o_h, o_T, o_Tcp, o_down, o_y, o_scat = (
            sem(n) for n in ("o_hot", "o_gath", "o_xg", "o_gu", "o_h1", "o_h", "o_T", "o_Tcp", "o_down", "o_y",
                             "o_scat"))

        block = ctx.enter_context(nc.Block())

        def expert_tile(jj, kind):
            return (3 * jj + kind + 3) % RING

        def expert_count(i, jj, kind):
            return (i * (3 * 8 // RING) + (3 * jj + kind) // RING + 1) * 16

        @block.sync
        def _(sp):
            def dense_tile(m, parts=1):
                slot = m % RAW_TILES
                if m >= RAW_TILES:
                    sp.wait_ge(proj_ready, DONE[2 * (m - RAW_TILES) + 1])
                sp.dma_start(raw[:, 2 * slot:2 * slot + 2, :], wdense[m].rearrange("p (c w) -> p c w", c=2)
                             ).then_inc(dense_ld[slot], 16)

            def dense_kinds(first, after):
                for m in range(CHUNK0[first] // 2, CHUNK0[after] // 2):
                    dense_tile(m)

            for half in range(2):
                sp.dma_start(xT[:, 4 * half:4 * half + 4, :], xT_in[:, 4 * half:4 * half + 4, :]
                             ).then_inc(xT_ld[half], 16)
                if half == 0:
                    dense_tile(0)
            sp.dma_start(cs[:], small).then_inc(small_in, 16)
            sp.dma_start(row[:], rows.partition_broadcast(P)).then_inc(small_in, 16)
            for m in range(1, RAW_TILES):
                dense_tile(m)
            sp.dma_start(memT[:], memT_in).then_inc(memT_ld, 16)
            for m in range(RAW_TILES, CHUNK0["q"] // 2):
                dense_tile(m)
            sp.wait_ge(rel_cp, 1)
            sp.dma_start(rel_scratch, bds[0:DIFF_HEADS, :]).then_inc(rel_stored, 16)
            dense_tile(CHUNK0["q"] // 2)
            sp.wait_ge(rel_stored, 16)
            sp.dma_start(rel_flipped[:], bass.AP(rel_scratch.tensor, 0, [[1, P], [384, DIFF_HEADS], [1, SEQ]])
                         ).then_inc(rel_ld, 16)
            for m in range(CHUNK0["q"] // 2 + 1, CHUNK0["cvb"] // 2):
                dense_tile(m)
            first = [CHUNK0["cvb"] // 2 + 2 * x for x in range(3)]
            for m in range(CHUNK0["cvb"] // 2, CHUNK0["co"] // 2):
                if m in first:
                    x = first.index(m)
                    sp.wait_ge(proj_ready, out_index("ssd", KB - 1) + 1)
                    sp.dma_start(ring[:, 3 + x, :], wstream[x]).then_inc(expert_ld[3 + x], 16)
                dense_tile(m)
            dense_kinds("co", "sh")
            for m in range(CHUNK0["sh"] // 2, N_CHUNKS // 2):
                dense_tile(m)
            for x in (4, 5, 3):
                sp.wait_ge(proj_ready, DONE[N_SPLIT - 1] if x > 3 else DONE[-1])
                if x == 4:
                    sp.wait_ge(xt_cp, 4)
                sp.dma_start(ring[:, x - 3, :], wstream[x]).then_inc(expert_ld[x - 3], 16)
            with sp.Fori(0, 3 * PAIRS // RING - 1) as k:
                for m in range(RING):
                    if m % 3 < 2:
                        sp.wait_ge(gu_mm, k * 2 + (m // 3 + 1))
                    else:
                        sp.wait_ge(down_mm, k * 4 + 2 * (m // 3 + 1))
                    slot = (m + 3) % RING
                    sp.dma_start(ring[:, slot, :], wstream[k * RING + (RING + m)]
                                 ).then_inc(expert_ld[slot], 16)
            sp.wait_ge(items_ld, 32)
            n_items = sp.value_load(items[0:1, P:P + 1], min_val=0, max_val=EXTRA)
            sp.wait_ge(down_mm, 2 * PAIRS)
            with sp.If(n_items > 0):
                with sp.Fori(0, n_items) as i:
                    item = sp.value_load(items[0:1, bass.ds(i, 1)], min_val=0, max_val=EXTRA - 1)
                    sp.wait_ge(o_scat, i)
                    for m in range(3):
                        sp.dma_start(ring[:, m, :], wstream[(item % PAIRS) * 3 + m]
                                     ).then_inc(extra_ld, 16)
            for t in range(TB):
                sp.wait_ge(ln_done, 3 * TB - TB + t + 1)
                sp.dma_start(out[0, t * P:(t + 1) * P, :], xres[:, t, :]).then_inc(stored, 16)
            sp.wait_ge(stored, 16 * TB)

        @block.gpsimd
        def _(pool):
            split = [0]

            def rests(upto):
                while split[0] <= upto:
                    q = split[0]
                    if not rest_by_dve(q):
                        pool.wait_ge(w_rounded, q + 1)
                        nc.gpsimd.tensor_tensor(w_lo[:, q % 6, :], raw[:, q % 6, :],
                                                w_hi[:, q % ROUNDED, :].bitcast(F32), ALU.subtract
                                                ).then_inc(w_rest_pool, 1)
                    split[0] += 1

            def decays(i):
                for t in range(TB):
                    if i == 0:
                        pool.wait_ge(a_done, 1)
                    else:
                        pool.wait_ge(seg_mm, 2 * (i - 1) + t + 1)
                    nc.gpsimd.tensor_tensor(gdec[:, t], strict.unsqueeze(1).to_broadcast([P, 4, P]),
                                            a_v[:, t, 4 * i:4 * i + 4].unsqueeze(2).to_broadcast([P, 4, P]),
                                            ALU.mult).then_inc(gdec_done, 1)

            def inputs_at_end(i):
                if i == 0:
                    pool.wait_ge(small_exp, 4)
                    pool.wait_ge(xs_cp, 8)
                else:
                    pool.wait_ge(off_mm, i)
                nc.gpsimd.tensor_tensor(xend[:], xsdt[:, 0, 256 * i:256 * i + 256].rearrange("p (h e) -> p h e", h=4),
                                        decay_end[:, 4 * i:4 * i + 4].unsqueeze(2).to_broadcast([P, 4, HEAD]),
                                        ALU.mult).then_inc(xend_done, 1)

            pool.wait_ge(small_in, 32)
            rests(CHUNK0["q"] + 7)
            decays(0)
            rests(CHUNK0["v"] + 3)
            inputs_at_end(0)
            rests(CHUNK0["z"] + 3)
            for i in range(1, XS_BLOCKS // 2):
                c0 = CHUNK0["z"] + 4 * i
                decays(i)
                rests(c0 + 1)
                inputs_at_end(i)
                rests(c0 + 3)
            rests(CHUNK0["ck"] + 1)
            for g in range(2):
                pool.wait_ge(mem_rounded, g + 1)
                nc.gpsimd.tensor_tensor(memT_r[1][:, 4 * g:4 * g + 4, :], memT[:, 4 * g:4 * g + 4, :],
                                        memT_r[0][:, 4 * g:4 * g + 4, :].bitcast(F32), ALU.subtract
                                        ).then_inc(mem_rest, 1)
            rests(CHUNK0["ck"] + 3)
            pool.wait_ge(y_mm, XS_BLOCKS // 2)
            pool.wait_ge(off_mm, XS_BLOCKS // 2)
            pool.wait_ge(xend_done, XS_BLOCKS // 2)
            pool.dma_start(xres[:], x_in).then_inc(xres_ld, 16)
            rests(CHUNK0["mix"] + 1)
            pool.wait_ge(proj_ready, out_index("ssd", KB - 1) + 1)
            pool.dma_start(ln1[:], lnp[0:1].rearrange("a b d -> (a b) d").partition_broadcast(P)).then_inc(ln_ld[0], 16)
            rests(CHUNK0["cq"] + 3)
            pool.wait_ge(proj_ready, out_index("cvb", 3) + 1)
            pool.dma_start(ln2[:], lnp[1:2].rearrange("a b d -> (a b) d").partition_broadcast(P)).then_inc(ln_ld[1], 16)
            rests(N_SPLIT - 1)
            pool.wait_ge(ln_done, 2 * TB)
            pool.dma_start(wsd[:], wshd).then_inc(wsd_ld, 16)
            pool.wait_ge(item_done, 2)
            pool.dma_start(items[0:1, 0:P], item_col[:, 0:1]).then_inc(items_ld, 16)
            pool.dma_start(items[0:1, P:P + 1], item_col[0:1, 1:2]).then_inc(items_ld, 16)
            pool.wait_ge(gu_mm, PAIRS)
            pool.dma_start(ln3[:], lnp[2:3].rearrange("a b d -> (a b) d").partition_broadcast(P)).then_inc(ln_ld[2], 16)

        @block.scalar
        def _(act):
            split = [0]

            def round_chunks(n):
                while split[0] < N_SPLIT and (split[0] < ROUNDED or DONE[split[0] - ROUNDED] <= n + 1):
                    q = split[0]
                    act.wait_ge(dense_ld[q // 2 % RAW_TILES], 16 * (q // 2 // RAW_TILES + 1))
                    if q >= ROUNDED:
                        act.wait_ge(proj_ready, DONE[q - ROUNDED])
                    nc.scalar.activation(w_hi[:, q % ROUNDED, :], raw[:, q % 6, :], ACT.Copy).then_inc(w_rounded, 1)
                    split[0] += 1

            def leave(kind, k, dst, scale=1.0):
                n = out_index(kind, k)
                act.wait_ge(proj_ready, n + 1)
                nc.scalar.activation(dst, S[n % 4][:, 0:SEQ], ACT.Copy, scale=scale).then_inc(act_took, 1)
                round_chunks(n)

            def leave_tokens(kind, k, dst, col0=0):
                c = col0 + k // TB * SEQ
                leave(kind, k, dst[:, k % TB, c:c + SEQ])

            for half in range(2):
                act.wait_ge(xT_ld[half], 16)
                nc.scalar.activation(xT_r[0][:, 4 * half:4 * half + 4, :], xT[:, 4 * half:4 * half + 4, :], ACT.Copy
                                     ).then_inc(x_rounded, 1)
                if half == 0:
                    act.wait_ge(dense_ld[0], 16)
                    nc.scalar.activation(w_hi[:, 0, :], raw[:, 0, :], ACT.Copy).then_inc(w_rounded, 1)
                    split[0] = 1
            round_chunks(-1)
            act.wait_ge(small_in, 32)
            nc.scalar.activation(wdt_r[0][:], w_dt, ACT.Copy).then_inc(x_rounded, 1)
            act.wait_ge(lam_dots, 2)
            nc.scalar.activation(exp_alog[:], row[:, R_ALOG:R_ALOG + SSD_HEADS], ACT.Exp).then_inc(small_exp, 1)
            nc.scalar.activation(lam_e[:], lam_d[:], ACT.Exp).then_inc(small_exp, 1)

            def conv_act(b):
                act.wait_ge(conv_done, b + 1)
                nc.scalar.activation(xc[:, b, :], acc[:, b % 2, :], ACT.Silu, bias=conv_b[:, b:b + 1]
                                     ).then_inc(conv_silu, 1)

            act.wait_ge(pad_zero, 1)
            for b in range(NXB):
                if b >= 4:
                    act.wait_ge(conv_done, b - 3)
                leave("xbc", b, xpad[:, b % 4, CONV - 1:PADDED])
                if b >= 1:
                    conv_act(b - 1)
            conv_act(NXB - 1)
            act.wait_ge(dt_pre, 1)
            nc.scalar.activation(dt_t[1][:], dt_t[1][:], ACT.Exp, scale=-1.0).then_inc(small_exp, 1)

            for h in range(DIFF_HEADS):
                leave("q", h, qT[:, h, :], scale=HEAD ** -0.5)
            for h in range(DIFF_HEADS):
                leave("k", h, kT[:, h, :])
            for k in range(4):
                act.wait_ge(flip_mm, k + 1)
                nc.scalar.activation(rel[:, 2 * k:2 * k + 2, :], W[k][:].rearrange("p (h k) -> p h k", h=2), ACT.Copy
                                     ).then_inc(flip_cp, 1)
            act.wait_ge(end_mm, 1)
            nc.scalar.activation(decay_end[:], W[0][:, 0:SSD_HEADS], ACT.Exp).then_inc(small_exp, 1)
            for k in range(8):
                leave_tokens("v", k, v)

            for i in range(8):
                for t in range(TB):
                    act.wait_ge(seg_mm, 2 * i + t + 1)
                    if i >= 1:
                        act.wait_ge(y_mm, i)
                    nc.scalar.activation(dec[:, t], W[2 + t][:].rearrange("p (h l) -> p h l", h=4), ACT.Exp
                                         ).then_inc(seg_exp, 1)
                act.wait_ge(amax_done, i + 1)
                for c, (o, w) in enumerate(((0, P), (P, SEQ), (P + SEQ, P), (2 * P + SEQ, SEQ))):
                    nc.scalar.activation(lg[:, o:o + w], lg[:, o:o + w], ACT.Exp, bias=a_neg[:, c:c + 1],
                                         accum_out=a_sum[:, c:c + 1]).then_inc(prob_exp, 1)
                kind, dst = ("z", z) if i < 4 else ("gate", gt)
                k0 = 4 * (i % 4)
                for j in range(2):
                    leave(kind, k0 + j, dst[:, k0 + j, :])
                    if i == 7:
                        act.wait_ge(memT_ld, 16)
                        nc.scalar.activation(memT_r[0][:, 4 * j:4 * j + 4, :], memT[:, 4 * j:4 * j + 4, :], ACT.Copy
                                             ).then_inc(mem_rounded, 1)
                act.wait_ge(off_mm, i + 1)
                if i >= 1:
                    act.wait_ge(y_done, i)
                nc.scalar.activation(fac[:], W[3][:, SEQ:2 * SEQ].rearrange("p (b l) -> p b l", b=2), ACT.Exp
                                     ).then_inc(fac_exp, 1)
                act.wait_ge(attnT_mm, i + 1)
                if i >= 1:
                    act.wait_ge(av_mm, i)
                nc.scalar.activation(attnT[:], W[0][:, 0:384], ACT.Copy).then_inc(attnT_cp, 1)
                leave(kind, k0 + 2, dst[:, k0 + 2, :])
                leave(kind, k0 + 3, dst[:, k0 + 3, :])
                act.wait_ge(av_mm, i + 1)
                nc.scalar.activation(oT[:, i, :], W[1][:, 0:SEQ], ACT.Copy).then_inc(av_cp, 1)

            def squares_of_y(g):
                act.wait_ge(yz_done, g + 1)
                nc.scalar.activation(z[:, 4 * g:4 * g + 4, :], xc[:, 4 * g:4 * g + 4, :], ACT.Square
                                     ).then_inc(squared, 1)

            act.wait_ge(av_cp, DIFF_HEADS)
            for k in range(4):
                nc.scalar.activation(sqd[:, 2 * k:2 * k + 2, :], oT[:, 2 * k:2 * k + 2, :], ACT.Square
                                     ).then_inc(squared, 1)
            act.wait_ge(act_took, taken_count(out_index("z", 15)))
            for g in range(GROUPS):
                nc.scalar.activation(z[:, 4 * g:4 * g + 4, :], z[:, 4 * g:4 * g + 4, :], ACT.Silu).then_inc(z_silu, 1)
                leave("ck", g, kcT[:, g, :])
            for k in range(GROUPS):
                squares_of_y(k)
                leave("ck", GROUPS + k, kcT[:, GROUPS + k, :])

            def root(k):
                w = 512 if k < GROUPS else SEQ
                act.wait_ge(rms_rcp, k + 1)
                nc.scalar.activation(rms[:, k, 0:w], rms[:, k, 0:w], ACT.Sqrt).then_inc(rms_sqrt, 1)

            for k in range(GROUPS):
                root(k)
            leave_tokens("cv", 0, vc)
            leave_tokens("cv", 1, vc)
            for g in range(2):
                act.wait_ge(oT_done, 4 * g + 4)
                nc.scalar.activation(oT_r[0][:, 4 * g:4 * g + 4, :], oT[:, 4 * g:4 * g + 4, :], ACT.Copy
                                     ).then_inc(oT_rounded, 1)
            leave_tokens("cv", 2, vc)
            leave_tokens("cv", 3, vc)
            act.wait_ge(act_took, taken_count(out_index("gate", 15)))
            for k in range(GROUPS):
                root(GROUPS + k)
            for g in (2, 3, 0, 1):
                nc.scalar.activation(gt[:, 4 * g:4 * g + 4, :], gt[:, 4 * g:4 * g + 4, :], ACT.Sigmoid
                                     ).then_inc(gate_sig, 1)
                round_chunks(out_index("diff", (g + 2) % 4))
            for g in range(GROUPS):
                act.wait_ge(yT_done, 4 * g + 4)
                nc.scalar.activation(yT_r[0][:, 4 * g:4 * g + 4, :], xc[:, 4 * g:4 * g + 4, :], ACT.Copy
                                     ).then_inc(yT_rounded, 1)
                round_chunks(out_index("diff", 4 + g))
            for k in range(KB):
                round_chunks(out_index("ssd", k))
                if k % 2:
                    act.wait_ge(mix_done, k + 1)
                    nc.scalar.activation(mixT_r[0][:, k - 1:k + 1, :], mixT[:, k - 1:k + 1, :], ACT.Copy
                                         ).then_inc(mixT_rounded, 1)
            for k in range(8):
                round_chunks(out_index("mix", k))
            for k in range(4):
                leave_tokens("cvb", k, vc, 512)

            def norm_sqrt(which):
                for t in range(TB):
                    act.wait_ge(ln_var, TB * which + t + 1)
                    nc.scalar.activation(rstd[:, t:t + 1], rvar[:, t:t + 1], ACT.Sqrt).then_inc(ln_sqrt, 1)

            def turned(which, dst):
                for k in range(4):
                    act.wait_ge(xt_mm, 4 * which + k + 1)
                    nc.scalar.activation(dst[:, 4 * (k % 2):4 * (k % 2) + 4, k // 2 * P:(k // 2 + 1) * P],
                                         W[k][:].rearrange("p (b t) -> p b t", b=4), ACT.Copy).then_inc(xt_cp, 1)

            norm_sqrt(0)
            turned(0, x1T_r[0])
            for k in range(KB):
                leave("cq", k, qcT[:, k, :], scale=(D // MEM_HEADS) ** -0.5)
            for h in range(MEM_HEADS):
                act.wait_ge(cmax_done, h + 1)
                for t in range(TB):
                    nc.scalar.activation(pc[:, h, t, :], W[h][:, t * SEQ:(t + 1) * SEQ], ACT.Exp,
                                         bias=c_neg[:, h, t:t + 1], accum_out=c_sum[:, h, t:t + 1]
                                         ).then_inc(cprob_exp, 1)
            for h in range(MEM_HEADS):
                act.wait_ge(cpT_mm, h + 1)
                nc.scalar.activation(pcT[:, h], W[h][:].rearrange("p (k q) -> p k q", k=2), ACT.Copy
                                     ).then_inc(cpT_cp, 1)
            for h in range(MEM_HEADS):
                act.wait_ge(cav_mm, h + 1)
                nc.scalar.activation(ocT_r[0][:, 2 * h:2 * h + 2, :], W[h][:].rearrange("p (k q) -> p k q", k=2), ACT.Copy
                                     ).then_inc(cav_cp, 1)
            for k in range(8):
                round_chunks(out_index("co", k))
            norm_sqrt(1)
            turned(1, x2T)
            act.wait_ge(score_mm, 1)
            nc.scalar.activation(scores[:], W[0][:, 0:TB * EXPERTS].rearrange("p (t e) -> p t e", t=TB), ACT.Sigmoid
                                 ).then_inc(score_sig, 1)
            for t in range(TB):
                act.wait_ge(ln_done, TB + t + 1)
                nc.scalar.activation(x2h[:, t, :], xres[:, t, :], ACT.Copy).then_inc(split_h, 1)
            act.wait_ge(xt_mm, 8)
            for t in range(TB):
                n = out_index("sh", t)
                act.wait_ge(proj_ready, n + 1)
                if t:
                    act.wait_ge(sh_done, t)
                nc.scalar.activation(h1[:], S[n % 4][:, 0:FF], ACT.Silu).then_inc(sh_silu, 1)
                act.wait_ge(hsT_mm, t + 1)
                nc.scalar.activation(hsT[:, :, t * P:(t + 1) * P],
                                     W[1][:, t * SEQ:(t + 1) * SEQ].rearrange("p (k q) -> p k q", k=2), ACT.Copy
                                     ).then_inc(hsT_cp, 1)
            nc.scalar.activation(ident_r[:], ident, ACT.Copy).then_inc(hsT_cp, 1)
            for k in range(0, KB, 2):
                act.wait_ge(gath_mm, k + 1)
                nc.scalar.activation(xg[0][:, k, :], S[0][:], ACT.Copy).then_inc(gath_act, 1)
            with act.Fori(0, PAIRS // 8) as i:
                for jj in range(8):
                    act.wait_ge(gu_mm, i * 8 + (jj + 1))
                    nc.scalar.activation(h1[:], S[2][:, 0:FF], ACT.Silu).then_inc(h_silu, 1)
                    act.wait_ge(gath_mm, i * 16 + (KB + 2 * jj + 1))
                    nc.scalar.activation(xg[(jj // 4 + 1) % 2][:, 2 * (jj % 4), :], S[0][:], ACT.Copy
                                         ).then_inc(gath_act, 1)
                    act.wait_ge(hT_mm, i * 8 + (jj + 1))
                    nc.scalar.activation(hT[:], S[2][:, 0:2 * P].rearrange("p (k s) -> p k s", k=2), ACT.Copy
                                         ).then_inc(hT_cp, 1)
                    act.wait_ge(gate_cp, i * 16 + 2 * (jj + 1))
                    for c in range(2):
                        act.wait_ge(down_mm, i * 16 + (2 * jj + c + 1))
                        nc.scalar.activation(yh[:, c * 512:(c + 1) * 512], (S[3], S[1])[c][:], ACT.Copy,
                                             scale=slot_gate[:, 0:1]).then_inc(yh_done, 1)
            act.wait_ge(items_ld, 32)
            n_items = act.value_load(items[0:1, P:P + 1], min_val=0, max_val=EXTRA)
            with act.If(n_items > 0):
                with act.Fori(0, n_items) as i:
                    act.wait_ge(o_gu, i + 1)
                    nc.scalar.activation(h1[:], S[2][:, 0:FF], ACT.Silu).then_inc(o_h1, 1)
                    act.wait_ge(o_down, i + 1)
                    for c in range(2):
                        nc.scalar.activation(yh[:, c * 512:(c + 1) * 512], (S[3], S[1])[c][:], ACT.Copy,
                                             scale=slot_gate[:, 0:1]).then_inc(o_y, 1)
            norm_sqrt(2)

        @block.vector
        def _(ve):
            steps = [0]

            def link(ins):
                steps[0] += 1
                ins.then_inc(dve, 1)
                ve.wait_ge(dve, steps[0])

            tt = nc.vector.tensor_tensor
            ts = nc.vector.tensor_scalar
            stt = nc.vector.scalar_tensor_tensor

            split = [0]

            def chunk_rests(n):
                while split[0] < N_SPLIT and (split[0] < ROUNDED or DONE[split[0] - ROUNDED] <= n + 1):
                    q = split[0]
                    if rest_by_dve(q):
                        ve.wait_ge(w_rounded, q + 1)
                        tt(w_lo[:, q % 6, :], raw[:, q % 6, :], w_hi[:, q % ROUNDED, :].bitcast(F32), ALU.subtract
                           ).then_inc(w_rest_dve, 1)
                    split[0] += 1

            link(nc.vector.memset(place_e[:], 0.0))
            nc.vector.memset(xpad[:], 0.0).then_inc(pad_zero, 1)
            for half in range(2):
                ve.wait_ge(x_rounded, half + 1)
                tt(xT_r[1][:, 4 * half:4 * half + 4, :], xT[:, 4 * half:4 * half + 4, :],
                   xT_r[0][:, 4 * half:4 * half + 4, :].bitcast(F32), ALU.subtract).then_inc(x_rest, 1)
                if half == 0:
                    ve.wait_ge(w_rounded, 1)
                    tt(w_lo[:, 0, :], raw[:, 0, :], w_hi[:, 0, :].bitcast(F32), ALU.subtract).then_inc(w_rest_dve, 1)
                    split[0] = 1
            chunk_rests(-1)
            ve.wait_ge(small_in, 32)
            ve.wait_ge(x_rounded, 3)
            tt(wdt_r[1][:], w_dt, wdt_r[0][:].bitcast(F32), ALU.subtract).then_inc(x_rest, 1)
            for k in range(2):
                q = R_LAM + 128 * k
                link(tt(lam_tmp[:], row[:, q:q + 64], row[:, q + 64:q + 128], ALU.mult))
                nc.vector.tensor_reduce(lam_d[:, k:k + 1], lam_tmp[:], AX.X, ALU.add).then_inc(lam_dots, 1)
                ve.wait_ge(lam_dots, k + 1)
            ve.wait_ge(small_exp, 2)
            link(stt(neg_lam[:], lam_e[:, 1:2], -LAM_INIT, lam_e[:, 0:1], ALU.add, ALU.subtract))
            link(ts(exp_alog[:], exp_alog[:], -1.0, None, ALU.mult))

            ve.wait_ge(pad_zero, 1)
            for b in range(NXB):
                ve.wait_ge(act_took, b + 1)
                if b >= 2:
                    ve.wait_ge(conv_silu, b - 1)
                link(ts(acc[:, b % 2, :], xpad[:, b % 4, 0:SEQ], conv_w[:, b, 0:1], None, ALU.mult))
                for j in range(1, CONV):
                    ins = stt(acc[:, b % 2, :], xpad[:, b % 4, j:j + SEQ], conv_w[:, b, j:j + 1], acc[:, b % 2, :],
                              ALU.mult, ALU.add)
                    if j < CONV - 1:
                        link(ins)
                ins.then_inc(conv_done, 1)
                chunk_rests(out_index("xbc", b))
                if b == 4:
                    ve.wait_ge(rel_mm, 1)
                    nc.vector.tensor_copy(bds[0:DIFF_HEADS, :], W[0][0:DIFF_HEADS, 0:384]).then_inc(rel_cp, 1)

            ve.wait_ge(dt_mm, 1)
            nc.vector.tensor_copy(dtT[0:SSD_HEADS, :], W[1][0:SSD_HEADS, 0:SEQ]).then_inc(dtT_cp, 1)
            ve.wait_ge(dtT_mm, 1)
            u, e, s, s2 = (x[:] for x in dt_t)
            raw_dt = W[1][:, SEQ:SEQ + TB * SSD_HEADS].rearrange("p (t h) -> p t h", t=TB)
            link(tt(u, raw_dt, row[:, R_DTB:R_DTB + SSD_HEADS].unsqueeze(1).to_broadcast([P, TB, SSD_HEADS]), ALU.add))
            link(ts(s, u, -1.0, None, ALU.mult))
            tt(e, u, s, ALU.max).then_inc(dt_pre, 1)
            ve.wait_ge(small_exp, 3)
            link(ts(s, e, 2.0, None, ALU.add))
            link(nc.vector.reciprocal(s2, s))
            link(tt(s, e, s2, ALU.mult))
            link(tt(s2, s, s, ALU.mult))
            link(ts(e, s2, 1.0 / 15, 1.0 / 13, ALU.mult, ALU.add))
            for c in (11, 9, 7, 5, 3, 1):
                link(tt(e, e, s2, ALU.mult))
                link(ts(e, e, 1.0 / c, None, ALU.add))
            link(tt(e, e, s, ALU.mult))
            link(ts(u, u, 0.0, None, ALU.max))
            link(stt(dt_v[:], e, 2.0, u, ALU.mult, ALU.add))
            tt(a_v[:], dt_v[:], exp_alog[:].unsqueeze(1).to_broadcast([P, TB, SSD_HEADS]), ALU.mult
               ).then_inc(a_done, 1)

            chunk_rests(out_index("k", 7))
            ve.wait_ge(cb_mm, GROUPS)
            for g in range(GROUPS):
                bank = W[(1 + g) % 4]
                tt(cbm[:, g].rearrange("p (a l) -> p a l", a=3)[:, 0:3:2, :],
                   bank[:, 0:384].rearrange("p (a l) -> p a l", a=3)[:, 0:3:2, :],
                   tri.unsqueeze(1).to_broadcast([P, 2, P]), ALU.mult).then_inc(cb_cp, 1)
                nc.vector.tensor_copy(cbm[:, g, P:2 * P], bank[:, P:2 * P]).then_inc(cb_cp, 1)
            for k in range(8):
                t, quad = k // 4, k % 4
                ve.wait_ge(xs_mm, k + 1)
                tt(xsdt[:, t, quad * 512:(quad + 1) * 512].rearrange("p (h e) -> p h e", h=8),
                   W[(1 + k) % 4][:].rearrange("p (h e) -> p h e", h=8),
                   dt_v[:, t, quad * 8:(quad + 1) * 8].unsqueeze(2).to_broadcast([P, 8, HEAD]), ALU.mult
                   ).then_inc(xs_cp, 1)

            chunk_rests(out_index("v", 3))
            ve.wait_ge(flip_cp, 4)
            for i in range(8):
                ve.wait_ge(logit_mm, i + 1)
                if i >= 1:
                    ve.wait_ge(attnT_mm, i)
                for m in range(2):
                    o = m * 384
                    for c, (o2, w, r0) in enumerate(((0, P, P), (P, SEQ, 0))):
                        ins = nc.vector.tensor_tensor_reduce(
                            lg[:, o + o2:o + o2 + w], W[m][:, o2:o2 + w], rel[:, i, r0:r0 + w], 1.0, -3.0e38,
                            ALU.add, ALU.max, a_max[:, 2 * m + c:2 * m + c + 1])
                        link(ins)
                ts(a_neg[:], a_max[:], -1.0, None, ALU.mult).then_inc(amax_done, 1)
                for t in range(TB):
                    ve.wait_ge(seg_exp, 2 * i + t + 1)
                    tt(dec[:, t], dec[:, t],
                       cbm[:, i // 2, 2 * t * P:(2 * t + 1) * P].unsqueeze(1).to_broadcast([P, 4, P]), ALU.mult
                       ).then_inc(masked_dec, 1)
                chunk_rests(out_index("z", 4 * i - 1) if i else out_index("v", 7))
                ve.wait_ge(prob_exp, 4 * i + 4)
                link(nc.vector.reciprocal(a_rcp[:], a_sum[:]))
                link(ts(a_rcp[:, 2:4], a_rcp[:, 2:4], neg_lam[:, 0:1], None, ALU.mult))
                link(ts(dtmp[:, 0:P], lg[:, 384:384 + P], a_rcp[:, 2:3], None, ALU.mult))
                link(ts(dtmp[:, P:384], lg[:, 512:768], a_rcp[:, 3:4], None, ALU.mult))
                link(stt(attn[:, 0:P], lg[:, 0:P], a_rcp[:, 0:1], dtmp[:, 0:P], ALU.mult, ALU.add))
                stt(attn[:, P:384], lg[:, P:384], a_rcp[:, 1:2], dtmp[:, P:384], ALU.mult, ALU.add
                    ).then_inc(attn_done, 1)
                ve.wait_ge(y_mm, i + 1)
                for j in range(2):
                    b = 2 * i + j
                    link(stt(xc[:, b, :], xc[:, b, :], d_skip[:, b:b + 1], W[2][:, j * SEQ:(j + 1) * SEQ],
                             ALU.mult, ALU.add))
                ve.wait_ge(fac_exp, i + 1)
                link(tt(yo[:], W[3][:, 0:SEQ].rearrange("p (b l) -> p b l", b=2), fac[:], ALU.mult))
                tt(xc[:, 2 * i:2 * i + 2, P:SEQ], xc[:, 2 * i:2 * i + 2, P:SEQ], yo[:], ALU.add).then_inc(y_done, 1)

            chunk_rests(out_index("gate", 15))
            for g in range(GROUPS):
                ve.wait_ge(z_silu, g + 1)
                ve.wait_ge(y_done, 2 * g + 2)
                tt(xc[:, 4 * g:4 * g + 4, :], xc[:, 4 * g:4 * g + 4, :], z[:, 4 * g:4 * g + 4, :], ALU.mult
                   ).then_inc(yz_done, 1)

            def mean_squares(k):
                w, width, factor = (512, P, SUBLN_SCALE ** 2) if k < GROUPS else (SEQ, INNER // GROUPS, 1.0)
                ve.wait_ge(ssq_mm, k + 1)
                link(ts(rms[:, k, 0:w], W[k % 4][:, 0:w], 1.0 / width / factor, EPS / factor, ALU.mult, ALU.add))
                nc.vector.reciprocal(rms[:, k, 0:w], rms[:, k, 0:w]).then_inc(rms_rcp, 1)

            for k in range(GROUPS):
                mean_squares(k)
            chunk_rests(out_index("ck", 3))
            for k in range(GROUPS):
                ve.wait_ge(rms_sqrt, k + 1)
                for j in range(2):
                    h = 2 * k + j
                    stt(oT[:, h, :], oT[:, h, :], subln, rms[:, k, j * SEQ:(j + 1) * SEQ], ALU.mult, ALU.mult
                        ).then_inc(oT_done, 1)
            chunk_rests(out_index("ck", 7))
            for k in range(GROUPS):
                mean_squares(GROUPS + k)
            for g in range(2):
                ve.wait_ge(oT_rounded, g + 1)
                tt(oT_r[1][:, 4 * g:4 * g + 4, :], oT[:, 4 * g:4 * g + 4, :],
                   oT_r[0][:, 4 * g:4 * g + 4, :].bitcast(F32), ALU.subtract).then_inc(oT_rest, 1)
            chunk_rests(out_index("cv", 3))
            ve.wait_ge(yz_done, GROUPS)

            def scale_y(g):
                ve.wait_ge(rms_sqrt, GROUPS + g + 1)
                for b in range(4 * g, 4 * g + 4):
                    stt(xc[:, b, :], xc[:, b, :], ssd_g[:, b:b + 1], rms[:, GROUPS + g, 0:SEQ], ALU.mult, ALU.mult
                        ).then_inc(yT_done, 1)

            scale_y(0)
            for k in range(KB):
                n = out_index("diff", k)
                ve.wait_ge(proj_ready, n + 1)
                ve.wait_ge(gate_sig, k // 4 + 1)
                tt(mixT[:, k, :], S[n % 4][:, 0:SEQ], gt[:, KB + k, :], ALU.mult).then_inc(dve_took, 1)
                chunk_rests(n)
                if k < GROUPS - 1:
                    scale_y(k + 1)
                if k >= GROUPS:
                    g = k - GROUPS
                    ve.wait_ge(yT_rounded, g + 1)
                    tt(yT_r[1][:, 4 * g:4 * g + 4, :], xc[:, 4 * g:4 * g + 4, :],
                       yT_r[0][:, 4 * g:4 * g + 4, :].bitcast(F32), ALU.subtract).then_inc(yT_rest, 1)

            def mix_rest(j):
                ve.wait_ge(mixT_rounded, j + 1)
                tt(mixT_r[1][:, 2 * j:2 * j + 2, :], mixT[:, 2 * j:2 * j + 2, :],
                   mixT_r[0][:, 2 * j:2 * j + 2, :].bitcast(F32), ALU.subtract).then_inc(mixT_rest, 1)

            for k in range(KB):
                n = out_index("ssd", k)
                ve.wait_ge(proj_ready, n + 1)
                ve.wait_ge(gate_sig, 2 + k // 4 + 1)
                tt(gt[:, k, :], S[n % 4][:, 0:SEQ], gt[:, k, :], ALU.mult).then_inc(dve_took, 1)
                ve.wait_ge(dve_took, taken_count(n))
                tt(mixT[:, k, :], mixT[:, k, :], gt[:, k, :], ALU.add).then_inc(mix_done, 1)
                if k % 2 == 0 and k:
                    mix_rest(k // 2 - 1)
                chunk_rests(n)
            mix_rest(3)

            def layer_norm(which, weights):
                for t in range(TB):
                    for c in range(2):
                        link(nc.vector.bn_stats(bn[:, t, c, :], xres[:, t, c * 512:(c + 1) * 512]))
                    link(nc.vector.bn_aggr(mv[:, t, :], bn[:, t].rearrange("p c s -> p (c s)")))
                    link(ts(rvar[:, t:t + 1], mv[:, t, 1:2], EPS, None, ALU.add))
                    nc.vector.reciprocal(rvar[:, t:t + 1], rvar[:, t:t + 1]).then_inc(ln_var, 1)
                ve.wait_ge(ln_ld[which], 16)
                for t in range(TB):
                    ve.wait_ge(ln_sqrt, TB * which + t + 1)
                    link(ts(xres[:, t, :], xres[:, t, :], mv[:, t, 0:1], rstd[:, t:t + 1], ALU.subtract, ALU.mult))
                    link(tt(xres[:, t, :], xres[:, t, :], weights[:, 0, :], ALU.mult))
                    tt(xres[:, t, :], xres[:, t, :], weights[:, 1, :], ALU.add).then_inc(ln_done, 1)

            def add_output(kind):
                for k in range(8):
                    n = out_index(kind, k)
                    ve.wait_ge(proj_ready, n + 1)
                    part = xres[:, k % TB, k // TB * SEQ:k // TB * SEQ + SEQ]
                    stt(part, part, ALPHA, S[n % 4][:, 0:SEQ], ALU.mult, ALU.add).then_inc(dve_took, 1)
                    chunk_rests(n)
                ve.wait_ge(dve_took, taken_count(out_index(kind, 7)))

            ve.wait_ge(xres_ld, 16)
            add_output("mix")
            layer_norm(0, ln1)
            chunk_rests(out_index("cvb", 3))
            for k in range(4):
                ve.wait_ge(xt_cp, k + 1)
                part = (slice(None), slice(4 * (k % 2), 4 * (k % 2) + 4), slice(k // 2 * P, (k // 2 + 1) * P))
                tt(x1T_r[1][part], W[k][:].rearrange("p (b t) -> p b t", b=4), x1T_r[0][part].bitcast(F32),
                   ALU.subtract).then_inc(xt_rest, 1)
            chunk_rests(out_index("cq", 7))
            for h in range(MEM_HEADS):
                ve.wait_ge(clog_mm, h + 1)
                nc.vector.tensor_reduce(c_neg[:, h, :], W[h][:].rearrange("p (t k) -> p t k", t=TB), AX.X, ALU.max,
                                        negate=True).then_inc(cmax_done, 1)
            for h in range(MEM_HEADS):
                ve.wait_ge(cprob_exp, TB * h + TB)
                link(nc.vector.reciprocal(c_rcp[:, h, :], c_sum[:, h, :]))
                for t in range(TB):
                    ts(pc[:, h, t, :], pc[:, h, t, :], c_rcp[:, h, t:t + 1], None, ALU.mult).then_inc(cprob_done, 1)
            for h in range(MEM_HEADS):
                ve.wait_ge(cav_cp, h + 1)
                tt(ocT_r[1][:, 2 * h:2 * h + 2, :], W[h][:].rearrange("p (k q) -> p k q", k=2),
                   ocT_r[0][:, 2 * h:2 * h + 2, :].bitcast(F32), ALU.subtract).then_inc(cav_rest, 1)
            ve.wait_ge(ln_done, TB)
            add_output("co")
            layer_norm(1, ln2)

            ve.wait_ge(score_sig, 1)
            link(tt(choice[:], scores[:], row[:, R_RB:R_RB + EXPERTS].unsqueeze(1).to_broadcast([P, TB, EXPERTS]),
                    ALU.add))
            for t in range(TB):
                for g in range(EGROUPS):
                    ins = nc.vector.max(max8[:, t, g, :], choice[:, t, 8 * g:8 * g + 8])
                    if g == EGROUPS - 1:
                        link(ins)
            link(tt(gsc[:], max8[:, :, :, 0], max8[:, :, :, 1], ALU.add))
            other = gsc[:].unsqueeze(2).to_broadcast([P, TB, EGROUPS, EGROUPS])
            own = gsc[:].unsqueeze(3).to_broadcast([P, TB, EGROUPS, EGROUPS])
            tt(gcmp[:], other, own, ALU.is_gt)
            link(tt(geq[:], other, own, ALU.is_equal))
            for t in range(TB):
                link(tt(geq[:, t], geq[:, t], lower8, ALU.mult))
            link(tt(gcmp[:], gcmp[:], geq[:], ALU.add))
            link(nc.vector.tensor_reduce(goff[:], gcmp[:], AX.X, ALU.add))
            link(ts(gmask[:], goff[:], TOP_GROUPS - 0.5, None, ALU.is_lt))
            link(ts(goff[:], gmask[:], -MASKED, MASKED, ALU.mult, ALU.add))
            for t in range(TB):
                by_group = masked[:, t].rearrange("p (g e) -> p g e", g=EGROUPS)
                link(tt(by_group, choice[:, t].rearrange("p (g e) -> p g e", g=EGROUPS),
                        gmask[:, t].unsqueeze(2).to_broadcast([P, EGROUPS, 8]), ALU.mult))
                link(tt(by_group, by_group, goff[:, t].unsqueeze(2).to_broadcast([P, EGROUPS, 8]), ALU.add))
            for t in range(TB):
                link(nc.vector.max(top8[:, t, :], masked[:, t, :]))
                link(nc.vector.match_replace(choice[:, t, :], top8[:, t, :], masked[:, t, :], -2.0 * MASKED))
            ts(sel[:], choice[:], -MASKED, None, ALU.is_gt).then_inc(sel_done, 1)
            ve.wait_ge(sel_done, 1)
            link(tt(gates_e[:], scores[:], sel[:], ALU.mult))
            link(nc.vector.tensor_reduce(w_sum[:], gates_e[:], AX.X, ALU.add))
            link(nc.vector.reciprocal(w_rcp[:], w_sum[:]))
            for t in range(TB):
                link(ts(gates_e[:, t, :], gates_e[:, t, :], w_rcp[:, t:t + 1], ROUTED_SCALE, ALU.mult, ALU.mult))
            ve.wait_ge(rank_mm, 1)
            tt(place_e[:, :, 0:EXPERTS], W[2][:, 0:TB * EXPERTS].rearrange("p (t e) -> p t e", t=TB), sel[:], ALU.mult
               ).then_inc(place_done, 1)
            ve.wait_ge(place_done, 1)

            def make_onehot(buf, first):
                for t in range(TB):
                    tt(onehot[:, buf, t], slot_no.unsqueeze(1).to_broadcast([P, PER_GROUP, SLOTS]),
                       place_e[:, t, first].unsqueeze(2).to_broadcast([P, PER_GROUP, SLOTS]), ALU.is_equal
                       ).then_inc(onehot_done, 1)

            make_onehot(0, slice(0, PER_GROUP))
            for t in range(TB):
                ve.wait_ge(split_h, t + 1)
                tt(x2l[:, t, :], xres[:, t, :], x2h[:, t, :].bitcast(F32), ALU.subtract).then_inc(split_l, 1)
            for t in range(TB):
                n = out_index("sh", TB + t)
                ve.wait_ge(sh_silu, t + 1)
                ve.wait_ge(proj_ready, n + 1)
                if t:
                    ve.wait_ge(hsT_mm, t)
                tt(hh[:], h1[:], S[n % 4][:, 0:FF], ALU.mult).then_inc(sh_done, 1)
            ve.wait_ge(place_done, 1)
            cnt = W[2][:, TB * EXPERTS:(TB + 1) * EXPERTS].rearrange("p (q e) -> p e q", e=2)
            link(nc.vector.tensor_copy(pair_n[:], cnt[:, 0, :]))
            tt(pair_n[:], pair_n[:], cnt[:, 1, :], ALU.max).then_inc(place_done, 1)
            ve.wait_ge(place_done, 2)
            for r in range(1, CHUNKS):
                ins = ts(flags[:, 0, (r - 1) * PAIRS:r * PAIRS], pair_n[:], SLOTS * r + 0.5, None, ALU.is_gt)
            link(ins)
            link(nc.vector.tensor_copy(item_eq[:], flags[:, 0, :]))
            cur, width = 0, 1
            while width < EXTRA:
                link(nc.vector.tensor_copy(flags[:, 1 - cur, 0:width], flags[:, cur, 0:width]))
                link(tt(flags[:, 1 - cur, width:EXTRA], flags[:, cur, width:EXTRA], flags[:, cur, 0:EXTRA - width],
                        ALU.add))
                cur, width = 1 - cur, 2 * width
            link(nc.vector.tensor_copy(item_f[:, 1:2], flags[:, cur, EXTRA - 1:EXTRA]))
            link(tt(item_eq[:], item_eq[:], flags[:, cur, :], ALU.mult))
            link(ts(item_eq[:], item_eq[:], part_no, None, ALU.is_equal))
            link(tt(item_eq[:], item_eq[:], cs[:, C_ITEMS:C_ITEMS + EXTRA],
                    ALU.mult))
            link(nc.vector.tensor_reduce(item_f[:, 0:1], item_eq[:], AX.X, ALU.add))
            nc.vector.tensor_copy(item_col[:], item_f[:]).then_inc(item_done, 2)
            for k in range(1, KB, 2):
                ve.wait_ge(gath_mm, k + 1)
                nc.vector.tensor_copy(xg[0][:, k, :], S[1][:]).then_inc(gath_dve, 1)
            with ve.Fori(0, PAIRS // 8) as i:
                for jj in range(8):
                    if jj % 4 == 0:
                        make_onehot((jj // 4 + 1) % 2, bass.ds(i * 16 + (8 * (jj // 4) + 8), PER_GROUP))
                    ve.wait_ge(h_silu, i * 8 + (jj + 1))
                    tt(hh[:], h1[:], S[2][:, FF:2 * FF], ALU.mult).then_inc(h_done, 1)
                    ve.wait_ge(scatT_mm, i * 8 + (jj + 1))
                    for c in range(2):
                        r = slice(c * SLOTS, (c + 1) * SLOTS)
                        nc.vector.tensor_copy(slot_gate[r, :], S[0][r, SEQ + c:SEQ + c + 1]).then_inc(gate_cp, 1)
                    nc.vector.tensor_copy(scatT[:], S[0][:, 0:SEQ]).then_inc(scatT_cp, 1)
                    ve.wait_ge(gath_mm, i * 16 + (KB + 2 * jj + 2))
                    nc.vector.tensor_copy(xg[(jj // 4 + 1) % 2][:, 2 * (jj % 4) + 1, :], S[0][:]).then_inc(gath_dve, 1)
                    for c in range(2):
                        ve.wait_ge(yh_done, i * 16 + (2 * jj + c + 1))
                        stt(yl[:, c * 512:(c + 1) * 512], (S[3], S[1])[c][:], slot_gate[:, 0:1],
                            yh[:, c * 512:(c + 1) * 512].bitcast(F32), ALU.mult, ALU.subtract).then_inc(yl_done, 1)
            ve.wait_ge(items_ld, 32)
            n_items = ve.value_load(items[0:1, P:P + 1], min_val=0, max_val=EXTRA)
            with ve.If(n_items > 0):
                with ve.Fori(0, n_items) as i:
                    item = ve.value_load(items[0:1, bass.ds(i, 1)], min_val=0, max_val=EXTRA - 1)
                    ve.wait_ge(o_scat, i)
                    for t in range(TB):
                        ts(place_off[:, t, :], place_e[:, t, bass.ds((item % PAIRS) * 2, 2)],
                           cs[:, bass.ds(item + C_ROFF, 1)], None, ALU.subtract).then_inc(o_hot, 1)
                    ve.wait_ge(o_hot, i * 4 + 2)
                    for t in range(TB):
                        tt(onehot[:, 0, t, 0:2, :], slot_no.unsqueeze(1).to_broadcast([P, 2, SLOTS]),
                           place_off[:, t, :].unsqueeze(2).to_broadcast([P, 2, SLOTS]), ALU.is_equal
                           ).then_inc(o_hot, 1)
                    ve.wait_ge(o_gath, i + 1)
                    for c in range(2):
                        nc.vector.tensor_copy(xg[0][:, 4 * c:4 * c + 4, 0:P],
                                              S[c][:].rearrange("p (k s) -> p k s", k=4)).then_inc(o_xg, 1)
                    ve.wait_ge(o_h1, i + 1)
                    tt(hh[:], h1[:], S[2][:, FF:2 * FF], ALU.mult).then_inc(o_h, 1)
                    ve.wait_ge(o_T, i + 1)
                    for c in range(2):
                        r = slice(c * SLOTS, (c + 1) * SLOTS)
                        nc.vector.tensor_copy(slot_gate[r, :], S[0][r, SEQ + c:SEQ + c + 1]).then_inc(o_Tcp, 1)
                    nc.vector.tensor_copy(scatT[:], S[0][:, 0:SEQ]).then_inc(o_Tcp, 1)
                    nc.vector.tensor_copy(hT[:], S[2][:, 0:2 * P].rearrange("p (k s) -> p k s", k=2)
                                          ).then_inc(o_Tcp, 1)
                    ve.wait_ge(o_y, i * 4 + 2)
                    for c in range(2):
                        stt(yl[:, c * 512:(c + 1) * 512], (S[3], S[1])[c][:], slot_gate[:, 0:1],
                            yh[:, c * 512:(c + 1) * 512].bitcast(F32), ALU.mult, ALU.subtract).then_inc(o_y, 1)
            ve.wait_ge(moe_mm, 1)
            for t in range(TB):
                for c in range(2):
                    half = xres[:, t, c * 512:(c + 1) * 512]
                    link(stt(half, half, ALPHA, W[2 * t + c][:], ALU.mult, ALU.add))
            layer_norm(2, ln3)

        @block.tensor
        def _(pe):
            mm = nc.tensor.matmul

            def bank_free(n):
                if n >= 4:
                    pe.wait_ge(dve_took if OUT_KIND[n - 4] in BY_DVE else act_took, taken_count(n - 4))

            def chunk_here(q):
                if q < N_SPLIT:
                    pe.wait_ge(w_rest_dve if rest_by_dve(q) else w_rest_pool, rest_count(q))
                else:
                    pe.wait_ge(dense_ld[q // 2 % RAW_TILES], 16 * (q // 2 // RAW_TILES + 1))

            def chunk(q, cols):
                return [w.rearrange("p (k c) -> p k c", c=cols) for w in (w_hi[:, q % ROUNDED, :], w_lo[:, q % 6, :])]

            def feature_major(kind, k, act_r, chunks=1, ready=None):
                n = out_index(kind, k)
                bank_free(n)
                for c in range(chunks):
                    q = CHUNK0[kind] + k * chunks + c
                    chunk_here(q)
                    w_h, w_l = chunk(q, P)
                    for b in range(KB):
                        kb = c * KB + b
                        if ready is not None and kb % 4 == 0:
                            pe.wait_ge(ready, kb // 4 + 1)
                        for j, (w, a) in enumerate(((w_h, act_r[0]), (w_h, act_r[1]), (w_l, act_r[0]))):
                            last = mm(S[n % 4][:, 0:SEQ], w[:, b, :], a[:, kb, :], start=(kb + j == 0),
                                      stop=(kb == chunks * KB - 1 and j == 2))
                last.then_inc(proj_ready, 1)

            def token_major(kind, k, act_r):
                n = out_index(kind, k)
                q, t = CHUNK0[kind] + k // TB * 2, k % TB
                bank_free(n)
                if t == 0:
                    chunk_here(q)
                    chunk_here(q + 1)
                for kb in range(KB):
                    rows, cols = slice(t * P, (t + 1) * P), kb % 4
                    if q < N_SPLIT:
                        w_h, w_l = chunk(q + kb // 4, SEQ)
                        parts = ((act_r[0], w_h), (act_r[1], w_h), (act_r[0], w_l))
                    else:
                        parts = ((act_r, raw[:, (q + kb // 4) % 6, :].rearrange("p (k c) -> p k c", c=SEQ)),)
                    for j, (a, w) in enumerate(parts):
                        last = mm(S[n % 4][:, 0:SEQ], a[:, kb, rows], w[:, cols, :], start=(kb + j == 0),
                                  stop=(kb == KB - 1 and j == len(parts) - 1))
                last.then_inc(proj_ready, 1)

            for b in range(NXB):
                feature_major("xbc", b, xT_r, ready=x_rest if b == 0 else None)
                if b == 1:
                    pe.wait_ge(small_in, 32)
                    mm(W[0][0:DIFF_HEADS, 0:384], cs[0:BUCKETS + 1, C_RB:C_RB + 8],
                       cs[0:BUCKETS + 1, C_HOT:C_HOT + 384], start=True, stop=True).then_inc(rel_mm, 1)
            pe.wait_ge(x_rest, 3)
            for kb in range(KB):
                for j, (w, a) in enumerate(((0, 0), (0, 1), (1, 0))):
                    last = mm(W[1][0:SSD_HEADS, 0:SEQ], wdt_r[w][:, kb, :], xT_r[a][:, kb, :], start=(kb + j == 0),
                              stop=(kb == KB - 1 and j == 2))
            last.then_inc(dt_mm, 1)
            for h in range(DIFF_HEADS):
                feature_major("q", h, xT_r)
                if h == 0:
                    pe.wait_ge(dtT_cp, 1)
                    for t in range(TB):
                        last = nc.tensor.transpose(W[1][:, SEQ + t * SSD_HEADS:SEQ + (t + 1) * SSD_HEADS],
                                                   dtT[0:SSD_HEADS, t * P:(t + 1) * P], ident[0:SSD_HEADS, 0:SSD_HEADS])
                    last.then_inc(dtT_mm, 1)
            for h in range(DIFF_HEADS):
                feature_major("k", h, xT_r)
            pe.wait_ge(rel_ld, 16)
            pe.wait_ge(rel_cp, 1)
            pe.wait_ge(a_done, 1)
            for k in range(4):
                mm(W[k][:], flip, rel_flipped[:, 2 * k:2 * k + 2, :], start=True, stop=True).then_inc(flip_mm, 1)
            pe.wait_ge(flip_cp, 4)
            mm(W[0][:, 0:SSD_HEADS], strict, a_v[:, 0, :], start=True, stop=True).then_inc(end_mm, 1)
            pe.wait_ge(conv_silu, NXB)
            for g in range(GROUPS):
                if g == 3:
                    pe.wait_ge(small_exp, 4)
                bank = W[(1 + g) % 4]
                bT, cT = xc[:, XS_BLOCKS + g, :], xc[:, XS_BLOCKS + GROUPS + g, :]
                mm(bank[:, 0:SEQ], bT[:, 0:P], cT, start=True, stop=True)
                mm(bank[:, SEQ:384], bT[:, P:SEQ], cT[:, P:SEQ], start=True, stop=True).then_inc(cb_mm, 1)
            for k in range(8):
                t, quad = k // 4, k % 4
                if k < 4:
                    pe.wait_ge(cb_cp, 2 * k + 2)
                else:
                    pe.wait_ge(xs_cp, k - 3)
                for j in range(4):
                    last = nc.tensor.transpose(W[(1 + k) % 4][:, j * P:(j + 1) * P],
                                               xc[:, 4 * quad + j, t * P:(t + 1) * P], ident)
                last.then_inc(xs_mm, 1)
            for k in range(8):
                token_major("v", k, xT_r)

            for i in range(8):
                for t in range(TB):
                    pe.wait_ge(gdec_done, 2 * i + t + 1)
                    if i == 0:
                        pe.wait_ge(xs_cp, 8)
                    else:
                        pe.wait_ge(y_done, i)
                    for h in range(4):
                        last = mm(W[2 + t][:, h * P:(h + 1) * P], gdec[:, t, h, :], tri, start=True, stop=True)
                    last.then_inc(seg_mm, 1)
                if i >= 1:
                    pe.wait_ge(attnT_cp, i)
                    pe.wait_ge(av_cp, i)
                if i == 0:
                    pe.wait_ge(act_took, taken_count(out_index("k", 7)))
                for m in range(2):
                    r = slice(HEAD * m, HEAD * m + HEAD)
                    mm(W[m][:, 0:P], qT[r, i, 0:P], kT[r, i, 0:P], start=True, stop=True)
                    last = mm(W[m][:, P:384], qT[r, i, P:SEQ], kT[r, i, :], start=True, stop=True)
                last.then_inc(logit_mm, 1)
                kind = "z" if i < 4 else "gate"
                k0 = 4 * (i % 4)
                feature_major(kind, k0, xT_r)
                feature_major(kind, k0 + 1, xT_r)
                pe.wait_ge(masked_dec, 2 * i + 2)
                for j in range(2):
                    for t in range(TB):
                        for h in range(2):
                            c = 256 * i + P * j + HEAD * h
                            last = mm(W[2][HEAD * h:HEAD * h + HEAD, j * SEQ + t * P:j * SEQ + (t + 1) * P],
                                      xsdt[:, t, c:c + HEAD], dec[:, t, 2 * j + h, :], start=True, stop=True)
                last.then_inc(y_mm, 1)
                pe.wait_ge(xend_done, i + 1)
                for j in range(2):
                    mm(W[3][:, j * P:(j + 1) * P], xend[:, 2 * j:2 * j + 2, :].rearrange("p h e -> p (h e)"),
                       cbm[:, i // 2, P:2 * P], start=True, stop=True)
                for j in range(2):
                    for h in range(2):
                        a_h = a_v[:, 1, 4 * i + 2 * j + h:4 * i + 2 * j + h + 1].to_broadcast([P, HEAD])
                        last = mm(W[3][HEAD * h:HEAD * h + HEAD, SEQ + j * P:SEQ + (j + 1) * P], a_h, tri,
                                  start=True, stop=True)
                last.then_inc(off_mm, 1)
                pe.wait_ge(attn_done, i + 1)
                for j in range(3):
                    last = nc.tensor.transpose(W[0][:, j * P:(j + 1) * P], attn[:, j * P:(j + 1) * P], ident)
                last.then_inc(attnT_mm, 1)
                feature_major(kind, k0 + 2, xT_r)
                feature_major(kind, k0 + 3, xT_r)
                if i == 0:
                    pe.wait_ge(act_took, taken_count(out_index("v", 7)))
                pe.wait_ge(attnT_cp, i + 1)
                mm(W[1][:, 0:SEQ], v[:, 0, i * P:(i + 1) * P], attnT[:, 0:SEQ], start=True, stop=False,
                   skip_group_check=True)
                mm(W[1][:, P:SEQ], v[:, 1, i * P:(i + 1) * P], attnT[:, SEQ:384], start=False, stop=True,
                   skip_group_check=True).then_inc(av_mm, 1)

            def sums_of_squares(k):
                pe.wait_ge(squared, k + 1)
                if k < GROUPS:
                    if k == 0:
                        pe.wait_ge(attnT_cp, 8)
                        pe.wait_ge(av_cp, 8)
                        pe.wait_ge(y_done, 8)
                    last = mm(W[k][:], ones, sqd[:, 2 * k:2 * k + 2, :], start=True, stop=True)
                else:
                    g = k - GROUPS
                    pe.wait_ge(rms_rcp, g + 1)
                    for j in range(4):
                        last = mm(W[g][:, 0:SEQ], ones, z[:, 4 * g + j, :], start=(j == 0), stop=(j == 3))
                last.then_inc(ssq_mm, 1)

            pe.wait_ge(mem_rest, 2)
            for k in range(8):
                feature_major("ck", k, memT_r)
                if k == 3:
                    for g in range(GROUPS):
                        sums_of_squares(g)
            for g in range(GROUPS):
                sums_of_squares(GROUPS + g)
            for k in range(4):
                token_major("cv", k, memT_r)
            pe.wait_ge(oT_rest, 2)
            for k in range(KB):
                feature_major("diff", k, oT_r)
            for k in range(KB):
                feature_major("ssd", k, yT_r, chunks=2, ready=yT_rest if k == 0 else None)
            pe.wait_ge(mixT_rest, 4)
            for k in range(8):
                token_major("mix", k, mixT_r)
            for k in range(4):
                token_major("cvb", k, memT_r)

            def turn(which):
                for t in range(TB):
                    pe.wait_ge(ln_done, TB * which + t + 1)
                    for c in range(2):
                        for j in range(4):
                            last = nc.tensor.transpose(W[2 * t + c][:, j * P:(j + 1) * P],
                                                       xres[:, t, (4 * c + j) * P:(4 * c + j + 1) * P], ident)
                        last.then_inc(xt_mm, 1)

            pe.wait_ge(rms_rcp, 2 * GROUPS)
            turn(0)
            pe.wait_ge(xt_rest, 4)
            for k in range(KB):
                feature_major("cq", k, x1T_r)
            for h in range(MEM_HEADS):
                pe.wait_ge(act_took, taken_count(out_index("cq", 2 * h + 1)))
                for t in range(TB):
                    for c in range(2):
                        last = mm(W[h][:, t * SEQ:(t + 1) * SEQ], qcT[:, 2 * h + c, t * P:(t + 1) * P],
                                  kcT[:, 2 * h + c, :], start=(c == 0), stop=(c == 1))
                last.then_inc(clog_mm, 1)
            for h in range(MEM_HEADS):
                pe.wait_ge(cprob_done, TB * (h + 1))
                for kb in range(2):
                    for t in range(TB):
                        last = nc.tensor.transpose(W[h][:, kb * SEQ + t * P:kb * SEQ + (t + 1) * P],
                                                   pc[:, h, t, kb * P:(kb + 1) * P], ident)
                last.then_inc(cpT_mm, 1)
            for h in range(MEM_HEADS):
                pe.wait_ge(cpT_cp, h + 1)
                for c in range(2):
                    for kb in range(2):
                        last = mm(W[h][:, c * SEQ:(c + 1) * SEQ], vc[:, kb, (2 * h + c) * P:(2 * h + c + 1) * P],
                                  pcT[:, h, kb, :], start=(kb == 0), stop=(kb == 1))
                last.then_inc(cav_mm, 1)
            pe.wait_ge(cav_rest, MEM_HEADS)
            for k in range(8):
                token_major("co", k, ocT_r)
            turn(1)
            pe.wait_ge(xt_cp, 8)
            for t in range(TB):
                for kb in range(KB):
                    last = mm(W[0][:, t * EXPERTS:(t + 1) * EXPERTS], x2T[:, kb, t * P:(t + 1) * P], w_router[:, kb, :],
                              start=(kb == 0), stop=(kb == KB - 1))
            last.then_inc(score_mm, 1)
            for k in range(4):
                token_major("sh", k, x2T)
            pe.wait_ge(sel_done, 1)
            mm(W[2][:, 0:EXPERTS], tri, sel[:, 0, :], start=True, stop=True)
            mm(W[2][:, EXPERTS:2 * EXPERTS], ones, sel[:, 0, :], start=True, stop=False)
            mm(W[2][:, EXPERTS:2 * EXPERTS], tri, sel[:, 1, :], start=False, stop=True)
            mm(W[2][:, 2 * EXPERTS:3 * EXPERTS], ones, sel[:, 0, :], start=True, stop=False)
            mm(W[2][:, 2 * EXPERTS:3 * EXPERTS], ones, sel[:, 1, :], start=False, stop=True).then_inc(rank_mm, 1)
            for t in range(TB):
                pe.wait_ge(sh_done, t + 1)
                for c in range(2):
                    last = nc.tensor.transpose(W[1][:, t * SEQ + c * P:t * SEQ + (c + 1) * P],
                                               hh[:, c * P:(c + 1) * P], ident)
                last.then_inc(hsT_mm, 1)

            def gather(block, bank, buf, done):
                parts = [(x, t) for t in range(TB) for x in (x2h, x2l)]
                for k, (x, t) in enumerate(parts):
                    last = mm(bank[:], x[:, t, block * P:(block + 1) * P],
                              onehot[:, buf, t].rearrange("p e s -> p (e s)"),
                              start=(k == 0), stop=(k == len(parts) - 1))
                last.then_inc(done, 1)

            pe.wait_ge(onehot_done, 2)
            pe.wait_ge(split_l, 2)
            pe.wait_ge(sh_done, 2)
            for k in range(KB):
                if k >= 2:
                    pe.wait_ge((gath_act, gath_dve)[k % 2], k // 2)
                gather(k, S[k % 2], 0, gath_mm)
            pe.wait_ge(hsT_cp, TB + 1)
            pe.wait_ge(wsd_ld, 16)
            pe.wait_ge(place_done, 2)

            def shared_down(kb, last_one):
                for t in range(TB):
                    for c in range(2):
                        last = mm(W[2 * t + c][:], hsT[:, kb, t * P:(t + 1) * P], wsd[:, kb, c * 512:(c + 1) * 512],
                                  start=not last_one, stop=last_one, skip_group_check=True)
                return last

            shared_down(0, False)

            def scatter(done=None):
                for t in range(TB):
                    for c in range(2):
                        for y in (yh, yl):
                            last = mm(W[2 * t + c][:], scatT[:, t * P:(t + 1) * P], y[:, c * 512:(c + 1) * 512],
                                      start=False, stop=False, skip_group_check=True)
                if done is not None:
                    last.then_inc(done, 1)

            def gate_up(x, col, slots, done):
                for kb in range(KB):
                    for e in range(2):
                        last = mm(S[2][e * SLOTS:(e + 1) * SLOTS, :], x[:, kb, col + e * SLOTS:col + (e + 1) * SLOTS],
                                  ring[:, slots[e], kb * 512:(kb + 1) * 512], start=(kb == 0), stop=(kb == KB - 1))
                last.then_inc(done, 1)

            def turn_onehot(buf, col, gates, done):
                for t in range(TB):
                    mm(S[0][:, t * P:(t + 1) * P], onehot[:, buf, t].rearrange("p e s -> p (e s)")[:, col:col + P],
                       ident_r[:], start=True, stop=True)
                for t in range(TB):
                    last = mm(S[0][:, SEQ:SEQ + 2],
                              onehot[:, buf, t].rearrange("p e s -> p (e s)")[:, col:col + P].bitcast(F32),
                              gates(t), start=(t == 0), stop=(t == TB - 1))
                last.then_inc(done, 1)

            def turn_h(done):
                for c in range(2):
                    last = nc.tensor.transpose(S[2][:, c * P:(c + 1) * P], hh[:, c * P:(c + 1) * P], ident)
                last.then_inc(done, 1)

            def down(c, slot, done):
                for kb in range(2):
                    for e in range(2):
                        o = (e * 2 + kb) * D + c * 512
                        last = mm((S[3], S[1])[c][e * SLOTS:(e + 1) * SLOTS, :], hT[:, kb, e * SLOTS:(e + 1) * SLOTS],
                                  ring[:, slot, o:o + 512], start=(kb == 0), stop=(kb == 1))
                if done is not None:
                    last.then_inc(done, 1)

            pe.wait_ge(gath_act, KB // 2)
            pe.wait_ge(gath_dve, KB // 2)
            with pe.Fori(0, PAIRS // 8) as i:
                for jj in range(8):
                    buf, col = jj // 4, (jj % 4) * P
                    if jj % 4 == 0:
                        pe.wait_ge(gath_act, i * 8 + (KB // 2 + jj))
                        pe.wait_ge(gath_dve, i * 8 + (KB // 2 + jj))
                    for kind in range(2):
                        pe.wait_ge(expert_ld[expert_tile(jj, kind)], expert_count(i, jj, kind))
                    gate_up(xg[buf], col, (expert_tile(jj, 0), expert_tile(jj, 1)), gu_mm)
                    if jj >= 1:
                        pe.wait_ge(yl_done, i * 16 + 2 * jj)
                        scatter()
                    pe.wait_ge(gath_dve, i * 8 + (KB // 2 + jj))
                    turn_onehot(buf, col, lambda t: gates_e[:, t, bass.ds(i * 16 + 2 * jj, 2)], scatT_mm)
                    pe.wait_ge(onehot_done, i * 4 + (2 * (jj // 4) + 4))
                    pe.wait_ge(scatT_cp, i * 8 + (jj + 1))
                    gather(2 * (jj % 4), S[0], (buf + 1) % 2, gath_mm)
                    pe.wait_ge(h_done, i * 8 + (jj + 1))
                    turn_h(hT_mm)
                    pe.wait_ge(gath_act, i * 8 + (KB // 2 + jj + 1))
                    gather(2 * (jj % 4) + 1, S[0], (buf + 1) % 2, gath_mm)
                    pe.wait_ge(hT_cp, i * 8 + (jj + 1))
                    pe.wait_ge(expert_ld[expert_tile(jj, 2)], expert_count(i, jj, 2))
                    down(0, expert_tile(jj, 2), down_mm)
                    down(1, expert_tile(jj, 2), down_mm)
                pe.wait_ge(yl_done, i * 16 + 16)
                scatter()
            pe.wait_ge(gath_dve, KB // 2 + PAIRS)
            pe.wait_ge(items_ld, 32)
            n_items = pe.value_load(items[0:1, P:P + 1], min_val=0, max_val=EXTRA)
            with pe.If(n_items > 0):
                with pe.Fori(0, n_items) as i:
                    item = pe.value_load(items[0:1, bass.ds(i, 1)], min_val=0, max_val=EXTRA - 1)
                    pe.wait_ge(o_hot, i * 4 + 4)
                    for k in range(KB):
                        parts = [(x, t) for t in range(TB) for x in (x2h, x2l)]
                        for n, (x, t) in enumerate(parts):
                            last = mm(S[k // 4][:, (k % 4) * P:(k % 4 + 1) * P], x[:, t, k * P:(k + 1) * P],
                                      onehot[:, 0, t, 0:2, :].rearrange("p e s -> p (e s)"),
                                      start=(n == 0), stop=(n == 3))
                    last.then_inc(o_gath, 1)
                    pe.wait_ge(o_xg, i * 2 + 2)
                    pe.wait_ge(extra_ld, i * 48 + 48)
                    gate_up(xg[0], 0, (0, 1), o_gu)
                    pe.wait_ge(o_h, i + 1)
                    for t in range(TB):
                        mm(S[0][:, t * P:(t + 1) * P], onehot[:, 0, t, 0:2, :].rearrange("p e s -> p (e s)"),
                           ident_r[:], start=True, stop=True)
                    for t in range(TB):
                        mm(S[0][:, SEQ:SEQ + 2], onehot[:, 0, t, 0:2, :].rearrange("p e s -> p (e s)").bitcast(F32),
                           gates_e[:, t, bass.ds((item % PAIRS) * 2, 2)], start=(t == 0), stop=(t == TB - 1))
                    turn_h(o_T)
                    pe.wait_ge(o_Tcp, i * 4 + 4)
                    down(0, 2, None)
                    down(1, 2, o_down)
                    pe.wait_ge(o_y, i * 4 + 4)
                    scatter(o_scat)
            shared_down(1, True).then_inc(moe_mm, 1)


def constants():
    c = np.zeros((P, C_CONVW), np.float32)
    p, f = np.arange(P)[:, None], np.arange(P)[None, :]
    c[:, C_ID:C_ID + P] = p == f
    c[:, C_TRI:C_TRI + P] = p <= f
    c[:, C_STRICT:C_STRICT + P] = p > f
    c[:, C_ONES:C_ONES + P] = 1.0
    c[:, C_FLIP:C_FLIP + P] = p + f == P - 1
    c[:, C_IOTA:C_IOTA + P] = f + 1
    c[:, C_LOW:C_LOW + 64] = (np.arange(8)[None, :] < np.arange(8)[:, None]).reshape(-1)
    item = np.arange(EXTRA)
    c[:, C_ROFF:C_ROFF + EXTRA] = SLOTS * (item // PAIRS + 1)
    c[:, C_ITEMS:C_ITEMS + EXTRA] = item
    c[:, C_ITEM + 1] = np.arange(P) + 1
    dist = SEQ - 1 - np.arange(384)
    exact = BUCKETS // 2
    d = np.maximum(dist, 1).astype(np.float32)
    large = exact + (np.log(d / exact) / math.log(MAX_DIST / exact) * (BUCKETS - exact)).astype(np.int32)
    bucket = np.where(dist < exact, dist, np.minimum(large, BUCKETS - 1))
    for j in range(384):
        if dist[j] >= 0:
            c[bucket[j], C_HOT + j] = 1.0
        else:
            c[BUCKETS, C_HOT + j] = MASKED
    return c


def lay_out(inp):
    f = {k: np.asarray(a, dtype=np.float32) for k, a in inp.items()}

    def tiles(w, cols, kbs=KB):
        n = w.shape[1] // cols
        return w.reshape(kbs, P, n, cols).transpose(2, 1, 0, 3).reshape(n, P, kbs * cols)

    w_in = f["w_in"][0]

    def tokens(w):
        return tiles(w, 2 * P)

    def features(w, kbs=KB):
        c = tiles(w, P, kbs)
        return c.reshape(-1, 2 * KB // kbs, P, kbs * P).transpose(0, 2, 1, 3).reshape(-1, P, TILE // 2)

    w_cv = f["w_ckv"][0][:, D:]
    wdense = np.concatenate([
        features(w_in[:, O_XBC:O_DT]), features(w_in[:, O_Q:O_V]), tokens(w_in[:, O_V:O_G]),
        features(w_in[:, 0:INNER]), features(w_in[:, O_G:]), features(f["w_ckv"][0][:, 0:D]), tokens(w_cv[:, 0:512]),
        features(f["w_diff_br"][0]), features(f["w_ssd_br"][0], XS_BLOCKS), tokens(f["w_mix_out"][0]),
        tokens(w_cv[:, 512:]), features(f["w_cq"][0]), tokens(f["w_co"][0]), tokens(f["w_sh_gu"][0]),
    ], axis=0)
    gu = f["w_exp_gu"][0].reshape(PAIRS, 2, KB, P, 2 * FF).transpose(0, 1, 3, 2, 4).reshape(PAIRS, 2, P, TILE)
    dn = f["w_exp_down"][0].reshape(PAIRS, 2, 2, P, D).transpose(0, 3, 1, 2, 4).reshape(PAIRS, 1, P, TILE)
    experts = np.concatenate([gu, dn], axis=1).reshape(3 * PAIRS, P, TILE)
    small = np.concatenate([
        constants(),
        f["conv_w"][0].reshape(CONV, NXB, P).transpose(2, 1, 0).reshape(P, NXB * CONV),
        f["conv_b"][0].reshape(NXB, P).T,
        f["ssd_norm_g"][0].reshape(XS_BLOCKS, P).T,
        np.repeat(f["d_skip"][0], HEAD).reshape(XS_BLOCKS, P).T,
        np.repeat(f["subln_g"][0].reshape(P, 1), 8, axis=1),
        np.concatenate([f["rel_bias"], np.ones((1, 8), np.float32), np.zeros((P - BUCKETS - 1, 8), np.float32)]),
        w_in[:, O_DT:O_Q].reshape(KB, P, SSD_HEADS).transpose(1, 0, 2).reshape(P, -1),
        f["w_router"][0].reshape(KB, P, EXPERTS).transpose(1, 0, 2).reshape(P, -1),
    ], axis=1)
    rows = np.concatenate([f["dt_bias"][0], f["a_log"][0], f["lambda_q1"][0], f["lambda_k1"][0], f["lambda_q2"][0],
                           f["lambda_k2"][0], f["router_bias"][0]])
    lnp = np.stack([np.stack([f[f"ln{i}_g"][0], f[f"ln{i}_b"][0]]) for i in (1, 2, 3)])

    def turned(x):
        return x[0].T.reshape(KB, P, -1).transpose(1, 0, 2)

    return {
        "small": small, "rows": rows, "lnp": lnp, "xT": turned(f["x"]), "memT": turned(f["mem"]),
        "x_tok": f["x"][0].reshape(TB, P, D).transpose(1, 0, 2), "wdense": wdense, "wstream": experts,
        "wshd": f["w_sh_down"][0].reshape(2, P, D).transpose(1, 0, 2),
    }


def kernel(**inputs):
    import concourse.bacc as bacc
    from concourse.bass_utils import run_bass_kernel_spmd

    nc = bacc.Bacc("TRN2", target_bir_lowering=False, num_devices=1)
    arrays = {f"in_{k}": np.ascontiguousarray(a) for k, a in lay_out(inputs).items()}
    args = [nc.dram_tensor(k, a.shape, mybir.dt.from_np(a.dtype), kind="ExternalInput").ap() for k, a in arrays.items()]
    out = nc.dram_tensor("out_dram", (1, SEQ, D), F32, kind="ExternalOutput").ap()
    layer_kernel(nc, *args, out)
    r = run_bass_kernel_spmd(nc, [arrays], core_ids=[0])
    return r.results[0]["out_dram"]
```

```python
import math
from contextlib import ExitStack

import numpy as np

import concourse.bass as bass
from concourse import mybir

F32 = mybir.dt.float32
F32R = mybir.dt.float32r
I32 = mybir.dt.int32
ALU = mybir.AluOpType
ACT = mybir.ActivationFunctionType
AX = mybir.AxisListType

P = 128
SEQ = 256
TB = SEQ // P
D = 1024
KB = D // P
INNER = 2048
SSD_HEADS = 32
HEAD = 64
GROUPS = 4
STATE = 128
CONV = 4
XBC = INNER + 2 * GROUPS * STATE
NXB = XBC // P
XS_BLOCKS = INNER // P
DIFF_HEADS = 8
MEM_HEADS = 4
BUCKETS = 32
MAX_DIST = 128
EXPERTS = 64
PAIRS = EXPERTS // 2
EGROUPS = 8
TOP_GROUPS = 4
FF = 256
SLOTS = 64
CHUNKS = SEQ // SLOTS
EXTRA = (CHUNKS - 1) * PAIRS
PER_GROUP = 4
ROUND = 8
ROUTED_SCALE = 2.5
ALPHA = 2.0 ** 0.25
EPS = 1e-5
LAM_INIT = 0.8 - 0.6 * math.exp(0.0)
SUBLN_SCALE = 1.0 - LAM_INIT
MASKED = -1.0e30
TILE = 4096

O_XBC = INNER
O_DT = O_XBC + XBC
O_Q = O_DT + SSD_HEADS
O_K = O_Q + D
O_V = O_K + D
O_G = O_V + D

STREAM = [("xbc", NXB, 1), ("q", 8, 1), ("k", 8, 1), ("v", 8, 1), ("z", 16, 1), ("gate", 16, 1), ("ck", 8, 1),
          ("cv", 4, 1), ("diff", 8, 1), ("ssd", 8, 2), ("mix", 8, 1), ("cvb", 4, 1), ("cq", 8, 1), ("co", 8, 1),
          ("sh", 4, 1)]
TOKEN_MAJOR = {"v", "cv", "cvb", "mix", "co", "sh"}
BY_DVE = {"ssd", "diff", "mix", "co", "sh"}
OUT_KIND = [k for k, m, _ in STREAM for _ in range(m)]
OUT0, CHUNK0, DONE = {}, {}, []
for _k, _m, _c in STREAM:
    OUT0[_k], CHUNK0[_k] = sum(m for k, m, _ in STREAM[:len(OUT0)]), len(DONE)
    for _q in range(_m * _c):
        DONE.append(OUT0[_k] + (2 * (_q // 2) + 2 if _k in TOKEN_MAJOR else _q // _c + 1))
N_CHUNKS = len(DONE)
N_SPLIT = CHUNK0["sh"]
CHUNK = KB * P
N_PLAIN = 2
RAW_TILES = 3
ROUNDED = 4
RING = 8

C_ID, C_TRI, C_STRICT, C_ONES, C_IOTA = 0, 128, 256, 384, 512
C_LOW, C_ROFF, C_ITEM, C_ITEMS, C_FLIP, C_HOT = 640, 704, 800, 808, 904, 1032
C_RES = C_HOT + 384
C_CONVW = C_RES + P
C_CONVB = C_CONVW + NXB * CONV
C_SSDG = C_CONVB + NXB
C_DSKIP = C_SSDG + XS_BLOCKS
C_SUBLN = C_DSKIP + XS_BLOCKS
C_RB = C_SUBLN + 8
C_WDT = C_RB + 8
C_WR = C_WDT + KB * SSD_HEADS
C_LN2 = C_WR + KB * EXPERTS
N_SMALL = C_LN2 + 2 * KB
R_DTB, R_ALOG, R_LAM, R_RB = 0, 32, 64, 320
N_ROW = 384


def out_index(kind, k=0):
    return OUT0[kind] + k


def rest_by_dve(q):
    paired = DONE[q - q % 2] == DONE[q - q % 2 + 1]
    return q == N_PLAIN or q % 4 == 3 or (paired and q % 2 == 1)


def rest_count(q):
    return sum(rest_by_dve(c) == rest_by_dve(q) for c in range(N_PLAIN, q + 1))


def taken_count(n):
    by = OUT_KIND[n] in BY_DVE
    return sum((k in BY_DVE) == by for k in OUT_KIND[:n + 1])


def layer_kernel(nc, small, rows, lnp, xT_in, memT_in, x_in, wdense, wstream, wshd, out):
    ctx = ExitStack()
    with ctx:
        def sb(name, shape, offset, dt=F32):
            return nc.alloc_sbuf_tensor_at(name, shape, dt, offset=offset)

        def sem(name):
            return ctx.enter_context(nc.semaphore(name))

        KIB = 1024
        at = 16512
        cs = sb("cs", [P, N_SMALL], at)
        at += N_SMALL * 4
        row = sb("row", [P, N_ROW], at)
        at += N_ROW * 4

        def tiny(name, shape, dt=F32):
            nonlocal at
            t = sb(name, shape, at, dt)
            at += (int(np.prod(shape[1:])) * 4 + 31) // 32 * 32
            return t

        dt_v = tiny("dt_v", [P, TB, SSD_HEADS])
        a_v = tiny("a_v", [P, TB, SSD_HEADS])
        a_r = [tiny(f"a_{n}", [P, TB, SSD_HEADS], F32R) for n in ("hi", "lo")]
        strict_r = tiny("strict_r", [P, P], F32R)
        dt_t = [tiny(f"dt_t{i}", [P, TB, SSD_HEADS]) for i in range(4)]
        exp_alog = tiny("exp_alog", [P, SSD_HEADS])
        decay_end = tiny("decay_end", [P, SSD_HEADS])
        lam_d = tiny("lam_d", [P, 2])
        lam_e = tiny("lam_e", [P, 2])
        neg_lam = tiny("neg_lam", [P, 1])
        lam_tmp = tiny("lam_tmp", [P, 64])
        a_max = tiny("a_max", [P, 4])
        a_neg = tiny("a_neg", [P, 4])
        a_sum = tiny("a_sum", [P, 4])
        a_rcp = tiny("a_rcp", [P, 4])
        c_neg = tiny("c_neg", [P, MEM_HEADS, TB])
        c_sum = tiny("c_sum", [P, MEM_HEADS, TB])
        c_rcp = tiny("c_rcp", [P, MEM_HEADS, TB])
        bn = tiny("bn", [P, TB, 4, 6])
        neg_mean = tiny("neg_mean", [P, TB])
        half_sum = tiny("half_sum", [P, 2])
        half_square = tiny("half_square", [P, 2])
        half_std = tiny("half_std", [P, 1])
        mv = tiny("mv", [P, TB, 2])
        rvar = tiny("rvar", [P, TB])
        rstd = tiny("rstd", [P, TB])
        max8 = tiny("max8", [P, TB, EGROUPS, 8])
        gsc = tiny("gsc", [P, TB, EGROUPS])
        gmask = tiny("gmask", [P, TB, EGROUPS])
        goff = tiny("goff", [P, TB, EGROUPS])
        top8 = tiny("top8", [P, TB, 8])
        w_sum = tiny("w_sum", [P, TB])
        w_rcp = tiny("w_rcp", [P, TB])
        slot_gate = tiny("slot_gate", [P, 1])
        place_off = tiny("place_off", [P, TB, 2])
        pair_n = tiny("pair_n", [P, PAIRS])
        item_col = tiny("item_col", [P, 2], I32)
        item_f = tiny("item_f", [P, 2])
        items = tiny("items", [P, P + 1], I32)
        slot_of = tiny("slot_of", [P, TB, EXPERTS + PER_GROUP])
        gates_e = tiny("gates_e", [P, TB, EXPERTS])
        RING0 = 131040
        W0 = RING0 - 6176 - 88 * KIB
        assert at <= W0, (at, W0)
        A = W0
        G = A + 8 * KIB
        FR = G + 8 * KIB
        E = FR + 8 * KIB
        C = E + 16 * KIB
        Z = C + 16 * KIB
        H = Z + 16 * KIB
        L = H + 16 * KIB
        SL3 = RING0 + 3 * 16 * KIB
        SL4 = SL3 + 16 * KIB
        ring = sb("ring", [P, 6, TILE], RING0)
        raw = sb("raw", [P, RAW_TILES * 2, CHUNK], RING0)
        w_lo = sb("w_lo", [P, RAW_TILES * 2, CHUNK], RING0, F32R)
        w_hi = sb("w_hi", [P, ROUNDED, CHUNK], RING0 + 24 * KIB, F32R)
        MEM = RING0 + 40 * KIB
        XH = SL4 + 24 * KIB
        xT = sb("xT", [P, KB, SEQ], Z)
        xT_r = (sb("xT_hi", [P, KB, SEQ], XH, F32R), sb("xT_lo", [P, KB, SEQ], A, F32R))
        wdt_r = (sb("wdt_hi", [P, KB, SSD_HEADS], L, F32R), sb("wdt_lo", [P, KB, SSD_HEADS], L + KIB, F32R))
        dtT = sb("dtT", [P, SEQ], L + 2 * KIB)
        mixT = sb("mixT", [P, KB, SEQ], A)
        mixT_r = (sb("mixT_hi", [P, KB, SEQ], H, F32R), sb("mixT_lo", [P, KB, SEQ], A, F32R))
        rel = sb("rel", [P, DIFF_HEADS, SEQ], G)
        rel_flipped = sb("rel_flipped", [P, DIFF_HEADS, SEQ], H)
        ln1 = sb("ln1", [P, 2, D], Z + 8 * KIB)
        ln2 = sb("ln2", [P, 2, D], G)
        v = sb("v", [P, TB, D], FR)
        qT = sb("qT", [P, DIFF_HEADS, SEQ], E)
        kT = sb("kT", [P, DIFF_HEADS, SEQ], E + 8 * KIB)
        oT = qT
        oT_r = (sb("oT_hi", [P, DIFF_HEADS, SEQ], C, F32R), sb("oT_lo", [P, DIFF_HEADS, SEQ], E, F32R))
        xsdt = sb("xsdt", [P, TB, INNER], C)
        sqd = sb("sqd", [P, DIFF_HEADS, SEQ], C)
        xres = sb("xres", [P, TB, D], C + 8 * KIB)
        z = sb("z", [P, XS_BLOCKS, SEQ], Z)
        gt = sb("gt", [P, 2 * KB, SEQ], H)
        xc = sb("xc", [P, NXB, SEQ], SL4)
        yT_r = (sb("yT_hi", [P, XS_BLOCKS, SEQ], Z, F32R), sb("yT_lo", [P, XS_BLOCKS, SEQ], SL4, F32R))
        cbm = sb("cbm", [P, GROUPS, 3 * P], SL4 + XS_BLOCKS * KIB)
        memT = sb("memT", [P, KB, SEQ], MEM)
        memT_r = (sb("memT_hi", [P, KB, SEQ], G, F32R), sb("memT_lo", [P, KB, SEQ], MEM, F32R))
        lg = sb("lg", [P, 768], L)
        attn = sb("attn", [P, 384], L + 3072)
        attnT = sb("attnT", [P, 384], L + 4608)
        dec = sb("dec", [P, TB, 4, P], SL3)
        a_tri = [sb(f"a_tri_{n}", [P, TB, 4, P], SL3 + (4 + 7 * i) * KIB, F32R) for i, n in enumerate(("hi", "lo"))]
        bds = sb("bds", [P, 384], SL3)
        PADDED = SEQ + CONV - 1
        xpad = sb("xpad", [P, 4, PADDED], SL3 + 8 * KIB)
        acc = sb("acc", [P, 2, SEQ], SL3 + 8 * KIB + 4160)
        fac = sb("fac", [P, 2, P], SL3 + 8 * KIB)
        yo = sb("yo", [P, 2, P], SL3 + 9 * KIB)
        xend = sb("xend", [P, 4, HEAD], SL3 + 10 * KIB)
        rms = sb("rms", [P, 8, 512], SL3)
        kcT = sb("kcT", [P, KB, SEQ], E + 8 * KIB)
        vc = sb("vc", [P, TB, D], FR)
        x1T_r = (sb("x1T_hi", [P, KB, SEQ], A, F32R), sb("x1T_lo", [P, KB, SEQ], Z, F32R))
        qcT = sb("qcT", [P, KB, SEQ], Z + 8 * KIB)
        pc = sb("pc", [P, MEM_HEADS, TB, SEQ], H)
        pcT = sb("pcT", [P, MEM_HEADS, TB, SEQ], H + 8 * KIB)
        ocT_r = (sb("ocT_hi", [P, KB, SEQ], A, F32R), sb("ocT_lo", [P, KB, SEQ], Z, F32R))
        x2T = sb("x2T", [P, KB, SEQ], FR)
        R = H + 8 * KIB
        scores = sb("scores", [P, TB, EXPERTS], R)
        choice = sb("choice", [P, TB, EXPERTS], R + 512)
        masked = sb("masked", [P, TB, EXPERTS], R + 1024)
        sel = sb("sel", [P, TB, EXPERTS], R + 1536)
        scoresT = sb("scoresT", [P, SEQ], R + 2 * KIB)
        gcmp = sb("gcmp", [P, TB, EGROUPS, EGROUPS], R + 3 * KIB)
        geq = sb("geq", [P, TB, EGROUPS, EGROUPS], R + 3 * KIB + 512)
        flags = sb("flags", [P, 2, EXTRA], L + 4 * KIB)
        item_eq = sb("item_eq", [P, EXTRA], L + 5 * KIB)
        wsd = sb("wsd", [P, 2, D], G)
        x2h = sb("x2h", [P, TB, D], Z, F32R)
        x2l = sb("x2l", [P, TB, D], Z + 8 * KIB, F32R)
        onehot = sb("onehot", [P, 2, TB, PER_GROUP, SLOTS], A, F32R)
        yh = sb("yh", [P, D], FR, F32R)
        yl = sb("yl", [P, D], FR + 4 * KIB, F32R)
        zero_r = sb("zero_r", [P, P], A + 4 * KIB, F32R)
        scatT = sb("scatT", [P, SEQ], A + 4 * KIB + 512, F32R)
        ident_r = sb("ident_r", [P, P], A + 5 * KIB + 512, F32R)
        hT = sb("hT", [P, 2, P], A + 6 * KIB)
        xg = [sb(f"xg{b}", [P, KB, PER_GROUP * SLOTS], H + 8 * KIB * b) for b in range(2)]
        half_tile = [P, TILE // 2]
        place_e = sb("place_e", [P, TILE], E)
        place_m, place_c = sb("place_m", half_tile, MEM), sb("place_c", half_tile, C)
        place_w, place_x = sb("place_w", half_tile, RING0 + 32 * KIB), sb("place_x", half_tile, C + 8 * KIB)

        def halves(tile):
            return tile[:, 0:TILE // 2], tile[:, TILE // 2:TILE]

        places = [halves(ring[:, n, :]) for n in (3, 4, 5)] + [
            halves(place_e), (place_m[:], place_c[:]), halves(ring[:, 1, :]), (place_w[:], place_x[:]),
            halves(ring[:, 0, :])]
        ln3 = sb("ln3", [P, 2, D], H + 8 * KIB)
        normed = sb("normed", [P, TB, D], Z)
        unread = sb("unread", [P, 512], Z + 8 * KIB)
        hsT = sb("hsT", [P, 2, SEQ], L)
        h1 = sb("h1", [P, FF], L + 2 * KIB)
        hh = sb("hh", [P, FF], L + 3 * KIB)

        S = [ctx.enter_context(nc.psum_tensor(f"stream{i}", [P, 512], F32)) for i in range(4)]
        W = [ctx.enter_context(nc.psum_tensor(f"work{i}", [P, 512], F32)) for i in range(4)]

        ident = cs[:, C_ID:C_ID + P]
        tri = cs[:, C_TRI:C_TRI + P]
        strict = cs[:, C_STRICT:C_STRICT + P]
        flip = cs[:, C_FLIP:C_FLIP + P]
        ones = cs[:, C_ONES:C_ONES + P]
        alpha_ident = cs[:, C_RES:C_RES + P]
        slot_no = cs[:, C_IOTA:C_IOTA + SLOTS]
        part_no = cs[:, C_ITEM + 1:C_ITEM + 2]
        lower8 = cs[:, C_LOW:C_LOW + 64].rearrange("p (i j) -> p i j", i=8)
        conv_w = cs[:, C_CONVW:C_CONVW + NXB * CONV].rearrange("p (b j) -> p b j", j=CONV)
        conv_b = cs[:, C_CONVB:C_CONVB + NXB]
        ssd_g = cs[:, C_SSDG:C_SSDG + XS_BLOCKS]
        d_skip = cs[:, C_DSKIP:C_DSKIP + XS_BLOCKS]
        subln = cs[:, C_SUBLN:C_SUBLN + 1]
        w_dt = cs[:, C_WDT:C_WDT + KB * SSD_HEADS].rearrange("p (k h) -> p k h", k=KB)
        ln2_g, ln2_b = cs[:, C_LN2:C_LN2 + KB], cs[:, C_LN2 + KB:C_LN2 + 2 * KB]
        w_router = cs[:, C_WR:C_WR + KB * EXPERTS].rearrange("p (k e) -> p k e", k=KB)
        rel_scratch = nc.dram_tensor("rel_scratch", [DIFF_HEADS, 384], F32, kind="Internal").ap()

        conv_in = sem("conv_in")
        small_in = sem("small_in")
        xT_ld = [sem(f"xT_ld{i}") for i in range(2)]
        memT_ld = sem("memT_ld")
        rel_ld = sem("rel_ld")
        ln_ld = sem("ln_ld")
        xres_ld = sem("xres_ld")
        wsd_ld = sem("wsd_ld")
        items_ld = sem("items_ld")
        first_ld = sem("first_ld")
        dense_ld = [sem(f"dense_ld{i}") for i in range(RAW_TILES)]
        expert_ld = [[sem(f"expert_ld{i}_{h}") for h in range(2)] for i in range(RING)]
        extra_ld = sem("extra_ld")
        stored = sem("stored")
        proj_ready = sem("proj_ready")
        rel_mm = sem("rel_mm")
        flip_mm = sem("flip_mm")
        dt_mm = sem("dt_mm")
        end_mm = sem("end_mm")
        cb_mm = sem("cb_mm")
        xs_mm = sem("xs_mm")
        seg_mm = sem("seg_mm")
        logit_mm = sem("logit_mm")
        y_mm = sem("y_mm")
        off_mm = sem("off_mm")
        attnT_mm = sem("attnT_mm")
        av_mm = sem("av_mm")
        ssq_mm = sem("ssq_mm")
        xt_mm = sem("xt_mm")
        clog_mm = sem("clog_mm")
        cpT_mm = sem("cpT_mm")
        cav_mm = sem("cav_mm")
        score_mm = sem("score_mm")
        scoreT_mm = sem("scoreT_mm")
        hsT_mm = sem("hsT_mm")
        rank_mm = sem("rank_mm")
        gath_mm = sem("gath_mm")
        gu_half = sem("gu_half")
        gu_mm = sem("gu_mm")
        scatT_mm = sem("scatT_mm")
        hT_mm = sem("hT_mm")
        down_mm = sem("down_mm")
        moe_mm = sem("moe_mm")
        w_rounded = sem("w_rounded")
        x_rounded = sem("x_rounded")
        mem_rounded = sem("mem_rounded")
        oT_rounded = sem("oT_rounded")
        yT_rounded = sem("yT_rounded")
        mixT_rounded = sem("mixT_rounded")
        act_took = sem("act_took")
        conv_silu = sem("conv_silu")
        small_exp = sem("small_exp")
        flip_cp = sem("flip_cp")
        seg_exp = sem("seg_exp")
        prob_exp = sem("prob_exp")
        fac_exp = sem("fac_exp")
        attnT_cp = sem("attnT_cp")
        av_cp = sem("av_cp")
        z_silu = sem("z_silu")
        squared = sem("squared")
        gate_sig = sem("gate_sig")
        rms_sqrt = sem("rms_sqrt")
        ln_sqrt = sem("ln_sqrt")
        xt_cp = sem("xt_cp")
        cprob_exp = sem("cprob_exp")
        cpT_cp = sem("cpT_cp")
        cav_cp = sem("cav_cp")
        score_sig = sem("score_sig")
        x2T_act = sem("x2T_act")
        norm_act = sem("norm_act")
        sh_silu = sem("sh_silu")
        hsT_cp = sem("hsT_cp")
        split_h = sem("split_h")
        gath_act = sem("gath_act")
        h_silu = sem("h_silu")
        hT_cp = sem("hT_cp")
        yh_done = sem("yh_done")
        dve = sem("dve_chain")
        w_rest_dve = sem("w_rest_dve")
        w_rest_pool = sem("w_rest_pool")
        x_rest = sem("x_rest")
        mem_rest = sem("mem_rest")
        oT_rest = sem("oT_rest")
        yT_rest = sem("yT_rest")
        mixT_rest = sem("mixT_rest")
        xt_rest = sem("xt_rest")
        cav_rest = sem("cav_rest")
        dtT_cp = sem("dtT_cp")
        dve_took = sem("dve_took")
        pad_zero = sem("pad_zero")
        rel_cp = sem("rel_cp")
        conv_done = sem("conv_done")
        lam_dots = sem("lam_dots")
        dt_pre = sem("dt_pre")
        a_done = sem("a_done")
        a_split = sem("a_split")
        cb_cp = sem("cb_cp")
        xs_cp = sem("xs_cp")
        amax_done = sem("amax_done")
        masked_dec = sem("masked_dec")
        attn_done = sem("attn_done")
        y_done = sem("y_done")
        yz_done = sem("yz_done")
        rms_rcp = sem("rms_rcp")
        ssq_took = sem("ssq_took")
        yT_done = sem("yT_done")
        oT_done = sem("oT_done")
        mix_done = sem("mix_done")
        ln_var = sem("ln_var")
        ln_done = sem("ln_done")
        cmax_done = sem("cmax_done")
        cprob_done = sem("cprob_done")
        sh_done = sem("sh_done")
        xhat_done = sem("xhat_done")
        x2T_dve = sem("x2T_dve")
        sel_done = sem("sel_done")
        place_done = sem("place_done")
        onehot_done = sem("onehot_done")
        split_l = sem("split_l")
        gath_dve = sem("gath_dve")
        h_done = sem("h_done")
        scatT_cp = sem("scatT_cp")
        gate_cp = sem("gate_cp")
        yl_done = sem("yl_done")
        item_done = sem("item_done")
        gdec_done = sem("gdec_done")
        xend_done = sem("xend_done")
        norm_pool = sem("norm_pool")
        o_hot, o_gath, o_xg, o_gu, o_h1, o_h, o_T, o_Tcp, o_down, o_y, o_scat = (
            sem(n) for n in ("o_hot", "o_gath", "o_xg", "o_gu", "o_h1", "o_h", "o_T", "o_Tcp", "o_down", "o_y",
                             "o_scat"))

        block = ctx.enter_context(nc.Block())

        def two_blocks(bank):
            return bank[:].rearrange("p (b s) -> p b s", b=2)

        def expert_tile(jj, kind):
            return (3 * jj + kind) % RING

        def expert_count(i, jj, kind):
            return (i * (3 * ROUND // RING) + (3 * jj + kind) // RING + 1) * 16

        @block.sync
        def _(sp):
            def dense_tile(m):
                slot = m % RAW_TILES
                if m >= RAW_TILES:
                    sp.wait_ge(proj_ready, DONE[2 * (m - RAW_TILES) + 1])
                sp.dma_start(raw[:, 2 * slot:2 * slot + 2, :], wdense[m].rearrange("p (c w) -> p c w", c=2)
                             ).then_inc(dense_ld[slot], 16)

            def expert_half(place, x, half):
                cols = slice(half * (TILE // 2), (half + 1) * (TILE // 2))
                sp.dma_start(places[place][half], wstream[x][:, cols]).then_inc(expert_ld[place][half], 16)

            def expert_halves(place, x):
                expert_half(place, x, 0)
                expert_half(place, x, 1)

            for half in range(2):
                sp.dma_start(xT[:, 4 * half:4 * half + 4, :], xT_in[:, 4 * half:4 * half + 4, :]
                             ).then_inc(xT_ld[half], 16)
                sp.dma_start(raw[:, half, :], wdense[0][:, half * CHUNK:(half + 1) * CHUNK]
                             ).then_inc((first_ld, dense_ld[0])[half], 16)
            dense_tile(1)
            sp.dma_start(cs[:, C_CONVW:C_SSDG], small[:, C_CONVW:C_SSDG]).then_inc(conv_in, 16)
            dense_tile(2)
            sp.dma_start(cs[:, 0:C_CONVW], small[:, 0:C_CONVW]).then_inc(small_in, 16)
            sp.dma_start(cs[:, C_SSDG:N_SMALL], small[:, C_SSDG:N_SMALL]).then_inc(small_in, 16)
            sp.dma_start(row[:], rows.partition_broadcast(P)).then_inc(small_in, 16)
            for m in range(RAW_TILES, CHUNK0["cvb"] // 2):
                dense_tile(m)
                if m == 7:
                    sp.wait_ge(rel_cp, 1)
                    sp.dma_start(rel_scratch, bds[0:DIFF_HEADS, :]).then_inc(rel_ld, 16)
                if m == 8:
                    sp.wait_ge(rel_ld, 16)
                    sp.dma_start(rel_flipped[:],
                                 bass.AP(rel_scratch.tensor, 0, [[1, P], [384, DIFF_HEADS], [1, SEQ]])
                                 ).then_inc(rel_ld, 16)
                if m == 11:
                    sp.dma_start(memT[:], memT_in).then_inc(memT_ld, 16)
            for m in range(CHUNK0["cvb"] // 2, CHUNK0["co"] // 2 + RAW_TILES):
                dense_tile(m)
            sp.wait_ge(proj_ready, out_index("ssd", KB - 1) + 1)
            for x in range(3):
                expert_halves(x, x)
            sp.wait_ge(clog_mm, MEM_HEADS)
            expert_halves(3, 3)
            dense_tile(CHUNK0["co"] // 2 + RAW_TILES)
            sp.wait_ge(proj_ready, out_index("cvb", 3) + 1)
            expert_halves(4, 4)
            for m in range(CHUNK0["co"] // 2 + RAW_TILES + 1, N_CHUNKS // 2):
                dense_tile(m)
            sp.wait_ge(proj_ready, DONE[N_SPLIT - 1])
            expert_halves(5, 5)
            sp.wait_ge(split_l, 2)
            expert_halves(6, 6)
            sp.wait_ge(proj_ready, DONE[-1])
            expert_halves(7, 7)

            def refill(pair, place, x, tiles=3):
                for half in range(2):
                    sp.wait_ge((gu_half, gu_mm)[half], pair + 1)
                    for m in range(min(tiles, 2)):
                        expert_half((place + m) % RING, x + m, half)
                if tiles == 3:
                    sp.wait_ge(down_mm, pair * 2 + 2)
                    expert_halves((place + 2) % RING, x + 2)

            refilled = PAIRS - 1 - RING // 3
            with sp.Fori(0, refilled // ROUND) as k:
                for j in range(ROUND):
                    refill(k * ROUND + j, 3 * j % RING, k * (3 * ROUND) + (RING + 3 * j))
            for pair in range(refilled // ROUND * ROUND, refilled):
                refill(pair, 3 * pair % RING, RING + 3 * pair)
            refill(refilled, 3 * refilled % RING, RING + 3 * refilled, tiles=1)
            sp.wait_ge(items_ld, 32)
            n_items = sp.value_load(items[0:1, P:P + 1], min_val=0, max_val=EXTRA)
            sp.wait_ge(down_mm, 2 * PAIRS)
            with sp.If(n_items > 0):
                with sp.Fori(0, n_items) as i:
                    item = sp.value_load(items[0:1, bass.ds(i, 1)], min_val=0, max_val=EXTRA - 1)
                    sp.wait_ge(o_scat, i + 1)
                    for m in range(3):
                        sp.dma_start(ring[:, m, :], wstream[(item % PAIRS) * 3 + m]
                                     ).then_inc(extra_ld, 16)
            for t in range(TB):
                sp.wait_ge(ln_done, TB + 1 + t + 1)
                sp.dma_start(out[0, t * P:(t + 1) * P, :], normed[:, t, :]).then_inc(stored, 16)
            sp.wait_ge(stored, 16 * TB)

        @block.gpsimd
        def _(pool):
            split = [N_PLAIN]

            def rests(upto):
                while split[0] <= upto:
                    q = split[0]
                    if not rest_by_dve(q):
                        pool.wait_ge(w_rounded, q + 1 - N_PLAIN)
                        nc.gpsimd.tensor_tensor(w_lo[:, q % 6, :], raw[:, q % 6, :],
                                                w_hi[:, q % ROUNDED, :].bitcast(F32), ALU.subtract
                                                ).then_inc(w_rest_pool, 1)
                    split[0] += 1

            def decays(i):
                for t in range(TB):
                    if i == 0:
                        pool.wait_ge(a_split, 2)
                    else:
                        pool.wait_ge(seg_mm, 2 * (i - 1) + t + 1)
                    for dst, a in zip(a_tri, a_r):
                        nc.gpsimd.tensor_tensor(dst[:, t], tri.unsqueeze(1).to_broadcast([P, 4, P]),
                                                a[:, t, 4 * i:4 * i + 4].bitcast(F32).unsqueeze(2
                                                    ).to_broadcast([P, 4, P]), ALU.mult).then_inc(gdec_done, 1)

            def inputs_at_end(i):
                if i == 0:
                    pool.wait_ge(small_exp, 4)
                    pool.wait_ge(xs_cp, 8)
                else:
                    pool.wait_ge(off_mm, i)
                nc.gpsimd.tensor_tensor(xend[:], xsdt[:, 0, 256 * i:256 * i + 256].rearrange("p (h e) -> p h e", h=4),
                                        decay_end[:, 4 * i:4 * i + 4].unsqueeze(2).to_broadcast([P, 4, HEAD]),
                                        ALU.mult).then_inc(xend_done, 1)

            rests(CHUNK0["q"] + 7)
            pool.wait_ge(small_in, 48)
            decays(0)
            rests(CHUNK0["v"] + 3)
            inputs_at_end(0)
            rests(CHUNK0["z"] + 3)
            for i in range(1, XS_BLOCKS // 2):
                c0 = CHUNK0["z"] + 4 * i
                decays(i)
                rests(c0 + 1)
                inputs_at_end(i)
                rests(c0 + 3)
            rests(CHUNK0["ck"] + 1)
            for g in range(2):
                pool.wait_ge(mem_rounded, g + 1)
                nc.gpsimd.tensor_tensor(memT_r[1][:, 4 * g:4 * g + 4, :], memT[:, 4 * g:4 * g + 4, :],
                                        memT_r[0][:, 4 * g:4 * g + 4, :].bitcast(F32), ALU.subtract
                                        ).then_inc(mem_rest, 1)
            rests(CHUNK0["ck"] + 3)
            pool.wait_ge(y_mm, XS_BLOCKS // 2)
            pool.wait_ge(off_mm, XS_BLOCKS // 2)
            pool.wait_ge(xend_done, XS_BLOCKS // 2)
            pool.dma_start(xres[:], x_in).then_inc(xres_ld, 16)
            rests(CHUNK0["mix"] + 1)
            pool.wait_ge(proj_ready, out_index("ssd", KB - 1) + 1)
            pool.dma_start(ln1[:], lnp[0:1].rearrange("a b d -> (a b) d").partition_broadcast(P)).then_inc(ln_ld, 16)
            rests(CHUNK0["cq"] + 3)
            pool.wait_ge(proj_ready, out_index("cvb", 3) + 1)
            pool.dma_start(ln2[:], lnp[1:2].rearrange("a b d -> (a b) d").partition_broadcast(P)).then_inc(ln_ld, 16)
            rests(N_SPLIT - 1)
            pool.wait_ge(xhat_done, 2)
            pool.wait_ge(ln_ld, 32)
            pool.wait_ge(xt_mm, 8)
            nc.gpsimd.tensor_tensor(xres[:, 1, :], xres[:, 1, :], ln2[:, 0, :], ALU.mult).then_inc(norm_pool, 1)
            pool.wait_ge(norm_pool, 1)
            nc.gpsimd.tensor_tensor(xres[:, 1, :], xres[:, 1, :], ln2[:, 1, :], ALU.add).then_inc(norm_pool, 1)
            pool.wait_ge(norm_pool, 2)
            pool.wait_ge(ln_done, TB + 1)
            pool.dma_start(wsd[:], wshd).then_inc(wsd_ld, 16)
            pool.wait_ge(item_done, 2)
            pool.dma_start(items[0:1, 0:P], item_col[:, 0:1]).then_inc(items_ld, 16)
            pool.dma_start(items[0:1, P:P + 1], item_col[0:1, 1:2]).then_inc(items_ld, 16)
            pool.wait_ge(gu_mm, PAIRS)
            pool.dma_start(ln3[:], lnp[2:3].rearrange("a b d -> (a b) d").partition_broadcast(P)).then_inc(ln_ld, 16)

        @block.scalar
        def _(act):
            split = [N_PLAIN]

            def round_chunks(n):
                while split[0] < N_SPLIT and (split[0] < ROUNDED or DONE[split[0] - ROUNDED] <= n + 1):
                    q = split[0]
                    act.wait_ge(dense_ld[q // 2 % RAW_TILES], 16 * (q // 2 // RAW_TILES + 1))
                    if q >= ROUNDED:
                        act.wait_ge(proj_ready, DONE[q - ROUNDED])
                    nc.scalar.activation(w_hi[:, q % ROUNDED, :], raw[:, q % 6, :], ACT.Copy).then_inc(w_rounded, 1)
                    split[0] += 1

            def leave(kind, k, dst, scale=1.0, then_round=True):
                n = out_index(kind, k)
                act.wait_ge(proj_ready, n + 1)
                nc.scalar.activation(dst, S[n % 4][:, 0:SEQ], ACT.Copy, scale=scale).then_inc(act_took, 1)
                if then_round:
                    round_chunks(n)

            def leave_tokens(kind, k, dst, col0=0, then_round=True):
                c = col0 + k // TB * SEQ
                leave(kind, k, dst[:, k % TB, c:c + SEQ], then_round=then_round)

            for half in range(2):
                act.wait_ge(xT_ld[half], 16)
                nc.scalar.activation(xT_r[0][:, 4 * half:4 * half + 4, :], xT[:, 4 * half:4 * half + 4, :], ACT.Copy
                                     ).then_inc(x_rounded, 1)
            round_chunks(-1)

            def conv_act(b):
                act.wait_ge(conv_done, b + 1)
                nc.scalar.activation(xc[:, b, :], acc[:, b % 2, :], ACT.Silu, bias=conv_b[:, b:b + 1]
                                     ).then_inc(conv_silu, 1)

            act.wait_ge(pad_zero, 1)
            act.wait_ge(conv_in, 16)
            for b in range(NXB):
                if b >= 4:
                    act.wait_ge(conv_done, b - 3)
                leave("xbc", b, xpad[:, b % 4, CONV - 1:PADDED])
                if b >= 1:
                    conv_act(b - 1)
                if b == 8:
                    act.wait_ge(small_in, 48)
                    nc.scalar.activation(wdt_r[0][:], w_dt, ACT.Copy).then_inc(x_rounded, 1)
                    act.wait_ge(lam_dots, 2)
                    nc.scalar.activation(exp_alog[:], row[:, R_ALOG:R_ALOG + SSD_HEADS], ACT.Exp
                                         ).then_inc(small_exp, 1)
                    nc.scalar.activation(lam_e[:], lam_d[:], ACT.Exp).then_inc(small_exp, 1)
            conv_act(NXB - 1)
            for h in range(DIFF_HEADS):
                leave("q", h, qT[:, h, :], scale=HEAD ** -0.5)
                if h == 1:
                    act.wait_ge(dt_pre, 1)
                    nc.scalar.activation(dt_t[1][:], dt_t[1][:], ACT.Exp, scale=-1.0).then_inc(small_exp, 1)
            for h in range(DIFF_HEADS):
                leave("k", h, kT[:, h, :])
            for k in range(4):
                act.wait_ge(flip_mm, k + 1)
                nc.scalar.activation(rel[:, 2 * k:2 * k + 2, :], W[k][:].rearrange("p (h k) -> p h k", h=2), ACT.Copy
                                     ).then_inc(flip_cp, 1)
            act.wait_ge(end_mm, 1)
            nc.scalar.activation(decay_end[:], W[0][:, 0:SSD_HEADS], ACT.Exp).then_inc(small_exp, 1)
            for k in range(8):
                leave_tokens("v", k, v)

            for i in range(8):
                for t in range(TB):
                    act.wait_ge(seg_mm, 2 * i + t + 1)
                    if i >= 1:
                        act.wait_ge(y_mm, i)
                    nc.scalar.activation(dec[:, t], W[2 + t][:].rearrange("p (h l) -> p h l", h=4), ACT.Exp
                                         ).then_inc(seg_exp, 1)
                act.wait_ge(amax_done, i + 1)
                for c, (o, w) in enumerate(((0, P), (P, SEQ), (P + SEQ, P), (2 * P + SEQ, SEQ))):
                    nc.scalar.activation(lg[:, o:o + w], lg[:, o:o + w], ACT.Exp, bias=a_neg[:, c:c + 1],
                                         accum_out=a_sum[:, c:c + 1]).then_inc(prob_exp, 1)
                kind, dst = ("z", z) if i < 4 else ("gate", gt)
                k0 = 4 * (i % 4)
                for j in range(2):
                    leave(kind, k0 + j, dst[:, k0 + j, :])
                    if i == 7:
                        act.wait_ge(memT_ld, 16)
                        nc.scalar.activation(memT_r[0][:, 4 * j:4 * j + 4, :], memT[:, 4 * j:4 * j + 4, :], ACT.Copy
                                             ).then_inc(mem_rounded, 1)
                act.wait_ge(off_mm, i + 1)
                if i >= 1:
                    act.wait_ge(y_done, i)
                nc.scalar.activation(fac[:], W[3][:, SEQ:2 * SEQ].rearrange("p (b l) -> p b l", b=2), ACT.Exp
                                     ).then_inc(fac_exp, 1)
                act.wait_ge(attnT_mm, i + 1)
                if i >= 1:
                    act.wait_ge(av_mm, i)
                nc.scalar.activation(attnT[:], W[0][:, 0:384], ACT.Copy).then_inc(attnT_cp, 1)
                leave(kind, k0 + 2, dst[:, k0 + 2, :])
                leave(kind, k0 + 3, dst[:, k0 + 3, :], then_round=False)
                act.wait_ge(av_mm, i + 1)
                nc.scalar.activation(oT[:, i, :], W[1][:, 0:SEQ], ACT.Copy).then_inc(av_cp, 1)
                round_chunks(out_index(kind, k0 + 3))

            def squares_of_y(g):
                act.wait_ge(yz_done, g + 1)
                nc.scalar.activation(z[:, 4 * g:4 * g + 4, :], xc[:, 4 * g:4 * g + 4, :], ACT.Square
                                     ).then_inc(squared, 1)

            act.wait_ge(av_cp, DIFF_HEADS)
            for k in range(4):
                nc.scalar.activation(sqd[:, 2 * k:2 * k + 2, :], oT[:, 2 * k:2 * k + 2, :], ACT.Square
                                     ).then_inc(squared, 1)
            act.wait_ge(act_took, taken_count(out_index("z", 15)))
            for g in range(GROUPS):
                nc.scalar.activation(z[:, 4 * g:4 * g + 4, :], z[:, 4 * g:4 * g + 4, :], ACT.Silu).then_inc(z_silu, 1)
                leave("ck", g, kcT[:, g, :])
            for k in range(GROUPS):
                squares_of_y(k)
                leave("ck", GROUPS + k, kcT[:, GROUPS + k, :])

            def root(k):
                w = 512 if k < GROUPS else SEQ
                act.wait_ge(rms_rcp, k + 1)
                nc.scalar.activation(rms[:, k, 0:w], rms[:, k, 0:w], ACT.Sqrt).then_inc(rms_sqrt, 1)

            for k in range(GROUPS):
                root(k)
            for g in range(2):
                act.wait_ge(oT_done, 4 * g + 4)
                nc.scalar.activation(oT_r[0][:, 4 * g:4 * g + 4, :], oT[:, 4 * g:4 * g + 4, :], ACT.Copy
                                     ).then_inc(oT_rounded, 1)
            leave_tokens("cv", 0, vc)
            leave_tokens("cv", 1, vc)
            leave_tokens("cv", 2, vc)
            leave_tokens("cv", 3, vc)
            act.wait_ge(act_took, taken_count(out_index("gate", 15)))
            for k in range(GROUPS):
                root(GROUPS + k)
            for g in (2, 3, 0, 1):
                nc.scalar.activation(gt[:, 4 * g:4 * g + 4, :], gt[:, 4 * g:4 * g + 4, :], ACT.Sigmoid
                                     ).then_inc(gate_sig, 1)
                round_chunks(out_index("diff", (g + 2) % 4))
            for g in range(GROUPS):
                act.wait_ge(yT_done, 4 * g + 4)
                nc.scalar.activation(yT_r[0][:, 4 * g:4 * g + 4, :], xc[:, 4 * g:4 * g + 4, :], ACT.Copy
                                     ).then_inc(yT_rounded, 1)
                round_chunks(out_index("diff", 4 + g))
            for k in range(KB):
                act.wait_ge(mix_done, k + 1)
                nc.scalar.activation(mixT_r[0][:, k, :], mixT[:, k, :], ACT.Copy).then_inc(mixT_rounded, 1)
                round_chunks(out_index("ssd", k))
            for k in range(8):
                round_chunks(out_index("mix", k))
            def norm_sqrt(which):
                for t in range(TB):
                    act.wait_ge(ln_var, TB * which + t + 1)
                    nc.scalar.activation(rstd[:, t:t + 1], rvar[:, t:t + 1], ACT.Sqrt).then_inc(ln_sqrt, 1)

            def turned(dst, t):
                for k in (2 * t, 2 * t + 1):
                    act.wait_ge(xt_mm, k + 1)
                    nc.scalar.activation(dst[:, 4 * (k % 2):4 * (k % 2) + 4, k // 2 * P:(k // 2 + 1) * P],
                                         W[k][:].rearrange("p (b t) -> p b t", b=4), ACT.Copy).then_inc(xt_cp, 1)

            norm_sqrt(0)
            for k in range(3):
                leave_tokens("cvb", k, vc, 512)
            turned(x1T_r[0], 0)
            leave_tokens("cvb", 3, vc, 512, then_round=False)
            turned(x1T_r[0], 1)
            round_chunks(out_index("cvb", 3))
            for k in range(KB):
                leave("cq", k, qcT[:, k, :], scale=(D // MEM_HEADS) ** -0.5)
            for h in range(MEM_HEADS):
                act.wait_ge(cmax_done, h + 1)
                for t in range(TB):
                    nc.scalar.activation(pc[:, h, t, :], W[h][:, t * SEQ:(t + 1) * SEQ], ACT.Exp,
                                         bias=c_neg[:, h, t:t + 1], accum_out=c_sum[:, h, t:t + 1]
                                         ).then_inc(cprob_exp, 1)
            for h in range(MEM_HEADS):
                act.wait_ge(cpT_mm, h + 1)
                nc.scalar.activation(pcT[:, h], W[h][:].rearrange("p (k q) -> p k q", k=2), ACT.Copy
                                     ).then_inc(cpT_cp, 1)
            for h in range(MEM_HEADS):
                act.wait_ge(cav_mm, h + 1)
                nc.scalar.activation(ocT_r[0][:, 2 * h:2 * h + 2, :],
                                     W[h][:].rearrange("p (k q) -> p k q", k=2), ACT.Copy
                                     ).then_inc(cav_cp, 1)
            for k in range(8):
                round_chunks(out_index("co", k))
            norm_sqrt(1)
            for t in range(TB):
                act.wait_ge(xt_mm, 4 + 2 * t + 1)
                for k in range(4):
                    nc.scalar.activation(x2T[:, k, t * P:(t + 1) * P], W[2 * t][:, k * P:(k + 1) * P], ACT.Identity,
                                         scale=ln2_g[:, k:k + 1], bias=ln2_b[:, k:k + 1]).then_inc(x2T_act, 1)
            act.wait_ge(score_mm, 1)
            nc.scalar.activation(scoresT[0:EXPERTS, :], W[0][0:EXPERTS, 0:SEQ], ACT.Sigmoid).then_inc(score_sig, 1)
            for t in range(TB):
                if t == 0:
                    act.wait_ge(ln_done, TB + 1)
                else:
                    act.wait_ge(norm_pool, 2)
                nc.scalar.activation(x2h[:, t, :], xres[:, t, :], ACT.Copy).then_inc(split_h, 1)
            act.wait_ge(xt_mm, 8)
            for t in range(TB):
                n = out_index("sh", t)
                act.wait_ge(proj_ready, n + 1)
                if t:
                    act.wait_ge(sh_done, t)
                nc.scalar.activation(h1[:], S[n % 4][:, 0:FF], ACT.Silu).then_inc(sh_silu, 1)
                act.wait_ge(hsT_mm, t + 1)
                nc.scalar.activation(hsT[:, :, t * P:(t + 1) * P],
                                     W[1][:, t * SEQ:(t + 1) * SEQ].rearrange("p (k q) -> p k q", k=2), ACT.Copy
                                     ).then_inc(hsT_cp, 1)
            nc.scalar.activation(ident_r[:], ident, ACT.Copy).then_inc(hsT_cp, 1)
            for k in range(0, 4, 2):
                act.wait_ge(gath_mm, k + 1)
                nc.scalar.activation(xg[0][:, 2 * k:2 * k + 2, :], two_blocks(S[k]), ACT.Copy).then_inc(gath_act, 1)
            with act.Fori(0, PAIRS // ROUND) as i:
                for jj in range(ROUND):
                    act.wait_ge(gu_mm, i * 8 + (jj + 1))
                    nc.scalar.activation(h1[:], S[2][:, 0:FF], ACT.Silu).then_inc(h_silu, 1)
                    act.wait_ge(gath_mm, i * 16 + (4 + 2 * jj + 1))
                    b = 4 * (jj % 2)
                    nc.scalar.activation(xg[(jj // 2 + 1) % 2][:, b:b + 2, :], two_blocks(S[1]), ACT.Copy
                                         ).then_inc(gath_act, 1)
                    act.wait_ge(hT_mm, i * 8 + (jj + 1))
                    nc.scalar.activation(hT[:], S[2][:, 0:2 * P].rearrange("p (k s) -> p k s", k=2), ACT.Copy
                                         ).then_inc(hT_cp, 1)
                    act.wait_ge(gate_cp, i * 16 + 2 * (jj + 1))
                    for c in range(2):
                        act.wait_ge(down_mm, i * 16 + (2 * jj + c + 1))
                        nc.scalar.activation(yh[:, c * 512:(c + 1) * 512], (S[3], S[1])[c][:], ACT.Copy,
                                             scale=slot_gate[:, 0:1]).then_inc(yh_done, 1)
            act.wait_ge(items_ld, 32)
            n_items = act.value_load(items[0:1, P:P + 1], min_val=0, max_val=EXTRA)
            with act.If(n_items > 0):
                with act.Fori(0, n_items) as i:
                    act.wait_ge(o_gu, i + 1)
                    nc.scalar.activation(h1[:], S[2][:, 0:FF], ACT.Silu).then_inc(o_h1, 1)
                    act.wait_ge(o_down, i + 1)
                    for c in range(2):
                        nc.scalar.activation(yh[:, c * 512:(c + 1) * 512], (S[3], S[1])[c][:], ACT.Copy,
                                             scale=slot_gate[:, 0:1]).then_inc(o_y, 1)
            steps = [0]

            def step(ins):
                steps[0] += 1
                ins.then_inc(norm_act, 1)
                act.wait_ge(norm_act, steps[0])

            act.wait_ge(moe_mm, 2)
            for c in range(2):
                step(nc.scalar.activation(unread[:], W[2 + c][:], ACT.Copy, accum_out=half_sum[:, c:c + 1]))
            act.wait_ge(ln_var, 2 * TB + 1)
            nc.scalar.activation(rstd[:, 0:1], rvar[:, 0:1], ACT.Sqrt).then_inc(ln_sqrt, 1)
            step(nc.scalar.activation(half_sum[:, 1:2], half_sum[:, 1:2], ACT.Copy, scale=-1.0 / D))
            step(nc.scalar.activation(neg_mean[:, 1:2], half_sum[:, 0:1], ACT.Identity, scale=-1.0 / D,
                                      bias=half_sum[:, 1:2]))
            for c in range(2):
                step(nc.scalar.activation(unread[:], W[2 + c][:], ACT.Square, bias=neg_mean[:, 1:2],
                                          accum_out=half_square[:, c:c + 1]))
            step(nc.scalar.activation(half_square[:, 1:2], half_square[:, 1:2], ACT.Copy, scale=1.0 / D, bias=EPS))
            nc.scalar.activation(half_std[:, 0:1], half_square[:, 0:1], ACT.Sqrt, scale=1.0 / D,
                                 bias=half_square[:, 1:2]).then_inc(ln_sqrt, 1)

        @block.vector
        def _(ve):
            steps = [0]

            def link(ins):
                steps[0] += 1
                ins.then_inc(dve, 1)
                ve.wait_ge(dve, steps[0])

            tt = nc.vector.tensor_tensor
            ts = nc.vector.tensor_scalar
            stt = nc.vector.scalar_tensor_tensor

            split = [N_PLAIN]

            def chunk_rests(n):
                while split[0] < N_SPLIT and (split[0] < ROUNDED or DONE[split[0] - ROUNDED] <= n + 1):
                    q = split[0]
                    if rest_by_dve(q):
                        ve.wait_ge(w_rounded, q + 1 - N_PLAIN)
                        tt(w_lo[:, q % 6, :], raw[:, q % 6, :], w_hi[:, q % ROUNDED, :].bitcast(F32), ALU.subtract
                           ).then_inc(w_rest_dve, 1)
                    split[0] += 1

            nc.vector.memset(xpad[:], 0.0).then_inc(pad_zero, 1)
            link(nc.vector.memset(slot_of[:], 0.0))
            for half in range(2):
                ve.wait_ge(x_rounded, half + 1)
                tt(xT_r[1][:, 4 * half:4 * half + 4, :], xT[:, 4 * half:4 * half + 4, :],
                   xT_r[0][:, 4 * half:4 * half + 4, :].bitcast(F32), ALU.subtract).then_inc(x_rest, 1)
            chunk_rests(-1)

            def small_parameters():
                ve.wait_ge(small_in, 48)
                ve.wait_ge(rel_mm, 1)
                nc.vector.tensor_copy(bds[0:DIFF_HEADS, :], W[0][0:DIFF_HEADS, 0:384]).then_inc(rel_cp, 1)
                for k in range(2):
                    q = R_LAM + 128 * k
                    link(tt(lam_tmp[:], row[:, q:q + 64], row[:, q + 64:q + 128], ALU.mult))
                    nc.vector.tensor_reduce(lam_d[:, k:k + 1], lam_tmp[:], AX.X, ALU.add).then_inc(lam_dots, 1)
                    ve.wait_ge(lam_dots, k + 1)
                ve.wait_ge(x_rounded, 3)
                tt(wdt_r[1][:], w_dt, wdt_r[0][:].bitcast(F32), ALU.subtract).then_inc(x_rest, 1)
                ve.wait_ge(small_exp, 2)
                link(stt(neg_lam[:], lam_e[:, 1:2], -LAM_INIT, lam_e[:, 0:1], ALU.add, ALU.subtract))
                link(ts(exp_alog[:], exp_alog[:], -1.0, None, ALU.mult))

            ve.wait_ge(pad_zero, 1)
            ve.wait_ge(conv_in, 16)
            for b in range(NXB):
                ve.wait_ge(act_took, b + 1)
                if b >= 2:
                    ve.wait_ge(conv_silu, b - 1)
                link(ts(acc[:, b % 2, :], xpad[:, b % 4, 0:SEQ], conv_w[:, b, 0:1], None, ALU.mult))
                for j in range(1, CONV):
                    ins = stt(acc[:, b % 2, :], xpad[:, b % 4, j:j + SEQ], conv_w[:, b, j:j + 1], acc[:, b % 2, :],
                              ALU.mult, ALU.add)
                    if j < CONV - 1:
                        link(ins)
                ins.then_inc(conv_done, 1)
                chunk_rests(out_index("xbc", b))
                if b == 8:
                    small_parameters()

            ve.wait_ge(dt_mm, 1)
            nc.vector.tensor_copy(dtT[0:SSD_HEADS, :], W[1][0:SSD_HEADS, 0:SEQ]).then_inc(dtT_cp, 1)
            ve.wait_ge(dt_mm, 2)
            u, e, s, s2 = (x[:] for x in dt_t)
            raw_dt = W[1][:, SEQ:SEQ + TB * SSD_HEADS].rearrange("p (t h) -> p t h", t=TB)
            link(tt(u, raw_dt, row[:, R_DTB:R_DTB + SSD_HEADS].unsqueeze(1).to_broadcast([P, TB, SSD_HEADS]), ALU.add))
            link(ts(s, u, -1.0, None, ALU.mult))
            tt(e, u, s, ALU.max).then_inc(dt_pre, 1)
            ve.wait_ge(small_exp, 3)
            link(ts(s, e, 2.0, None, ALU.add))
            link(nc.vector.reciprocal(s2, s))
            link(tt(s, e, s2, ALU.mult))
            link(tt(s2, s, s, ALU.mult))
            link(ts(e, s2, 1.0 / 15, 1.0 / 13, ALU.mult, ALU.add))
            for c in (11, 9, 7, 5, 3, 1):
                link(tt(e, e, s2, ALU.mult))
                link(ts(e, e, 1.0 / c, None, ALU.add))
            link(tt(e, e, s, ALU.mult))
            link(ts(u, u, 0.0, None, ALU.max))
            link(stt(dt_v[:], e, 2.0, u, ALU.mult, ALU.add))
            tt(a_v[:], dt_v[:], exp_alog[:].unsqueeze(1).to_broadcast([P, TB, SSD_HEADS]), ALU.mult
               ).then_inc(a_done, 1)
            ve.wait_ge(a_done, 1)
            link(nc.vector.tensor_copy(a_r[0][:], a_v[:]))
            tt(a_r[1][:], a_v[:], a_r[0][:].bitcast(F32), ALU.subtract).then_inc(a_split, 1)
            nc.vector.tensor_copy(strict_r[:], strict).then_inc(a_split, 1)

            chunk_rests(out_index("k", 7))
            ve.wait_ge(cb_mm, GROUPS)
            for g in range(GROUPS):
                bank = W[(1 + g) % 4]
                tt(cbm[:, g].rearrange("p (a l) -> p a l", a=3)[:, 0:3:2, :],
                   bank[:, 0:384].rearrange("p (a l) -> p a l", a=3)[:, 0:3:2, :],
                   tri.unsqueeze(1).to_broadcast([P, 2, P]), ALU.mult).then_inc(cb_cp, 1)
                nc.vector.tensor_copy(cbm[:, g, P:2 * P], bank[:, P:2 * P]).then_inc(cb_cp, 1)
            for k in range(8):
                t, quad = k // 4, k % 4
                ve.wait_ge(xs_mm, k + 1)
                tt(xsdt[:, t, quad * 512:(quad + 1) * 512].rearrange("p (h e) -> p h e", h=8),
                   W[(1 + k) % 4][:].rearrange("p (h e) -> p h e", h=8),
                   dt_v[:, t, quad * 8:(quad + 1) * 8].unsqueeze(2).to_broadcast([P, 8, HEAD]), ALU.mult
                   ).then_inc(xs_cp, 1)

            chunk_rests(out_index("v", 3))
            ve.wait_ge(flip_cp, 4)
            for i in range(8):
                ve.wait_ge(logit_mm, i + 1)
                if i >= 1:
                    ve.wait_ge(attnT_mm, i)
                for m in range(2):
                    o = m * 384
                    for c, (o2, w, r0) in enumerate(((0, P, P), (P, SEQ, 0))):
                        ins = nc.vector.tensor_tensor_reduce(
                            lg[:, o + o2:o + o2 + w], W[m][:, o2:o2 + w], rel[:, i, r0:r0 + w], 1.0, -3.0e38,
                            ALU.add, ALU.max, a_max[:, 2 * m + c:2 * m + c + 1])
                        link(ins)
                ts(a_neg[:], a_max[:], -1.0, None, ALU.mult).then_inc(amax_done, 1)
                for t in range(TB):
                    ve.wait_ge(seg_exp, 2 * i + t + 1)
                    tt(dec[:, t], dec[:, t],
                       cbm[:, i // 2, 2 * t * P:(2 * t + 1) * P].unsqueeze(1).to_broadcast([P, 4, P]), ALU.mult
                       ).then_inc(masked_dec, 1)
                chunk_rests(out_index("z", 4 * i - 1) if i else out_index("v", 7))
                ve.wait_ge(prob_exp, 4 * i + 4)
                link(nc.vector.reciprocal(a_rcp[:], a_sum[:]))
                link(ts(a_rcp[:, 2:4], a_rcp[:, 2:4], neg_lam[:, 0:1], None, ALU.mult))
                ts(lg[:, 384:512], lg[:, 384:512], a_rcp[:, 2:3], None, ALU.mult)
                link(ts(lg[:, 512:768], lg[:, 512:768], a_rcp[:, 3:4], None, ALU.mult))
                stt(attn[:, 0:P], lg[:, 0:P], a_rcp[:, 0:1], lg[:, 384:512], ALU.mult, ALU.add)
                stt(attn[:, P:384], lg[:, P:384], a_rcp[:, 1:2], lg[:, 512:768], ALU.mult, ALU.add
                    ).then_inc(attn_done, 1)
                ve.wait_ge(y_mm, i + 1)
                for j in range(2):
                    b = 2 * i + j
                    link(stt(xc[:, b, :], xc[:, b, :], d_skip[:, b:b + 1], W[2][:, j * SEQ:(j + 1) * SEQ],
                             ALU.mult, ALU.add))
                ve.wait_ge(fac_exp, i + 1)
                link(tt(yo[:], W[3][:, 0:SEQ].rearrange("p (b l) -> p b l", b=2), fac[:], ALU.mult))
                tt(xc[:, 2 * i:2 * i + 2, P:SEQ], xc[:, 2 * i:2 * i + 2, P:SEQ], yo[:], ALU.add).then_inc(y_done, 1)

            chunk_rests(out_index("gate", 15))
            for g in range(GROUPS):
                ve.wait_ge(z_silu, g + 1)
                ve.wait_ge(y_done, 2 * g + 2)
                tt(xc[:, 4 * g:4 * g + 4, :], xc[:, 4 * g:4 * g + 4, :], z[:, 4 * g:4 * g + 4, :], ALU.mult
                   ).then_inc(yz_done, 1)

            def mean_squares(k):
                w, width, factor = (512, P, SUBLN_SCALE ** 2) if k < GROUPS else (SEQ, INNER // GROUPS, 1.0)
                ve.wait_ge(ssq_mm, k + 1)
                ts(rms[:, k, 0:w], W[k % 4][:, 0:w], 1.0 / width / factor, EPS / factor, ALU.mult, ALU.add
                   ).then_inc(ssq_took, 1)

            def invert(k):
                w = 512 if k < GROUPS else SEQ
                ve.wait_ge(ssq_took, k + 1)
                nc.vector.reciprocal(rms[:, k, 0:w], rms[:, k, 0:w]).then_inc(rms_rcp, 1)

            for k in range(GROUPS):
                mean_squares(k)
            chunk_rests(out_index("ck", 3))
            for k in range(GROUPS):
                if k == GROUPS - 1:
                    chunk_rests(out_index("ck", 7))
                invert(k)
            for k in range(GROUPS):
                ve.wait_ge(rms_sqrt, k + 1)
                for j in range(2):
                    h = 2 * k + j
                    stt(oT[:, h, :], oT[:, h, :], subln, rms[:, k, j * SEQ:(j + 1) * SEQ], ALU.mult, ALU.mult
                        ).then_inc(oT_done, 1)
            chunk_rests(out_index("ck", 7))
            for g in range(2):
                ve.wait_ge(oT_rounded, g + 1)
                tt(oT_r[1][:, 4 * g:4 * g + 4, :], oT[:, 4 * g:4 * g + 4, :],
                   oT_r[0][:, 4 * g:4 * g + 4, :].bitcast(F32), ALU.subtract).then_inc(oT_rest, 1)
            chunk_rests(out_index("cv", 1))
            for k in range(GROUPS):
                mean_squares(GROUPS + k)
                invert(GROUPS + k)
            chunk_rests(out_index("cv", 3))
            ve.wait_ge(yz_done, GROUPS)

            def scale_y(g):
                ve.wait_ge(rms_sqrt, GROUPS + g + 1)
                for b in range(4 * g, 4 * g + 4):
                    stt(xc[:, b, :], xc[:, b, :], ssd_g[:, b:b + 1], rms[:, GROUPS + g, 0:SEQ], ALU.mult, ALU.mult
                        ).then_inc(yT_done, 1)

            scale_y(0)
            for k in range(KB):
                n = out_index("diff", k)
                ve.wait_ge(proj_ready, n + 1)
                ve.wait_ge(gate_sig, k // 4 + 1)
                tt(mixT[:, k, :], S[n % 4][:, 0:SEQ], gt[:, KB + k, :], ALU.mult).then_inc(dve_took, 1)
                if k < GROUPS - 1:
                    scale_y(k + 1)
                if k >= GROUPS:
                    g = k - GROUPS
                    ve.wait_ge(yT_rounded, g + 1)
                    tt(yT_r[1][:, 4 * g:4 * g + 4, :], xc[:, 4 * g:4 * g + 4, :],
                       yT_r[0][:, 4 * g:4 * g + 4, :].bitcast(F32), ALU.subtract).then_inc(yT_rest, 1)
                chunk_rests(n)

            for k in range(KB):
                n = out_index("ssd", k)
                ve.wait_ge(proj_ready, n + 1)
                ve.wait_ge(gate_sig, 2 + k // 4 + 1)
                tt(gt[:, k, :], S[n % 4][:, 0:SEQ], gt[:, k, :], ALU.mult).then_inc(dve_took, 1)
                ve.wait_ge(dve_took, taken_count(n))
                tt(mixT[:, k, :], mixT[:, k, :], gt[:, k, :], ALU.add).then_inc(mix_done, 1)
                ve.wait_ge(mixT_rounded, k + 1)
                tt(mixT_r[1][:, k, :], mixT[:, k, :], mixT_r[0][:, k, :].bitcast(F32), ALU.subtract
                   ).then_inc(mixT_rest, 1)
                chunk_rests(n)

            def variance(t, pieces):
                link(nc.vector.bn_aggr(mv[:, t, :], bn[:, t, 0:pieces].rearrange("p c s -> p (c s)")))
                ts(neg_mean[:, t:t + 1], mv[:, t, 0:1], -1.0, None, ALU.mult)
                link(ts(rvar[:, t:t + 1], mv[:, t, 1:2], EPS, None, ALU.add))
                nc.vector.reciprocal(rvar[:, t:t + 1], rvar[:, t:t + 1]).then_inc(ln_var, 1)

            def add_output(kind, before_last=None):
                for k in range(8):
                    if k == 7 and before_last is not None:
                        before_last()
                    n = out_index(kind, k)
                    t, c = k % TB, k // TB
                    ve.wait_ge(proj_ready, n + 1)
                    part = xres[:, t, c * SEQ:(c + 1) * SEQ]
                    stt(part, part, ALPHA, S[n % 4][:, 0:SEQ], ALU.mult, ALU.add).then_inc(dve_took, 1)
                    ve.wait_ge(dve_took, taken_count(n))
                    ins = nc.vector.bn_stats(bn[:, t, c, :], part)
                    if c == 3:
                        link(ins)
                        variance(t, 4)
                    chunk_rests(n)

            def normalise(which, t):
                ve.wait_ge(ln_sqrt, TB * which + t + 1)
                return ts(xres[:, t, :], xres[:, t, :], mv[:, t, 0:1], rstd[:, t:t + 1], ALU.subtract, ALU.mult)

            def gain_bias(t, weights):
                link(tt(xres[:, t, :], xres[:, t, :], weights[:, 0, :], ALU.mult))
                tt(xres[:, t, :], xres[:, t, :], weights[:, 1, :], ALU.add).then_inc(ln_done, 1)

            ve.wait_ge(xres_ld, 16)
            add_output("mix")
            ve.wait_ge(ln_ld, 16)
            for t in range(TB):
                link(normalise(0, t))
                gain_bias(t, ln1)
            chunk_rests(out_index("cvb", 1))
            for k in range(4):
                ve.wait_ge(xt_cp, k + 1)
                part = (slice(None), slice(4 * (k % 2), 4 * (k % 2) + 4), slice(k // 2 * P, (k // 2 + 1) * P))
                tt(x1T_r[1][part], W[k][:].rearrange("p (b t) -> p b t", b=4), x1T_r[0][part].bitcast(F32),
                   ALU.subtract).then_inc(xt_rest, 1)
            chunk_rests(out_index("cvb", 3))
            chunk_rests(out_index("cq", 7))
            for h in range(MEM_HEADS):
                ve.wait_ge(clog_mm, h + 1)
                nc.vector.tensor_reduce(c_neg[:, h, :], W[h][:].rearrange("p (t k) -> p t k", t=TB), AX.X, ALU.max,
                                        negate=True).then_inc(cmax_done, 1)
            for h in range(MEM_HEADS):
                ve.wait_ge(cprob_exp, TB * h + TB)
                link(nc.vector.reciprocal(c_rcp[:, h, :], c_sum[:, h, :]))
                for t in range(TB):
                    ts(pc[:, h, t, :], pc[:, h, t, :], c_rcp[:, h, t:t + 1], None, ALU.mult).then_inc(cprob_done, 1)
            for h in range(MEM_HEADS):
                ve.wait_ge(cav_cp, h + 1)
                tt(ocT_r[1][:, 2 * h:2 * h + 2, :], W[h][:].rearrange("p (k q) -> p k q", k=2),
                   ocT_r[0][:, 2 * h:2 * h + 2, :].bitcast(F32), ALU.subtract).then_inc(cav_rest, 1)
            ve.wait_ge(ln_done, TB)
            add_output("co", before_last=lambda: normalise(1, 0).then_inc(xhat_done, 1))
            normalise(1, 1).then_inc(xhat_done, 1)
            for t in range(TB):
                ve.wait_ge(xt_mm, 4 + 2 * t + 2)
                for k in range(4, KB):
                    ts(x2T[:, k, t * P:(t + 1) * P], W[2 * t + 1][:, (k - 4) * P:(k - 3) * P], ln2_g[:, k:k + 1],
                       ln2_b[:, k:k + 1], ALU.mult, ALU.add).then_inc(x2T_dve, 1)
            ve.wait_ge(ln_ld, 32)
            ve.wait_ge(xhat_done, 1)
            gain_bias(0, ln2)

            def rest_of_x(t):
                ve.wait_ge(split_h, t + 1)
                tt(x2l[:, t, :], xres[:, t, :], x2h[:, t, :].bitcast(F32), ALU.subtract).then_inc(split_l, 1)

            ve.wait_ge(scoreT_mm, 1)
            turned_scores = W[0][:, SEQ:SEQ + TB * EXPERTS].rearrange("p (t e) -> p t e", t=TB)
            nc.vector.tensor_copy(scores[:], turned_scores)
            link(tt(choice[:], turned_scores, row[:, R_RB:R_RB + EXPERTS].unsqueeze(1).to_broadcast([P, TB, EXPERTS]),
                    ALU.add))
            for t in range(TB):
                for g in range(EGROUPS):
                    ins = nc.vector.max(max8[:, t, g, :], choice[:, t, 8 * g:8 * g + 8])
                    if g == EGROUPS - 1:
                        link(ins)
            link(tt(gsc[:], max8[:, :, :, 0], max8[:, :, :, 1], ALU.add))
            other = gsc[:].unsqueeze(2).to_broadcast([P, TB, EGROUPS, EGROUPS])
            own = gsc[:].unsqueeze(3).to_broadcast([P, TB, EGROUPS, EGROUPS])
            tt(gcmp[:], other, own, ALU.is_gt)
            link(tt(geq[:], other, own, ALU.is_equal))
            for t in range(TB):
                link(tt(geq[:, t], geq[:, t], lower8, ALU.mult))
            link(tt(gcmp[:], gcmp[:], geq[:], ALU.add))
            link(nc.vector.tensor_reduce(goff[:], gcmp[:], AX.X, ALU.add))
            link(ts(gmask[:], goff[:], TOP_GROUPS - 0.5, None, ALU.is_lt))
            link(ts(goff[:], gmask[:], -MASKED, MASKED, ALU.mult, ALU.add))
            for t in range(TB):
                by_group = masked[:, t].rearrange("p (g e) -> p g e", g=EGROUPS)
                link(tt(by_group, choice[:, t].rearrange("p (g e) -> p g e", g=EGROUPS),
                        gmask[:, t].unsqueeze(2).to_broadcast([P, EGROUPS, 8]), ALU.mult))
                link(tt(by_group, by_group, goff[:, t].unsqueeze(2).to_broadcast([P, EGROUPS, 8]), ALU.add))
            for t in range(TB):
                link(nc.vector.max(top8[:, t, :], masked[:, t, :]))
                link(nc.vector.match_replace(choice[:, t, :], top8[:, t, :], masked[:, t, :], -2.0 * MASKED))
            ts(sel[:], choice[:], -MASKED, None, ALU.is_gt).then_inc(sel_done, 1)
            ve.wait_ge(sel_done, 1)
            link(tt(gates_e[:], scores[:], sel[:], ALU.mult))
            link(nc.vector.tensor_reduce(w_sum[:], gates_e[:], AX.X, ALU.add))
            link(nc.vector.reciprocal(w_rcp[:], w_sum[:]))
            for t in range(TB):
                link(ts(gates_e[:, t, :], gates_e[:, t, :], w_rcp[:, t:t + 1], ROUTED_SCALE, ALU.mult, ALU.mult))
            rest_of_x(0)
            ve.wait_ge(rank_mm, 1)
            tt(slot_of[:, :, 0:EXPERTS], W[2][:, 0:TB * EXPERTS].rearrange("p (t e) -> p t e", t=TB), sel[:], ALU.mult
               ).then_inc(place_done, 1)
            ve.wait_ge(place_done, 1)

            def make_onehot(buf, first):
                for t in range(TB):
                    tt(onehot[:, buf, t], slot_no.unsqueeze(1).to_broadcast([P, PER_GROUP, SLOTS]),
                       slot_of[:, t, first].unsqueeze(2).to_broadcast([P, PER_GROUP, SLOTS]), ALU.is_equal
                       ).then_inc(onehot_done, 1)

            make_onehot(0, slice(0, PER_GROUP))
            tt(zero_r[:], ones, ones, ALU.subtract).then_inc(onehot_done, 1)
            rest_of_x(1)
            for t in range(TB):
                n = out_index("sh", TB + t)
                ve.wait_ge(sh_silu, t + 1)
                ve.wait_ge(proj_ready, n + 1)
                if t:
                    ve.wait_ge(hsT_mm, t)
                tt(hh[:], h1[:], S[n % 4][:, 0:FF], ALU.mult).then_inc(sh_done, 1)
            ve.wait_ge(place_done, 1)
            cnt = W[2][:, TB * EXPERTS:(TB + 1) * EXPERTS].rearrange("p (q e) -> p e q", e=2)
            link(nc.vector.tensor_copy(pair_n[:], cnt[:, 0, :]))
            tt(pair_n[:], pair_n[:], cnt[:, 1, :], ALU.max).then_inc(place_done, 1)
            ve.wait_ge(place_done, 2)
            for k in range(1, 4, 2):
                ve.wait_ge(gath_mm, k + 1)
                nc.vector.tensor_copy(xg[0][:, 2 * k:2 * k + 2, :], two_blocks(S[k])).then_inc(gath_dve, 1)
            for r in range(1, CHUNKS):
                ins = ts(flags[:, 0, (r - 1) * PAIRS:r * PAIRS], pair_n[:], SLOTS * r + 0.5, None, ALU.is_gt)
            link(ins)
            link(nc.vector.tensor_copy(item_eq[:], flags[:, 0, :]))
            cur, width = 0, 1
            while width < EXTRA:
                link(nc.vector.tensor_copy(flags[:, 1 - cur, 0:width], flags[:, cur, 0:width]))
                link(tt(flags[:, 1 - cur, width:EXTRA], flags[:, cur, width:EXTRA], flags[:, cur, 0:EXTRA - width],
                        ALU.add))
                cur, width = 1 - cur, 2 * width
            link(nc.vector.tensor_copy(item_f[:, 1:2], flags[:, cur, EXTRA - 1:EXTRA]))
            link(tt(item_eq[:], item_eq[:], flags[:, cur, :], ALU.mult))
            link(ts(item_eq[:], item_eq[:], part_no, None, ALU.is_equal))
            link(tt(item_eq[:], item_eq[:], cs[:, C_ITEMS:C_ITEMS + EXTRA],
                    ALU.mult))
            link(nc.vector.tensor_reduce(item_f[:, 0:1], item_eq[:], AX.X, ALU.add))
            nc.vector.tensor_copy(item_col[:], item_f[:]).then_inc(item_done, 2)
            with ve.Fori(0, PAIRS // ROUND) as i:
                for jj in range(ROUND):
                    if jj % 2 == 0:
                        make_onehot((jj // 2 + 1) % 2, bass.ds(i * 16 + (4 * (jj // 2) + 4), PER_GROUP))
                    ve.wait_ge(h_silu, i * 8 + (jj + 1))
                    tt(hh[:], h1[:], S[2][:, FF:2 * FF], ALU.mult).then_inc(h_done, 1)
                    ve.wait_ge(scatT_mm, i * 8 + (jj + 1))
                    for c in range(2):
                        r = slice(c * SLOTS, (c + 1) * SLOTS)
                        nc.vector.tensor_copy(slot_gate[r, :], S[0][r, SEQ + c:SEQ + c + 1]).then_inc(gate_cp, 1)
                    nc.vector.tensor_copy(scatT[:], S[0][:, 0:SEQ]).then_inc(scatT_cp, 1)
                    ve.wait_ge(gath_mm, i * 16 + (4 + 2 * jj + 2))
                    b = 4 * (jj % 2) + 2
                    nc.vector.tensor_copy(xg[(jj // 2 + 1) % 2][:, b:b + 2, :], two_blocks(S[0])
                                          ).then_inc(gath_dve, 1)
                    for c in range(2):
                        ve.wait_ge(yh_done, i * 16 + (2 * jj + c + 1))
                        stt(yl[:, c * 512:(c + 1) * 512], (S[3], S[1])[c][:], slot_gate[:, 0:1],
                            yh[:, c * 512:(c + 1) * 512].bitcast(F32), ALU.mult, ALU.subtract).then_inc(yl_done, 1)
            ve.wait_ge(items_ld, 32)
            n_items = ve.value_load(items[0:1, P:P + 1], min_val=0, max_val=EXTRA)
            with ve.If(n_items > 0):
                with ve.Fori(0, n_items) as i:
                    item = ve.value_load(items[0:1, bass.ds(i, 1)], min_val=0, max_val=EXTRA - 1)
                    ve.wait_ge(o_scat, i + 1)
                    for t in range(TB):
                        ts(place_off[:, t, :], slot_of[:, t, bass.ds((item % PAIRS) * 2, 2)],
                           cs[:, bass.ds(item + C_ROFF, 1)], None, ALU.subtract).then_inc(o_hot, 1)
                    ve.wait_ge(o_hot, i * 4 + 2)
                    for t in range(TB):
                        tt(onehot[:, 0, t, 0:2, :], slot_no.unsqueeze(1).to_broadcast([P, 2, SLOTS]),
                           place_off[:, t, :].unsqueeze(2).to_broadcast([P, 2, SLOTS]), ALU.is_equal
                           ).then_inc(o_hot, 1)
                    ve.wait_ge(o_gath, i + 1)
                    for c in range(2):
                        nc.vector.tensor_copy(xg[0][:, 4 * c:4 * c + 4, 0:P],
                                              S[c][:].rearrange("p (k s) -> p k s", k=4)).then_inc(o_xg, 1)
                    ve.wait_ge(o_h1, i + 1)
                    tt(hh[:], h1[:], S[2][:, FF:2 * FF], ALU.mult).then_inc(o_h, 1)
                    ve.wait_ge(o_T, i + 1)
                    for c in range(2):
                        r = slice(c * SLOTS, (c + 1) * SLOTS)
                        nc.vector.tensor_copy(slot_gate[r, :], S[0][r, SEQ + c:SEQ + c + 1]).then_inc(o_Tcp, 1)
                    nc.vector.tensor_copy(scatT[:], S[0][:, 0:SEQ]).then_inc(o_Tcp, 1)
                    nc.vector.tensor_copy(hT[:], S[2][:, 0:2 * P].rearrange("p (k s) -> p k s", k=2)
                                          ).then_inc(o_Tcp, 1)
                    ve.wait_ge(o_y, i * 4 + 2)
                    for c in range(2):
                        stt(yl[:, c * 512:(c + 1) * 512], (S[3], S[1])[c][:], slot_gate[:, 0:1],
                            yh[:, c * 512:(c + 1) * 512].bitcast(F32), ALU.mult, ALU.subtract).then_inc(o_y, 1)
            ve.wait_ge(moe_mm, 1)
            for c in range(2):
                ins = nc.vector.bn_stats(bn[:, 0, c, :], W[c][:])
            link(ins)
            variance(0, 2)
            ve.wait_ge(ln_ld, 48)
            for t in range(TB):
                if t:
                    ve.wait_ge(ln_sqrt, 2 * TB + 2)
                for c in range(2):
                    cols = slice(c * 512, (c + 1) * 512)
                    ins = stt(normed[:, t, cols], W[2 * t + c][:], neg_mean[:, t:t + 1], ln3[:, 0, cols],
                              ALU.add, ALU.mult)
                if t:
                    ins = nc.vector.reciprocal(rstd[:, 1:2], half_std[:, 0:1])
                link(ins)
                if t == 0:
                    ve.wait_ge(ln_sqrt, 2 * TB + 1)
                stt(normed[:, t, :], normed[:, t, :], rstd[:, t:t + 1], ln3[:, 1, :], ALU.mult, ALU.add
                    ).then_inc(ln_done, 1)

        @block.tensor
        def _(pe):
            mm = nc.tensor.matmul

            def bank_free(n):
                if n >= 4:
                    pe.wait_ge(dve_took if OUT_KIND[n - 4] in BY_DVE else act_took, taken_count(n - 4))

            def chunk_here(q):
                if N_PLAIN <= q < N_SPLIT:
                    pe.wait_ge(w_rest_dve if rest_by_dve(q) else w_rest_pool, rest_count(q))
                elif q == 0:
                    pe.wait_ge(first_ld, 16)
                else:
                    pe.wait_ge(dense_ld[q // 2 % RAW_TILES], 16 * (q // 2 // RAW_TILES + 1))

            def chunk(q, cols):
                return [w.rearrange("p (k c) -> p k c", c=cols) for w in (w_hi[:, q % ROUNDED, :], w_lo[:, q % 6, :])]

            def feature_major(kind, k, act_r, chunks=1, ready=None):
                n = out_index(kind, k)
                bank_free(n)
                for c in range(chunks):
                    q = CHUNK0[kind] + k * chunks + c
                    chunk_here(q)
                    w_h, w_l = chunk(q, P)
                    parts = ((w_h, act_r[0]), (w_h, act_r[1]), (w_l, act_r[0]))
                    if q < N_PLAIN:
                        parts = ((raw[:, q, :].rearrange("p (k c) -> p k c", c=P), xT),)
                    for b in range(KB):
                        kb = c * KB + b
                        if q < N_PLAIN and kb % 4 == 0:
                            pe.wait_ge(xT_ld[kb // 4], 16)
                        if ready is not None and kb % 4 == 0:
                            pe.wait_ge(ready, kb // 4 + 1)
                        for j, (w, a) in enumerate(parts):
                            last = mm(S[n % 4][:, 0:SEQ], w[:, b, :], a[:, kb, :], start=(kb + j == 0),
                                      stop=(kb == chunks * KB - 1 and j == len(parts) - 1))
                last.then_inc(proj_ready, 1)

            def token_major(kind, k, act_r, midway=None, ready=None):
                n = out_index(kind, k)
                q, t = CHUNK0[kind] + k // TB * 2, k % TB
                bank_free(n)
                if t == 0:
                    chunk_here(q)
                    chunk_here(q + 1)
                for kb in range(KB):
                    if kb == 4 and midway is not None:
                        midway()
                    if ready is not None:
                        pe.wait_ge(ready, kb + 1)
                    rows, cols = slice(t * P, (t + 1) * P), kb % 4
                    if q < N_SPLIT:
                        w_h, w_l = chunk(q + kb // 4, SEQ)
                        parts = ((act_r[0], w_h), (act_r[1], w_h), (act_r[0], w_l))
                    else:
                        parts = ((act_r, raw[:, (q + kb // 4) % 6, :].rearrange("p (k c) -> p k c", c=SEQ)),)
                    for j, (a, w) in enumerate(parts):
                        last = mm(S[n % 4][:, 0:SEQ], a[:, kb, rows], w[:, cols, :], start=(kb + j == 0),
                                  stop=(kb == KB - 1 and j == len(parts) - 1))
                last.then_inc(proj_ready, 1)

            def keep_warm(bank, lhsT, rhs, times):
                for _ in range(times):
                    mm(bank, lhsT, rhs, start=True, stop=True)

            pe.wait_ge(pad_zero, 1)
            keep_warm(W[3][:, 0:SEQ], xpad[:, 0, 0:P], xpad[:, 1, 0:SEQ], 4)
            for b in range(NXB):
                feature_major("xbc", b, xT_r, ready=x_rest if b == N_PLAIN else None)
                if b == 6:
                    pe.wait_ge(small_in, 48)
                    mm(W[0][0:DIFF_HEADS, 0:384], cs[0:BUCKETS + 1, C_RB:C_RB + 8],
                       cs[0:BUCKETS + 1, C_HOT:C_HOT + 384], start=True, stop=True).then_inc(rel_mm, 1)
            pe.wait_ge(x_rest, 3)
            for kb in range(KB):
                for j, (w, a) in enumerate(((0, 0), (0, 1), (1, 0))):
                    last = mm(W[1][0:SSD_HEADS, 0:SEQ], wdt_r[w][:, kb, :], xT_r[a][:, kb, :], start=(kb + j == 0),
                              stop=(kb == KB - 1 and j == 2))
            last.then_inc(dt_mm, 1)
            for h in range(DIFF_HEADS):
                feature_major("q", h, xT_r)
                if h == 1:
                    pe.wait_ge(dtT_cp, 1)
                    for t in range(TB):
                        last = nc.tensor.transpose(W[1][:, SEQ + t * SSD_HEADS:SEQ + (t + 1) * SSD_HEADS],
                                                   dtT[0:SSD_HEADS, t * P:(t + 1) * P], ident[0:SSD_HEADS, 0:SSD_HEADS])
                    last.then_inc(dt_mm, 1)
            for h in range(DIFF_HEADS):
                feature_major("k", h, xT_r)
            pe.wait_ge(rel_ld, 32)
            pe.wait_ge(rel_cp, 1)
            pe.wait_ge(a_done, 1)
            for k in range(4):
                mm(W[k][:], flip, rel_flipped[:, 2 * k:2 * k + 2, :], start=True, stop=True).then_inc(flip_mm, 1)
            pe.wait_ge(flip_cp, 4)
            mm(W[0][:, 0:SSD_HEADS], strict, a_v[:, 0, :], start=True, stop=True).then_inc(end_mm, 1)
            pe.wait_ge(conv_silu, NXB)
            for g in range(GROUPS):
                if g == 3:
                    pe.wait_ge(small_exp, 4)
                bank = W[(1 + g) % 4]
                bT, cT = xc[:, XS_BLOCKS + g, :], xc[:, XS_BLOCKS + GROUPS + g, :]
                mm(bank[:, 0:SEQ], bT[:, 0:P], cT, start=True, stop=True)
                mm(bank[:, SEQ:384], bT[:, P:SEQ], cT[:, P:SEQ], start=True, stop=True).then_inc(cb_mm, 1)
            for k in range(8):
                t, quad = k // 4, k % 4
                if k < 4:
                    pe.wait_ge(cb_cp, 2 * k + 2)
                else:
                    pe.wait_ge(xs_cp, k - 3)
                for j in range(4):
                    last = nc.tensor.transpose(W[(1 + k) % 4][:, j * P:(j + 1) * P],
                                               xc[:, 4 * quad + j, t * P:(t + 1) * P], ident)
                last.then_inc(xs_mm, 1)
            for k in range(8):
                token_major("v", k, xT_r)

            for i in range(8):
                for t in range(TB):
                    pe.wait_ge(gdec_done, 4 * i + 2 * t + 2)
                    if i == 0:
                        pe.wait_ge(xs_cp, 8)
                    else:
                        pe.wait_ge(y_done, i)
                    for j in range(2):
                        last = mm(W[2 + t][:], strict_r[:], a_tri[j][:, t].rearrange("p h l -> p (h l)"),
                                  start=(j == 0), stop=(j == 1))
                    last.then_inc(seg_mm, 1)
                if i >= 1:
                    pe.wait_ge(attnT_cp, i)
                    pe.wait_ge(av_cp, i)
                if i == 0:
                    pe.wait_ge(act_took, taken_count(out_index("k", 7)))
                for m in range(2):
                    r = slice(HEAD * m, HEAD * m + HEAD)
                    mm(W[m][:, 0:P], qT[r, i, 0:P], kT[r, i, 0:P], start=True, stop=True)
                    last = mm(W[m][:, P:384], qT[r, i, P:SEQ], kT[r, i, :], start=True, stop=True)
                last.then_inc(logit_mm, 1)
                kind = "z" if i < 4 else "gate"
                k0 = 4 * (i % 4)
                feature_major(kind, k0, xT_r)
                feature_major(kind, k0 + 1, xT_r)
                pe.wait_ge(masked_dec, 2 * i + 2)
                for j in range(2):
                    for t in range(TB):
                        for h in range(2):
                            c = 256 * i + P * j + HEAD * h
                            last = mm(W[2][HEAD * h:HEAD * h + HEAD, j * SEQ + t * P:j * SEQ + (t + 1) * P],
                                      xsdt[:, t, c:c + HEAD], dec[:, t, 2 * j + h, :], start=True, stop=True)
                last.then_inc(y_mm, 1)
                pe.wait_ge(xend_done, i + 1)
                for j in range(2):
                    mm(W[3][:, j * P:(j + 1) * P], xend[:, 2 * j:2 * j + 2, :].rearrange("p h e -> p (h e)"),
                       cbm[:, i // 2, P:2 * P], start=True, stop=True)
                for j in range(2):
                    for h in range(2):
                        a_h = a_v[:, 1, 4 * i + 2 * j + h:4 * i + 2 * j + h + 1].to_broadcast([P, HEAD])
                        last = mm(W[3][HEAD * h:HEAD * h + HEAD, SEQ + j * P:SEQ + (j + 1) * P], a_h, tri,
                                  start=True, stop=True)
                last.then_inc(off_mm, 1)
                pe.wait_ge(attn_done, i + 1)
                for j in range(3):
                    last = nc.tensor.transpose(W[0][:, j * P:(j + 1) * P], attn[:, j * P:(j + 1) * P], ident)
                last.then_inc(attnT_mm, 1)
                feature_major(kind, k0 + 2, xT_r)
                feature_major(kind, k0 + 3, xT_r)
                if i == 0:
                    pe.wait_ge(act_took, taken_count(out_index("v", 7)))
                pe.wait_ge(attnT_cp, i + 1)
                mm(W[1][:, 0:SEQ], v[:, 0, i * P:(i + 1) * P], attnT[:, 0:SEQ], start=True, stop=False,
                   skip_group_check=True)
                mm(W[1][:, P:SEQ], v[:, 1, i * P:(i + 1) * P], attnT[:, SEQ:384], start=False, stop=True,
                   skip_group_check=True).then_inc(av_mm, 1)

            def sums_of_squares(k):
                pe.wait_ge(squared, k + 1)
                if k < GROUPS:
                    if k == 0:
                        pe.wait_ge(attnT_cp, 8)
                        pe.wait_ge(av_cp, 8)
                        pe.wait_ge(y_done, 8)
                    last = mm(W[k][:], ones, sqd[:, 2 * k:2 * k + 2, :], start=True, stop=True)
                else:
                    g = k - GROUPS
                    pe.wait_ge(ssq_took, g + 1)
                    for j in range(4):
                        last = mm(W[g][:, 0:SEQ], ones, z[:, 4 * g + j, :], start=(j == 0), stop=(j == 3))
                last.then_inc(ssq_mm, 1)

            pe.wait_ge(mem_rest, 2)
            for k in range(8):
                feature_major("ck", k, memT_r)
                if k == 3:
                    for g in range(GROUPS):
                        sums_of_squares(g)
            for g in range(GROUPS):
                sums_of_squares(GROUPS + g)
            for k in range(4):
                token_major("cv", k, memT_r)
            pe.wait_ge(oT_rest, 2)
            for k in range(KB):
                feature_major("diff", k, oT_r)
            for k in range(KB):
                feature_major("ssd", k, yT_r, chunks=2, ready=yT_rest if k == 0 else None)
            for k in range(8):
                token_major("mix", k, mixT_r, ready=mixT_rest if k == 0 else None)
            def turn(t):
                for c in range(2):
                    for j in range(4):
                        last = nc.tensor.transpose(W[2 * t + c][:, j * P:(j + 1) * P],
                                                   xres[:, t, (4 * c + j) * P:(4 * c + j + 1) * P], ident)
                    last.then_inc(xt_mm, 1)

            for k in range(3):
                token_major("cvb", k, memT_r)
            pe.wait_ge(rms_rcp, 2 * GROUPS)
            pe.wait_ge(ln_done, 1)
            turn(0)
            token_major("cvb", 3, memT_r)
            pe.wait_ge(ln_done, 2)
            turn(1)
            pe.wait_ge(xt_rest, 4)
            for k in range(KB):
                feature_major("cq", k, x1T_r)
            for h in range(MEM_HEADS):
                pe.wait_ge(act_took, taken_count(out_index("cq", 2 * h + 1)))
                for t in range(TB):
                    for c in range(2):
                        last = mm(W[h][:, t * SEQ:(t + 1) * SEQ], qcT[:, 2 * h + c, t * P:(t + 1) * P],
                                  kcT[:, 2 * h + c, :], start=(c == 0), stop=(c == 1))
                last.then_inc(clog_mm, 1)
            for h in range(MEM_HEADS):
                pe.wait_ge(cprob_done, TB * (h + 1))
                for kb in range(2):
                    for t in range(TB):
                        last = nc.tensor.transpose(W[h][:, kb * SEQ + t * P:kb * SEQ + (t + 1) * P],
                                                   pc[:, h, t, kb * P:(kb + 1) * P], ident)
                last.then_inc(cpT_mm, 1)
            for h in range(MEM_HEADS):
                pe.wait_ge(cpT_cp, h + 1)
                for c in range(2):
                    for kb in range(2):
                        last = mm(W[h][:, c * SEQ:(c + 1) * SEQ], vc[:, kb, (2 * h + c) * P:(2 * h + c + 1) * P],
                                  pcT[:, h, kb, :], start=(kb == 0), stop=(kb == 1))
                last.then_inc(cav_mm, 1)
            pe.wait_ge(cav_rest, MEM_HEADS)
            for k in range(8):
                token_major("co", k, ocT_r)
            bank_free(out_index("sh", 0))
            for t in range(TB):
                pe.wait_ge(xhat_done, t + 1)
                turn(t)
                keep_warm(S[0][:, 0:SEQ], ocT_r[0][:, 0, 0:P], ocT_r[0][:, 1, :], 13)
            pe.wait_ge(x2T_act, 8)
            pe.wait_ge(x2T_dve, 8)
            for kb in range(KB):
                last = mm(W[0][0:EXPERTS, 0:SEQ], w_router[:, kb, :], x2T[:, kb, :], start=(kb == 0),
                          stop=(kb == KB - 1))
            last.then_inc(score_mm, 1)

            def turn_scores():
                pe.wait_ge(score_sig, 1)
                for t in range(TB):
                    last = nc.tensor.transpose(W[0][:, SEQ + t * EXPERTS:SEQ + (t + 1) * EXPERTS],
                                               scoresT[0:EXPERTS, t * P:(t + 1) * P], ident[0:EXPERTS, 0:EXPERTS])
                last.then_inc(scoreT_mm, 1)

            token_major("sh", 0, x2T, midway=turn_scores)
            token_major("sh", 1, x2T)
            token_major("sh", 2, x2T)
            pe.wait_ge(sel_done, 1)
            mm(W[2][:, 0:EXPERTS], tri, sel[:, 0, :], start=True, stop=True)
            mm(W[2][:, EXPERTS:2 * EXPERTS], ones, sel[:, 0, :], start=True, stop=False)
            mm(W[2][:, EXPERTS:2 * EXPERTS], tri, sel[:, 1, :], start=False, stop=True)
            mm(W[2][:, 2 * EXPERTS:3 * EXPERTS], ones, sel[:, 0, :], start=True, stop=False)
            mm(W[2][:, 2 * EXPERTS:3 * EXPERTS], ones, sel[:, 1, :], start=False, stop=True).then_inc(rank_mm, 1)
            token_major("sh", 3, x2T)

            def turn_shared(t):
                pe.wait_ge(sh_done, t + 1)
                for c in range(2):
                    last = nc.tensor.transpose(W[1][:, t * SEQ + c * P:t * SEQ + (c + 1) * P],
                                               hh[:, c * P:(c + 1) * P], ident)
                last.then_inc(hsT_mm, 1)

            def gather(block, bank, buf, done):
                parts = [(x, t) for t in range(TB) for x in (x2h, x2l)]
                for b in range(2):
                    for k, (x, t) in enumerate(parts):
                        last = mm(bank[:, b * SEQ:(b + 1) * SEQ], x[:, t, (block + b) * P:(block + b + 1) * P],
                                  onehot[:, buf, t].rearrange("p e s -> p (e s)"),
                                  start=(k == 0), stop=(k == len(parts) - 1))
                last.then_inc(done, 1)

            pe.wait_ge(onehot_done, 3)
            pe.wait_ge(split_l, 2)
            for k in range(4):
                if k < 2:
                    turn_shared(k)
                    pe.wait_ge(sh_silu, k + 1)
                gather(2 * k, S[k], 0, gath_mm)
            pe.wait_ge(hsT_cp, TB + 1)
            pe.wait_ge(wsd_ld, 16)
            pe.wait_ge(place_done, 2)

            def bound_sums(first, done=None):
                for t in range(TB):
                    for c in range(2):
                        last = mm(W[2 * t + c][:], zero_r[:],
                                  onehot[:, 0].rearrange("p t e s -> p (t e s)"),
                                  start=first, stop=not first, skip_group_check=True)
                    if done is not None:
                        last.then_inc(done, 1)

            bound_sums(True)

            def shared_down():
                for t in range(TB):
                    for c in range(2):
                        for kb in range(2):
                            mm(W[2 * t + c][:], hsT[:, kb, t * P:(t + 1) * P], wsd[:, kb, c * 512:(c + 1) * 512],
                               start=False, stop=False, skip_group_check=True)

            def residual():
                for t in range(TB):
                    for c in range(2):
                        for x in (x2h, x2l):
                            mm(W[2 * t + c][:], alpha_ident, x[:, t, c * 512:(c + 1) * 512].bitcast(F32),
                               start=False, stop=False, skip_group_check=True)

            def scatter(done=None):
                for t in range(TB):
                    for c in range(2):
                        for y in (yh, yl):
                            last = mm(W[2 * t + c][:], scatT[:, t * P:(t + 1) * P], y[:, c * 512:(c + 1) * 512],
                                      start=False, stop=False, skip_group_check=True)
                if done is not None:
                    last.then_inc(done, 1)

            def gate_up(x, col, tiles, done, landed=None):
                for kb in range(KB):
                    if landed is not None and kb % 4 == 0:
                        landed(kb // 4)
                    for e in range(2):
                        last = mm(S[2][e * SLOTS:(e + 1) * SLOTS, :], x[:, kb, col + e * SLOTS:col + (e + 1) * SLOTS],
                                  tiles[e][kb // 4][:, kb % 4 * 512:(kb % 4 + 1) * 512],
                                  start=(kb == 0), stop=(kb == KB - 1))
                    if kb == KB // 2 - 1:
                        last.then_inc(gu_half, 1)
                last.then_inc(done, 1)

            def turn_onehot(buf, col, gates, done):
                for t in range(TB):
                    mm(S[0][:, t * P:(t + 1) * P], onehot[:, buf, t].rearrange("p e s -> p (e s)")[:, col:col + P],
                       ident_r[:], start=True, stop=True)
                for t in range(TB):
                    last = mm(S[0][:, SEQ:SEQ + 2],
                              onehot[:, buf, t].rearrange("p e s -> p (e s)")[:, col:col + P].bitcast(F32),
                              gates(t), start=(t == 0), stop=(t == TB - 1))
                last.then_inc(done, 1)

            def turn_h(done):
                for c in range(2):
                    last = nc.tensor.transpose(S[2][:, c * P:(c + 1) * P], hh[:, c * P:(c + 1) * P], ident)
                last.then_inc(done, 1)

            def down(c, tile, done):
                for kb in range(2):
                    for e in range(2):
                        o = kb * D + c * 512
                        last = mm((S[3], S[1])[c][e * SLOTS:(e + 1) * SLOTS, :], hT[:, kb, e * SLOTS:(e + 1) * SLOTS],
                                  tile[e][:, o:o + 512], start=(kb == 0), stop=(kb == 1))
                if done is not None:
                    last.then_inc(done, 1)

            def expert_pairs(i):
                for jj in range(ROUND):
                    buf, col = jj // 2 % 2, (jj % 2) * P
                    if jj % 2 == 0:
                        pe.wait_ge(gath_act, i * 8 + (2 + jj))
                        pe.wait_ge(gath_dve, i * 8 + (2 + jj))

                    def landed(half):
                        for kind in range(2):
                            pe.wait_ge(expert_ld[expert_tile(jj, kind)][half], expert_count(i, jj, kind))

                    gate_up(xg[buf], col, [places[expert_tile(jj, e)] for e in range(2)], gu_mm, landed)
                    if jj >= 1:
                        pe.wait_ge(yl_done, i * 16 + 2 * jj)
                        scatter()
                    pe.wait_ge(gath_dve, i * 8 + (2 + jj))
                    turn_onehot(buf, col, lambda t: gates_e[:, t, bass.ds(i * 16 + 2 * jj, 2)], scatT_mm)
                    pe.wait_ge(onehot_done, i * 8 + (2 * (jj // 2) + 5))
                    gather(4 * (jj % 2), S[1], (buf + 1) % 2, gath_mm)
                    pe.wait_ge(h_done, i * 8 + (jj + 1))
                    turn_h(hT_mm)
                    pe.wait_ge(scatT_cp, i * 8 + (jj + 1))
                    gather(4 * (jj % 2) + 2, S[0], (buf + 1) % 2, gath_mm)
                    pe.wait_ge(hT_cp, i * 8 + (jj + 1))
                    for half in range(2):
                        pe.wait_ge(expert_ld[expert_tile(jj, 2)][half], expert_count(i, jj, 2))
                    down(0, places[expert_tile(jj, 2)], down_mm)
                    pe.wait_ge(gath_act, i * 8 + (2 + jj + 1))
                    down(1, places[expert_tile(jj, 2)], down_mm)
                pe.wait_ge(yl_done, i * 16 + 16)
                scatter()
            with pe.Fori(0, PAIRS // ROUND // 2) as i:
                expert_pairs(i)
            shared_down()
            residual()
            with pe.Fori(PAIRS // ROUND // 2, PAIRS // ROUND) as i:
                expert_pairs(i)
            pe.wait_ge(gath_dve, 2 + PAIRS)
            pe.wait_ge(items_ld, 32)
            n_items = pe.value_load(items[0:1, P:P + 1], min_val=0, max_val=EXTRA)
            with pe.If(n_items > 0):
                mm(W[0][:, 0:P], zero_r[:], zero_r[:], start=False, stop=False, skip_group_check=True
                   ).then_inc(o_scat, 1)
                with pe.Fori(0, n_items) as i:
                    item = pe.value_load(items[0:1, bass.ds(i, 1)], min_val=0, max_val=EXTRA - 1)
                    pe.wait_ge(o_hot, i * 4 + 4)
                    for k in range(KB):
                        parts = [(x, t) for t in range(TB) for x in (x2h, x2l)]
                        for n, (x, t) in enumerate(parts):
                            last = mm(S[k // 4][:, (k % 4) * P:(k % 4 + 1) * P], x[:, t, k * P:(k + 1) * P],
                                      onehot[:, 0, t, 0:2, :].rearrange("p e s -> p (e s)"),
                                      start=(n == 0), stop=(n == 3))
                    last.then_inc(o_gath, 1)
                    pe.wait_ge(o_xg, i * 2 + 2)
                    pe.wait_ge(extra_ld, i * 48 + 48)
                    gate_up(xg[0], 0, [halves(ring[:, e, :]) for e in range(2)], o_gu)
                    pe.wait_ge(o_h, i + 1)
                    for t in range(TB):
                        mm(S[0][:, t * P:(t + 1) * P], onehot[:, 0, t, 0:2, :].rearrange("p e s -> p (e s)"),
                           ident_r[:], start=True, stop=True)
                    for t in range(TB):
                        mm(S[0][:, SEQ:SEQ + 2], onehot[:, 0, t, 0:2, :].rearrange("p e s -> p (e s)").bitcast(F32),
                           gates_e[:, t, bass.ds((item % PAIRS) * 2, 2)], start=(t == 0), stop=(t == TB - 1))
                    turn_h(o_T)
                    pe.wait_ge(o_Tcp, i * 4 + 4)
                    down(0, halves(ring[:, 2, :]), None)
                    down(1, halves(ring[:, 2, :]), o_down)
                    pe.wait_ge(o_y, i * 4 + 4)
                    scatter(o_scat)
            bound_sums(False, moe_mm)


def constants():
    c = np.zeros((P, C_CONVW), np.float32)
    p, f = np.arange(P)[:, None], np.arange(P)[None, :]
    c[:, C_ID:C_ID + P] = p == f
    c[:, C_TRI:C_TRI + P] = p <= f
    c[:, C_STRICT:C_STRICT + P] = p > f
    c[:, C_ONES:C_ONES + P] = 1.0
    c[:, C_FLIP:C_FLIP + P] = p + f == P - 1
    c[:, C_IOTA:C_IOTA + P] = f + 1
    c[:, C_RES:C_RES + P] = ALPHA * (p == f)
    c[:, C_LOW:C_LOW + 64] = (np.arange(8)[None, :] < np.arange(8)[:, None]).reshape(-1)
    item = np.arange(EXTRA)
    c[:, C_ROFF:C_ROFF + EXTRA] = SLOTS * (item // PAIRS + 1)
    c[:, C_ITEMS:C_ITEMS + EXTRA] = item
    c[:, C_ITEM + 1] = np.arange(P) + 1
    dist = SEQ - 1 - np.arange(384)
    exact = BUCKETS // 2
    d = np.maximum(dist, 1).astype(np.float32)
    large = exact + (np.log(d / exact) / math.log(MAX_DIST / exact) * (BUCKETS - exact)).astype(np.int32)
    bucket = np.where(dist < exact, dist, np.minimum(large, BUCKETS - 1))
    for j in range(384):
        if dist[j] >= 0:
            c[bucket[j], C_HOT + j] = 1.0
        else:
            c[BUCKETS, C_HOT + j] = MASKED
    return c


def lay_out(inp):
    f = {k: np.asarray(a, dtype=np.float32) for k, a in inp.items()}

    def tiles(w, cols, kbs=KB):
        n = w.shape[1] // cols
        return w.reshape(kbs, P, n, cols).transpose(2, 1, 0, 3).reshape(n, P, kbs * cols)

    w_in = f["w_in"][0]

    def tokens(w):
        return tiles(w, 2 * P)

    def features(w, kbs=KB):
        c = tiles(w, P, kbs)
        return c.reshape(-1, 2 * KB // kbs, P, kbs * P).transpose(0, 2, 1, 3).reshape(-1, P, TILE // 2)

    w_cv = f["w_ckv"][0][:, D:]
    wdense = np.concatenate([
        features(w_in[:, O_XBC:O_DT]), features(w_in[:, O_Q:O_V]), tokens(w_in[:, O_V:O_G]),
        features(w_in[:, 0:INNER]), features(w_in[:, O_G:]), features(f["w_ckv"][0][:, 0:D]), tokens(w_cv[:, 0:512]),
        features(f["w_diff_br"][0]), features(f["w_ssd_br"][0], XS_BLOCKS), tokens(f["w_mix_out"][0]),
        tokens(w_cv[:, 512:]), features(f["w_cq"][0]), tokens(f["w_co"][0]), tokens(f["w_sh_gu"][0]),
    ], axis=0)
    gu = f["w_exp_gu"][0].reshape(PAIRS, 2, KB, P, 2 * FF).transpose(0, 1, 3, 2, 4).reshape(PAIRS, 2, P, TILE)
    dn = f["w_exp_down"][0].reshape(PAIRS, 2, 2, P, D).transpose(0, 3, 1, 2, 4).reshape(PAIRS, 1, P, TILE)
    experts = np.concatenate([gu, dn], axis=1).reshape(3 * PAIRS, P, TILE)
    small = np.concatenate([
        constants(),
        f["conv_w"][0].reshape(CONV, NXB, P).transpose(2, 1, 0).reshape(P, NXB * CONV),
        f["conv_b"][0].reshape(NXB, P).T,
        f["ssd_norm_g"][0].reshape(XS_BLOCKS, P).T,
        np.repeat(f["d_skip"][0], HEAD).reshape(XS_BLOCKS, P).T,
        np.repeat(f["subln_g"][0].reshape(P, 1), 8, axis=1),
        np.concatenate([f["rel_bias"], np.ones((1, 8), np.float32), np.zeros((P - BUCKETS - 1, 8), np.float32)]),
        w_in[:, O_DT:O_Q].reshape(KB, P, SSD_HEADS).transpose(1, 0, 2).reshape(P, -1),
        f["w_router"][0].reshape(KB, P, EXPERTS).transpose(1, 0, 2).reshape(P, -1),
        f["ln2_g"][0].reshape(KB, P).T,
        f["ln2_b"][0].reshape(KB, P).T,
    ], axis=1)
    rows = np.concatenate([f["dt_bias"][0], f["a_log"][0], f["lambda_q1"][0], f["lambda_k1"][0], f["lambda_q2"][0],
                           f["lambda_k2"][0], f["router_bias"][0]])
    lnp = np.stack([np.stack([f[f"ln{i}_g"][0], f[f"ln{i}_b"][0]]) for i in (1, 2, 3)])

    def turned(x):
        return x[0].T.reshape(KB, P, -1).transpose(1, 0, 2)

    return {
        "small": small, "rows": rows, "lnp": lnp, "xT": turned(f["x"]), "memT": turned(f["mem"]),
        "x_tok": f["x"][0].reshape(TB, P, D).transpose(1, 0, 2), "wdense": wdense, "wstream": experts,
        "wshd": f["w_sh_down"][0].reshape(2, P, D).transpose(1, 0, 2),
    }


def kernel(**inputs):
    import concourse.bacc as bacc
    from concourse.bass_utils import run_bass_kernel_spmd

    nc = bacc.Bacc("TRN2", target_bir_lowering=False, num_devices=1)
    arrays = {f"in_{k}": np.ascontiguousarray(a) for k, a in lay_out(inputs).items()}
    args = [nc.dram_tensor(k, a.shape, mybir.dt.from_np(a.dtype), kind="ExternalInput").ap() for k, a in arrays.items()]
    out = nc.dram_tensor("out_dram", (1, SEQ, D), F32, kind="ExternalOutput").ap()
    layer_kernel(nc, *args, out)
    r = run_bass_kernel_spmd(nc, [arrays], core_ids=[0])
    return r.results[0]["out_dram"]
```
